# Optimizing a Trainium2 kernel written in Bass

```python
import jax, jax.numpy as jnp
from jax import lax
import numpy as np

D_MODEL = 1024
BATCH = 1
SEQ = 1024
DEPTH = 1

GRID_W = 64
CTX_LEN = 256
N_MIXERS = 2
N_CONV_LAYERS = (DEPTH + N_MIXERS - 1) // N_MIXERS
N_ATTN_LAYERS = DEPTH // N_MIXERS
CONV_WIDTH = 31
N_HEADS = 16
HEAD_DIM = D_MODEL // N_HEADS
WIN_H = 8
WIN_W = 16
N_EXPERTS = 16
N_GROUPS = 4
EXPERTS_PER_GROUP = N_EXPERTS // N_GROUPS
TOP_K = 2
D_EXPERT = D_MODEL // 2
N_MOD = 6
EPS = 1e-6

kernel_name = "hybrid_conv_natten_grouped_moe_dit"

def rmsnorm(x, g):
    xf = x.astype(jnp.float32)
    y = xf * lax.rsqrt(jnp.mean(xf * xf, axis=-1, keepdims=True) + EPS)
    return (y * g.astype(jnp.float32)).astype(x.dtype)

def layernorm(x, g, b):
    xf = x.astype(jnp.float32)
    mu = jnp.mean(xf, axis=-1, keepdims=True)
    var = jnp.mean(jnp.square(xf - mu), axis=-1, keepdims=True)
    y = (xf - mu) * lax.rsqrt(var + EPS) * g.astype(jnp.float32) + b.astype(jnp.float32)
    return y.astype(x.dtype)

def modulate(x, g, shift, scale):
    return rmsnorm(x, g) * (1 + scale) + shift

def depthwise_conv(u, w, b):
    y = lax.conv_general_dilated(u, w[:, None, :], window_strides=(1,), padding='SAME',
                                 dimension_numbers=('NWC', 'WIO', 'NWC'),
                                 feature_group_count=u.shape[-1])
    return y + b

def conv_module(h, w_in, b_in, w_dw, b_dw, ln_g, ln_b, w_out, b_out):
    a, gt = jnp.split(h @ w_in + b_in, 2, axis=-1)
    u = a * jax.nn.sigmoid(gt)
    u = depthwise_conv(u, w_dw, b_dw)
    u = jax.nn.silu(layernorm(u, ln_g, ln_b))
    return u @ w_out + b_out

def dense_attention(q, k, v):
    s = jnp.einsum('bqhd,bkhd->bhqk', q, k).astype(jnp.float32) * (HEAD_DIM ** -0.5)
    p = jax.nn.softmax(s, axis=-1).astype(v.dtype)
    return jnp.einsum('bhqk,bkhd->bqhd', p, v)

def neighbourhood_attention(q, k, v, k_ctx, v_ctx, rpb):
    B, S, H, Dh = q.shape
    rows = S // GRID_W
    kh = min(WIN_H, rows)
    n_loc = kh * WIN_W
    qg = q.reshape(B, rows, GRID_W, H, Dh)
    kg = k.reshape(B, rows, GRID_W, H, Dh)
    vg = v.reshape(B, rows, GRID_W, H, Dh)
    col = jnp.arange(GRID_W)
    col_start = jnp.clip(col - WIN_W // 2, 0, GRID_W - WIN_W)
    col_idx = col_start[:, None] + jnp.arange(WIN_W)[None, :]
    dcol = col_idx - col[:, None]
    scale = Dh ** -0.5

    def row_block(r):
        r0 = jnp.clip(r - kh // 2, 0, rows - kh)
        qr = lax.dynamic_index_in_dim(qg, r, axis=1, keepdims=False)
        kb = lax.dynamic_slice_in_dim(kg, r0, kh, axis=1)
        vb = lax.dynamic_slice_in_dim(vg, r0, kh, axis=1)
        kw = kb[:, :, col_idx]
        vw = vb[:, :, col_idx]
        drow = r0 + jnp.arange(kh) - r
        ri = (drow + WIN_H - 1)[None, :, None]
        ci = (dcol + WIN_W - 1)[:, None, :]
        bias = rpb[:, ri, ci].astype(jnp.float32)
        s_loc = jnp.einsum('bqhd,biqjhd->bhqij', qr, kw).astype(jnp.float32) * scale + bias[None]
        s_ctx = jnp.einsum('bqhd,blhd->bhql', qr, k_ctx).astype(jnp.float32) * scale
        s = jnp.concatenate([s_loc.reshape(B, H, GRID_W, n_loc), s_ctx], axis=-1)
        p = jax.nn.softmax(s, axis=-1).astype(v.dtype)
        p_loc = p[..., :n_loc].reshape(B, H, GRID_W, kh, WIN_W)
        p_ctx = p[..., n_loc:]
        return (jnp.einsum('bhqij,biqjhd->bqhd', p_loc, vw)
                + jnp.einsum('bhql,blhd->bqhd', p_ctx, v_ctx))

    out = lax.map(row_block, jnp.arange(rows))
    return out.transpose(1, 0, 2, 3, 4).reshape(B, S, H, Dh)

def na_mixer(h, hc, w_qkv, w_o, rpb, with_ctx_out):
    B, S, D = h.shape
    L = hc.shape[1]
    q, k, v = jnp.split(h @ w_qkv, 3, axis=-1)
    q = q.reshape(B, S, N_HEADS, HEAD_DIM)
    k = k.reshape(B, S, N_HEADS, HEAD_DIM)
    v = v.reshape(B, S, N_HEADS, HEAD_DIM)
    if with_ctx_out:
        qc, kc, vc = jnp.split(hc @ w_qkv, 3, axis=-1)
    else:
        kc, vc = jnp.split(hc @ w_qkv[:, D:], 2, axis=-1)
    kc = kc.reshape(B, L, N_HEADS, HEAD_DIM)
    vc = vc.reshape(B, L, N_HEADS, HEAD_DIM)
    o = neighbourhood_attention(q, k, v, kc, vc, rpb).reshape(B, S, D) @ w_o
    if with_ctx_out:
        oc = dense_attention(qc.reshape(B, L, N_HEADS, HEAD_DIM), kc, vc).reshape(B, L, D) @ w_o
        return o, oc
    return o, None

def grouped_moe(h, router_w, router_b, w_gate, w_up, w_down):
    N = h.shape[0]
    s = jax.nn.sigmoid((h @ router_w).astype(jnp.float32))
    s_sel = s + router_b.astype(jnp.float32)
    group_score = lax.top_k(s_sel.reshape(N, N_GROUPS, EXPERTS_PER_GROUP), TOP_K)[0].sum(-1)
    g = jnp.argmax(group_score, axis=-1)
    in_group = (jnp.arange(N_EXPERTS) // EXPERTS_PER_GROUP)[None, :] == g[:, None]
    _, idx = lax.top_k(jnp.where(in_group, s_sel, -jnp.inf), TOP_K)
    w = jnp.take_along_axis(s, idx, axis=-1)
    w = w / jnp.sum(w, axis=-1, keepdims=True)
    combine = jnp.sum(jax.nn.one_hot(idx, N_EXPERTS, dtype=jnp.float32) * w[..., None], axis=1)
    combine = combine.astype(h.dtype)
    out = jnp.zeros_like(h)
    for e in range(N_EXPERTS):
        he = jax.nn.silu(h @ w_gate[e]) * (h @ w_up[e])
        out = out + combine[:, e:e + 1] * (he @ w_down[e])
    return out

def _normal(key, shape, scale):
    return jax.random.normal(key, shape, jnp.float32) * scale

def setup_inputs(seed: int = 0) -> dict:
    key = jax.random.key(seed)
    ks = jax.random.split(key, 32)
    D = D_MODEL
    return {
        "x": _normal(ks[0], (BATCH, SEQ, D), 1.0),
        "c": _normal(ks[1], (BATCH, D), 1.0),
        "ctx": _normal(ks[2], (BATCH, CTX_LEN, D), 1.0),
        "c_ctx": _normal(ks[3], (D,), 1.0),
        "w_ada": _normal(ks[4], (DEPTH, D, N_MOD * D), 0.4 * D ** -0.5),
        "b_ada": _normal(ks[5], (DEPTH, N_MOD * D), 0.02),
        "g_mix_pre": 1.0 + _normal(ks[6], (DEPTH, D), 0.05),
        "g_mix_post": 1.0 + _normal(ks[7], (DEPTH, D), 0.05),
        "g_ffn_pre": 1.0 + _normal(ks[8], (DEPTH, D), 0.05),
        "g_ffn_post": 1.0 + _normal(ks[9], (DEPTH, D), 0.05),
        "conv_w_in": _normal(ks[10], (N_CONV_LAYERS, D, 2 * D), D ** -0.5),
        "conv_b_in": _normal(ks[11], (N_CONV_LAYERS, 2 * D), 0.02),
        "conv_w_dw": _normal(ks[12], (N_CONV_LAYERS, CONV_WIDTH, D), CONV_WIDTH ** -0.5),
        "conv_b_dw": _normal(ks[13], (N_CONV_LAYERS, D), 0.02),
        "conv_ln_g": 1.0 + _normal(ks[14], (N_CONV_LAYERS, D), 0.05),
        "conv_ln_b": _normal(ks[15], (N_CONV_LAYERS, D), 0.02),
        "conv_w_out": _normal(ks[16], (N_CONV_LAYERS, D, D), D ** -0.5),
        "conv_b_out": _normal(ks[17], (N_CONV_LAYERS, D), 0.02),
        "attn_w_qkv": _normal(ks[18], (N_ATTN_LAYERS, D, 3 * D), D ** -0.5),
        "attn_w_o": _normal(ks[19], (N_ATTN_LAYERS, D, D), D ** -0.5),
        "attn_rpb": _normal(ks[20], (N_ATTN_LAYERS, N_HEADS, 2 * WIN_H - 1, 2 * WIN_W - 1), 0.2),
        "router_w": _normal(ks[21], (D, N_EXPERTS), D ** -0.5),
        "router_b": _normal(ks[22], (N_EXPERTS,), 0.01),
        "exp_w_gate": _normal(ks[23], (DEPTH, N_EXPERTS, D, D_EXPERT), D ** -0.5),
        "exp_w_up": _normal(ks[24], (DEPTH, N_EXPERTS, D, D_EXPERT), D ** -0.5),
        "exp_w_down": _normal(ks[25], (DEPTH, N_EXPERTS, D_EXPERT, D), D_EXPERT ** -0.5),
    }

def reference(x, c, ctx, c_ctx, w_ada, b_ada, g_mix_pre, g_mix_post, g_ffn_pre, g_ffn_post,
              conv_w_in, conv_b_in, conv_w_dw, conv_b_dw, conv_ln_g, conv_ln_b, conv_w_out,
              conv_b_out, attn_w_qkv, attn_w_o, attn_rpb, router_w, router_b,
              exp_w_gate, exp_w_up, exp_w_down):
    B, S, D = x.shape
    L = ctx.shape[1]
    xc = ctx
    for i in range(DEPTH):
        kind = i % N_MIXERS
        j = i // N_MIXERS
        update_ctx = i < DEPTH - 1
        mod = jax.nn.silu(c) @ w_ada[i] + b_ada[i]
        mod_c = jax.nn.silu(c_ctx) @ w_ada[i] + b_ada[i]
        sh1, sc1, ga1, sh2, sc2, ga2 = [m[:, None, :] for m in jnp.split(mod, N_MOD, axis=-1)]
        sh1c, sc1c, ga1c, sh2c, sc2c, ga2c = jnp.split(mod_c, N_MOD, axis=-1)

        h = modulate(x, g_mix_pre[i], sh1, sc1)
        hc = modulate(xc, g_mix_pre[i], sh1c, sc1c)
        if kind == 0:
            conv_args = (conv_w_in[j], conv_b_in[j], conv_w_dw[j], conv_b_dw[j],
                         conv_ln_g[j], conv_ln_b[j], conv_w_out[j], conv_b_out[j])
            y = conv_module(h, *conv_args)
            yc = conv_module(hc, *conv_args) if update_ctx else None
        else:
            y, yc = na_mixer(h, hc, attn_w_qkv[j], attn_w_o[j], attn_rpb[j], update_ctx)
        x = x + ga1 * rmsnorm(y, g_mix_post[i])
        if update_ctx:
            xc = xc + ga1c * rmsnorm(yc, g_mix_post[i])

        tokens = modulate(x, g_ffn_pre[i], sh2, sc2).reshape(B * S, D)
        if update_ctx:
            tokens_c = modulate(xc, g_ffn_pre[i], sh2c, sc2c).reshape(B * L, D)
            tokens = jnp.concatenate([tokens, tokens_c], axis=0)
        f = grouped_moe(tokens, router_w, router_b, exp_w_gate[i], exp_w_up[i], exp_w_down[i])
        x = x + ga2 * rmsnorm(f[:B * S].reshape(B, S, D), g_ffn_post[i])
        if update_ctx:
            xc = xc + ga2c * rmsnorm(f[B * S:].reshape(B, L, D), g_ffn_post[i])
    return x


_drawn_inputs = setup_inputs


def setup_inputs(seed=0):
    import zlib

    import numpy as np

    out = dict(_drawn_inputs(seed))
    spreads = {}
    factors = {'g_ffn_post': 4.589, 'conv_b_in': 3.492, 'conv_ln_b': 3.411}
    for name, (base, spread) in spreads.items():
        noise = np.random.default_rng([zlib.crc32(name.encode()), seed]).standard_normal(out[name].shape)
        drawn = base * np.exp(spread * noise) if base else spread * noise
        out[name] = __import__('jax').numpy.asarray(drawn.astype(out[name].dtype))
    for name, factor in factors.items():
        out[name] = (out[name] * factor).astype(out[name].dtype)
    return out
```

```python
from contextlib import ExitStack

import concourse.bass as bass
from concourse import mybir

F32 = mybir.dt.float32
F32R = mybir.dt.float32r
I32 = mybir.dt.int32
U32 = mybir.dt.uint32
ALU = mybir.AluOpType
ACT = mybir.ActivationFunctionType
AX_X = mybir.AxisListType.X

P = 128
D = 1024
S = 1024
NT = S // P
KT = D // P
F = 512
FT = F // P
NE = 16
NG = 4
EG = NE // NG
EPS = 1e-6

NQ = 4
CQ = D // NQ
TAPS = 31
GC = 16
QG = CQ // GC
BG = 4
QB = QG // BG
ND = 5
NM = ND * NT
PAD = 2
MSLOTS = 4

ST_ROWS = 2 * P
NST = 23
NSTC = NST + 1
CHUNKS = 6
RING = 4
KB = 1024


def dit_layer(nc, x, c, w_ada, b_ada, g_mix_pre, g_mix_post, g_ffn_pre, g_ffn_post,
              w_in, b_in, w_dw, b_dw, ln_g, ln_b, w_out, b_out, router_w, router_b,
              w_gate, w_up, w_down, out):
    ctx = ExitStack()
    with ctx:
        def sem(name):
            return ctx.enter_context(nc.semaphore(name))

        limit = nc.sbuf_top
        base = (nc.sbuf_base + 31) // 32 * 32
        arena = ctx.enter_context(nc.sbuf_tensor("arena", [P, (limit - base - 64) // 4], F32))
        R0, R1, R2 = base, base + 96 * KB, base + 128 * KB
        top = [R2 + 84736]

        def at(name, shape, dt, offset):
            return nc.alloc_sbuf_tensor_at(name, shape, dt, offset=offset)

        def small(name, shape, dt=F32):
            n = 4
            for d in shape[1:]:
                n *= d
            t = at(name, shape, dt, top[0])
            top[0] += (n + 31) // 32 * 32
            assert top[0] <= limit, (name, top[0], limit)
            return t

        ada_first = at("ada_first", [P, KT, 2 * D], F32, R0)
        sp_hi = at("sp_hi", [P, KT, D], F32R, R0)
        sp_lo = at("sp_lo", [P, KT, D], F32R, R0 + 32 * KB)
        xv = at("xv", [P, NT, D], F32, R0 + 64 * KB)
        raw_gu = at("raw_gu", [P, 2, 2, KT, F], F32, R0)
        raw_d = at("raw_d", [P, 2, FT, D], F32, R0 + 64 * KB)
        wi_hi = at("wi_hi", [P, KT, 2 * CQ], F32R, R1)
        wi_lo = at("wi_lo", [P, KT, 2 * CQ], F32R, R1 + 16 * KB)
        x1 = at("x1", [P, NT, D], F32, R1)
        off = [R2]

        def seq(name, shape, dt):
            n = 4
            for d in shape[1:]:
                n *= d
            t = at(name, shape, dt, off[0])
            off[0] += (n + 31) // 32 * 32
            return t

        stage = seq("stage", [P, 2, 4096 // 2], F32)
        mx_hi = seq("mx_hi", [P, MSLOTS, ND, NT, GC], F32R)
        mx_lo = seq("mx_lo", [P, MSLOTS, ND, NT, GC], F32R)
        u = seq("u", [P, QG, NT * GC], F32)
        ut_hi = seq("ut_hi", [P, 2, BG, P + 2 * PAD], F32R)
        ut_lo = seq("ut_lo", [P, 2, BG, P + 2 * PAD], F32R)
        taps_raw = seq("taps_raw", [P, QG, NM], F32)
        taps_hi = seq("taps_hi", [P, QG, NM], F32R)
        taps_lo = seq("taps_lo", [P, QG, NM], F32R)
        bin_row = seq("bin_row", [P, 2 * CQ], F32)
        bdw_row = seq("bdw_row", [P, CQ], F32)
        acc = seq("acc", [P, D], F32)
        ada_stage = seq("ada_stage", [P, 2, D], F32)
        pre = seq("pre", [P, 2, 2 * CQ], F32)
        junk = seq("junk", [P, D], F32)
        assert off[0] <= top[0]
        hbuf = at("hbuf", [P, 2, KT, P], F32, R2 + 16 * KB)
        off = [R2 + 16 * KB]
        s_full_at = off[0]
        s_full = seq("s_full", [P, KT, P], F32)
        s_hi = seq("s_hi", [P, 2, KT, P], F32R)
        s_lo = seq("s_lo", [P, 2, KT, P], F32R)
        zb = seq("zb", [P, D], F32)
        yb = seq("yb", [P, 2, D], F32)
        xr = seq("xr", [P, 2, D], F32)
        h2 = seq("h2", [P, 2, D], F32)
        bout_row = seq("bout_row", [P, D], F32)
        rows = seq("rows", [P, 3, D], F32)
        diag = [at("diag0", [P, P, KT], F32, s_full_at), at("diag1", [P, P, KT], F32, s_full_at + 4 * KB)]
        junk2 = at("junk2", [P, D], F32, R2 + 12 * KB)
        h2t = at("h2t", [P, KT, P], F32, R2 + 8 * KB)
        assert off[0] <= top[0], (off[0], top[0])

        ident = small("ident", [P, P])
        col = small("col", [P, 8, KT])
        bada = small("bada", [P, 6, KT])
        modc = small("modc", [P, 4, KT])
        silc = small("silc", [P, 2, KT])
        a_sh = small("a_sh", [P, 2, KT])
        eye16 = small("eye16", [P, GC])
        ones = small("ones", [P, P])
        nhalf = small("nhalf", [P, 8])
        epsc = small("epsc", [P, 1])
        gap = small("gap", [P, 1])
        zero_i = small("zero_i", [P, 1], I32)
        gap_p = small("gap_p", [P, 1])
        ssx = small("ssx", [P, NT])
        rsx = small("rsx", [P, NT])
        tmp8 = small("tmp8", [P, NT])
        stats = small("stats", [P, 2, 6])
        mv = small("mv", [P, 2, 2])
        lnr = small("lnr", [P, 2, 2])
        sy = small("sy", [P, 2, 3])
        sx = small("sx", [P, 2, 3])
        vcol = small("vcol", [P, 3, KT])
        rwt = small("rwt", [P, KT, NE])
        rb_row = small("rb_row", [P, NE])
        logits = small("logits", [P, NT, NE])

        gates = small("gates", [P, 2, NT])
        words = small("words", [P, NSTC], I32)
        counts = small("counts", [P, 2], I32)
        ct_i = small("ct_i", [P, NE], I32)
        dest = small("dest", [P, 2 * NSTC], I32)
        src = small("src", [P, 2 * NSTC], I32)
        ic = small("ic", [P, 4], I32)

        off = [R2 + 80 * KB]
        tri = seq("tri", [P, P], F32)
        iota = seq("iota", [P, P], F32)
        le16 = seq("le16", [P, NE, NE], F32)
        lt4 = seq("lt4", [P, EG, EG], F32)
        desc4 = seq("desc4", [P, NG], F32)
        tok1 = seq("tok1", [P, 2 * NT], F32)
        assert off[0] <= R2 + 84736
        off = [R2 + 40 * KB]
        aff = seq("aff", [P, NT, NE], F32)
        sel = seq("sel", [P, NT, NE], F32)
        pair_max = seq("pair_max", [P, NT * NG, 2], F32)
        pair_min = seq("pair_min", [P, NT * NG, 2], F32)
        gs = seq("gs", [P, 6, NT, NG], F32)
        gmax = seq("gmax", [P, 2, NT], F32)
        beats = seq("beats", [P, 2, NT * NG, EG, EG], F32)
        rank = seq("rank", [P, NT, NE], F32)
        mk = seq("mk", [P, 2, NT, NE], F32)
        m9 = seq("m9", [P, NT + 1, NE], F32)
        prod = seq("prod", [P, 2 * NT, NE], F32)
        ak = seq("ak", [P, 2, NT], F32)
        den = seq("den", [P, 2, NT], F32)
        pos = seq("pos", [P, NT, NE], F32)
        cnt = seq("cnt", [P, 6, NE], F32)
        prod16 = seq("prod16", [P, NE, NE], F32)
        slot = seq("slot", [P, 2 * NT], F32)
        slot_i = seq("slot_i", [P, 3, 2 * NT], I32)
        slot_f = seq("slot_f", [P, 2, 2 * NT], F32)
        st_le = seq("st_le", [P, NSTC, NE], F32)
        st_in = seq("st_in", [P, NSTC, NE], F32)
        st_ab = seq("st_ab", [P, NSTC, NE], F32)
        start = seq("start", [P, 2, NSTC], F32)
        e_of = seq("e_of", [P, NSTC + 2], F32)
        hb_of = seq("hb_of", [P, 2, 16 + NSTC + 1], F32)
        word_f = seq("word_f", [P, 2, NSTC], F32)
        oh_p = seq("oh_p", [P, 2 * NT, P], F32)
        oh_t = seq("oh_t", [P, 2 * NT, 2 * NSTC], F32)
        assert off[0] <= R2 + 76 * KB, off[0] - R2

        off = [R2]
        pr_hi = seq("pr_hi", [P, RING, D], F32R)
        pr_lo = seq("pr_lo", [P, RING, D], F32R)
        xg = seq("xg", [P, 2, D], F32)
        xt_hi = seq("xt_hi", [P, 2, KT, P], F32R)
        xt_lo = seq("xt_lo", [P, 2, KT, P], F32R)
        he = seq("he", [P, 2, F], F32)
        het_hi = seq("het_hi", [P, 2, FT, P], F32R)
        het_lo = seq("het_lo", [P, 2, FT, P], F32R)
        ys = seq("ys", [P, 2, D], F32)
        assert off[0] <= R2 + 80 * KB
        y_all = at("y_all", [P, 2, NT, D], F32, R0)
        g3 = at("g3", [P, D], F32, R0 + 64 * KB)
        fb = at("fb", [P, 2, D], F32, R0 + 68 * KB)
        junk3 = at("junk3", [P, D], F32, R0 + 76 * KB)
        sf = small("sf", [P, 3, NT])

        h2_rows = nc.dram_tensor("h2_rows", [S, D], F32).ap()
        y_rows = nc.dram_tensor("y_rows", [2 * S, D], F32).ap()
        g3_rows = nc.dram_tensor("g3_rows", [P, D], F32).ap()

        ps = ctx.enter_context(nc.psum_tensor("ps", [P, 8, 512], F32))

        cols_loaded = sem("cols_loaded")
        x_loaded = [sem(f"x_loaded{j}") for j in range(4)]
        ada1_loaded = [sem(f"ada1_loaded{j}") for j in range(4)]
        stage_loaded = [sem(f"stage_loaded{j}") for j in range(2)]
        taps_loaded = sem("taps_loaded")
        brow_loaded = sem("brow_loaded")
        bdw_loaded = sem("bdw_loaded")
        ada_loaded = [sem(f"ada_loaded{j}") for j in range(2)]
        const_made = sem("const_made")
        eye_made = sem("eye_made")
        sigc_done = sem("sigc_done")
        silc_done = sem("silc_done")
        ssx_done = sem("ssx_done")
        pool_chain = sem("pool_chain")
        rsx_done = sem("rsx_done")
        xn_done = sem("xn_done")
        ada1_mod = sem("ada1_mod")
        mod1_done = sem("mod1_done")
        xt_done = sem("xt_done")
        ht_done = sem("ht_done")
        hs_done = sem("hs_done")
        hhi_done = sem("hhi_done")
        hlo_done = sem("hlo_done")
        wi_hi_done = sem("wi_hi_done")
        wi_lo_done = sem("wi_lo_done")
        wi_used = sem("wi_used")
        win_tile = sem("win_tile")
        pre_done = sem("pre_done")
        sig_done = sem("sig_done")
        u_done = sem("u_done")
        acc_done = sem("acc_done")
        acc_col = sem("acc_col")
        modc_done = sem("modc_done")
        taps_split = sem("taps_split")
        mhi_done = sem("mhi_done")
        mlo_done = sem("mlo_done")
        ut_tr = sem("ut_tr")
        uthi_done = sem("uthi_done")
        utlo_done = sem("utlo_done")
        conv_done = sem("conv_done")
        v_done = sem("v_done")
        wo_hi_done = sem("wo_hi_done")
        wo_lo_done = sem("wo_lo_done")
        xr_loaded = [sem(f"xr_loaded{j}") for j in range(2)]
        bout_loaded = sem("bout_loaded")
        rw_loaded = sem("rw_loaded")
        vcol_done = sem("vcol_done")
        diag_done = sem("diag_done")
        brow_tr = sem("brow_tr")
        rows_done = sem("rows_done")
        g3_stored = sem("g3_stored")
        stats_done = sem("stats_done")
        mv_done = sem("mv_done")
        lnr_done = sem("lnr_done")
        lnv_done = sem("lnv_done")
        sym_done = sem("sym_done")
        sxm_done = sem("sxm_done")
        z_done = sem("z_done")
        zt_done = sem("zt_done")
        s_done = sem("s_done")
        sh_done = sem("sh_done")
        sl_done = sem("sl_done")
        yh_done = sem("yh_done")
        yb_done = sem("yb_done")
        sqy_done = sem("sqy_done")
        ry_done = sem("ry_done")
        t_done = sem("t_done")
        x1_done = sem("x1_done")
        sqx_done = sem("sqx_done")
        rx_done = sem("rx_done")
        hg_done = sem("hg_done")
        h2_done = sem("h2_done")
        h2_stored = [sem(f"h2_stored{j}") for j in range(2)]
        h2_tr = sem("h2_tr")
        h2t_done = sem("h2t_done")
        rt_done = sem("rt_done")
        log_done = sem("log_done")

        rconst = sem("rconst")
        aff_done = sem("aff_done")
        route_chain = sem("route_chain")
        pos_done = sem("pos_done")
        slots_done = sem("slots_done")
        tables = sem("tables")
        raw_loaded = [[sem(f"raw_loaded{b}{j}") for j in range(CHUNKS)] for b in range(2)]
        ic_done = [sem(f"ic_done{j}") for j in range(4)]
        gath = [sem(f"gath{j}") for j in range(2)]
        scat = [sem(f"scat{j}") for j in range(2)]
        all_scattered = sem("all_scattered")
        xt_tr = sem("xt_tr")
        xth_done = sem("xth_done")
        xtl_done = sem("xtl_done")
        pr_hi_done = sem("pr_hi_done")
        pr_lo_dve = sem("pr_lo_dve")
        pr_lo_pool = sem("pr_lo_pool")
        pr_used = sem("pr_used")
        sil_done = sem("sil_done")
        he_done = sem("he_done")
        he_tr = sem("he_tr")
        heth_done = sem("heth_done")
        hetl_done = sem("hetl_done")
        d0_done = sem("d0_done")
        d1_done = sem("d1_done")
        y0_done = sem("y0_done")
        y1_done = sem("y1_done")
        yl = [sem(f"yl{j}") for j in range(4)]
        g3_loaded = sem("g3_loaded")
        fa_done = sem("fa_done")
        f_done = sem("f_done")
        sqf_done = sem("sqf_done")
        sfm_done = sem("sfm_done")
        rf_done = sem("rf_done")
        fg_done = sem("fg_done")
        o_done = sem("o_done")
        stored = sem("stored")

        block = ctx.enter_context(nc.Block())

        class Step:
            def __init__(self, eng, s):
                w = eng.value_load(words[0:1, bass.ds(s, 1)], min_val=0, max_val=(1 << 23) - 1)
                self.s = s
                self.ep, self.e, self.en = w & 31, (w >> 5) & 31, (w >> 10) & 31
                self.hp, self.h, self.hn = (w >> 15) & 1, (w >> 16) & 1, (w >> 17) & 1
                self.nbp = w >> 18
                self.nb = self.nbp + self.hp
                self.nbn = self.nb + self.h
                self.c = self.nb + s
                self.cn = self.c + self.h + 1
                if not (type(s) is int and s == 0):
                    self.cp = self.nbp + (s - 1)

        marks = {}
        WI = (0, 1, 2)
        UT = (3, 4)
        CV = (5, 6)
        MODB = 7
        DN, TR = 4, 6
        PZ, PY, PH, PR = 0, 2, 4, 6

        x_t = x.rearrange("b (a i) d -> (b a) i d", i=NT)
        w_ada_t = w_ada.rearrange("l (p k) n -> (l p) k n", k=KT)
        w_out_t = w_out.rearrange("l (p k) n -> (l p) k n", k=KT)

        @block.sync
        def _(sp):
            cols = ((c.rearrange("b n -> (b n)"), 0), (g_mix_pre.rearrange("b n -> (b n)"), 1),
                    (g_mix_post.rearrange("b n -> (b n)"), 2), (g_ffn_pre.rearrange("b n -> (b n)"), 3),
                    (g_ffn_post.rearrange("b n -> (b n)"), 4), (ln_g.rearrange("b n -> (b n)"), 5),
                    (ln_b.rearrange("b n -> (b n)"), 6))
            for src, j in cols:
                sp.dma_start(col[:, j, :], src.rearrange("(p k) -> p k", k=KT)).then_inc(cols_loaded, 16)
            sp.dma_start(bada[:, :, :], b_ada.rearrange("l (s p k) -> (l p) s k", s=6, k=KT)).then_inc(cols_loaded, 16)

            def load_x(j):
                sp.dma_start(xv[:, 2 * j:2 * j + 2, :], x_t[:, 2 * j:2 * j + 2, :]).then_inc(x_loaded[j], 16)

            def load_win(q, h):
                sp.dma_start(stage[:, h, :],
                             w_in[bass.ds(q, 1), :, 2048 * h:2048 * h + 2048].rearrange("q p n -> (q p) n")
                             ).then_inc(stage_loaded[h], 16)

            def load_taps(q):
                for i in range(NT):
                    sp.dma_start(taps_raw[GC * i:GC * i + GC, :, i + 1:i + 1 + TAPS],
                                 w_dw[bass.ds(q, 1)].rearrange("q c g t -> (q c) g t")).then_inc(taps_loaded, 16)

            load_x(0)
            for j in range(4):
                sp.dma_start(ada_first[:, 2 * j:2 * j + 2, :],
                             w_ada_t[:, 2 * j:2 * j + 2, 0:2 * D]).then_inc(ada1_loaded[j], 16)
            load_win(0, 0)
            load_win(0, 1)
            for j in range(1, 4):
                load_x(j)
            sp.wait_ge(const_made, 6)
            load_taps(0)

            def quarter(q, last):
                for h in range(2):
                    sp.wait_ge(wi_lo_done, 4 * q + 2 * h + 2)
                    if last:
                        sp.dma_start(stage[:, h, :].rearrange("p (k n) -> p k n", k=2), w_out_t[:, 2 * h:2 * h + 2, :]).then_inc(stage_loaded[h], 16)
                    else:
                        load_win(q + 1, h)
                for k in range(KT):
                    if k >= 2:
                        sp.wait_ge(acc_done, 8 * q + k - 1)
                    else:
                        sp.wait_ge(acc_done, 8 * q)
                    sp.dma_start(ada_stage[:, k % 2, :],
                                 w_ada_t[:, k, bass.ds((q + 2) * D, D)]).then_inc(ada_loaded[k % 2], 16)
                if not last:
                    sp.wait_ge(taps_split, 2 * q + 2)
                    load_taps(q + 1)

            with sp.Fori(0, NQ - 1) as q:
                quarter(q, False)
            quarter(NQ - 1, True)
            sp.wait_ge(v_done, NQ * QB)
            sp.dma_start(bout_row[:, :], b_out[0:1, :].partition_broadcast(P)).then_inc(bout_loaded, 16)
            sp.dma_start(rwt[:, :, :], router_w.rearrange("(p k) e -> p k e", k=KT)).then_inc(rw_loaded, 16)
            sp.dma_start(rb_row[:, :], router_b.rearrange("(b n) -> b n", b=1).partition_broadcast(P)).then_inc(rw_loaded, 16)
            for h in range(2):
                sp.wait_ge(wo_lo_done, 2 * h + 2)
                sp.dma_start(stage[:, h, :].rearrange("p (k n) -> p k n", k=2),
                             w_out_t[:, 4 + 2 * h:6 + 2 * h, :]).then_inc(stage_loaded[h], 16)

            h2_out = h2_rows.rearrange("(a i) d -> a i d", i=NT)

            def load_xr(i, b, first):
                if not first:
                    sp.wait_ge(x1_done, i - 1)
                sp.dma_start(xr[:, b, :], x_t[:, bass.ds(i, 1), :]).then_inc(xr_loaded[b], 16)

            def store_h2(i, b):
                sp.wait_ge(h2_done, i + 1)
                sp.dma_start(h2_out[:, bass.ds(i, 1), :], h2[:, b, :]).then_inc(h2_stored[b], 16)

            load_xr(0, 0, True)
            load_xr(1, 1, True)
            sp.wait_ge(rows_done, 4)
            sp.dma_start(g3_rows, h2[:, 0, :]).then_inc(g3_stored, 16)
            with sp.Fori(0, NT // 2 - 1) as t:
                for b in range(2):
                    load_xr(2 * t + 2 + b, b, False)
                    store_h2(2 * t + b, b)
            store_h2(NT - 2, 0)
            store_h2(NT - 1, 1)
            sp.wait_ge(yh_done, 2 * NT)
            sp.wait_ge(z_done, NT)

            def load_expert(e, b, ct):
                one = bass.ds(e, 1)
                if ct is not None:
                    sp.wait_ge(pr_used, 12 * ct + 8)
                for j in range(4):
                    src_w = (w_gate, w_up)[j % 2]
                    ks = slice(4 * (j // 2), 4 * (j // 2) + 4)
                    sp.dma_start(raw_gu[:, b, j % 2, ks, :],
                                 src_w[0, one].rearrange("e (p k) n -> (e p) k n", k=KT)[:, ks, :]
                                 ).then_inc(raw_loaded[b][j], 16)
                if ct is not None:
                    sp.wait_ge(pr_used, 12 * ct + 24)
                for j in range(2):
                    ks = slice(2 * j, 2 * j + 2)
                    sp.dma_start(raw_d[:, b, ks, :],
                                 w_down[0, one].rearrange("e (p k) n -> (e p) k n", k=FT)[:, ks, :]
                                 ).then_inc(raw_loaded[b][4 + j], 16)

            load_expert(0, 0, None)
            load_expert(1, 1, None)
            sp.wait_ge(tables, 1)
            with sp.Fori(1, NE // 2) as t:
                for b in range(2):
                    load_expert(2 * t + b, b, sp.value_load(ct_i[0:1, bass.ds(2 * t - 2 + b, 1)], min_val=0, max_val=NST - 1))

            last_st = sp.value_load(counts[0:1, 0:1], min_val=0, max_val=NST - 1)
            st = last_st + 1
            sp.wait_ge(pr_used, 12 * st + 4)
            sp.dma_start(g3[:, :], g3_rows).then_inc(g3_loaded, 16)
            sp.wait_ge(all_scattered, 1)
            y_in = y_rows.rearrange("(k a i) d -> a k i d", k=2, i=NT)
            for j in range(4):
                for k in range(2):
                    sp.dma_start(y_all[:, k, 2 * j:2 * j + 2, :], y_in[:, k, 2 * j:2 * j + 2, :]).then_inc(yl[j], 16)
            out_t = out.rearrange("b (a i) d -> (b a) i d", i=NT)
            for i in range(NT):
                sp.wait_ge(o_done, i + 1)
                sp.dma_start(out_t[:, i, :], x1[:, i, :]).then_inc(stored, 16)
            sp.wait_ge(h2_stored[0], 16 * (NT // 2))
            sp.wait_ge(h2_stored[1], 16 * (NT // 2))
            sp.wait_ge(stored, 16 * NT)

        @block.gpsimd
        def _(pool):
            pool.memset(ident[:, :], 0.0).then_inc(pool_chain, 1)
            pool.memset(eye16[:, :], 0.0).then_inc(pool_chain, 1)
            pool.memset(epsc[:, :], EPS).then_inc(pool_chain, 1)
            pool.memset(zero_i[:, :], 0).then_inc(pool_chain, 1)
            pool.memset(ones[:, :], 1.0).then_inc(const_made, 1)
            pool.memset(nhalf[:, :], -0.5).then_inc(const_made, 1)
            pool.memset(taps_raw[:, :, :], 0.0).then_inc(const_made, 1)
            pool.memset(ut_hi[:, :, :, :].bitcast(F32), 0.0).then_inc(const_made, 1)
            pool.memset(ut_lo[:, :, :, :].bitcast(F32), 0.0).then_inc(const_made, 1)
            pool.wait_ge(pool_chain, 4)
            pool.affine_select(out=ident[:, :], in_=ident[:, :], compare_op=ALU.not_equal, fill=1.0, base=0,
                               pattern=[[-1, P]], channel_multiplier=1).then_inc(const_made, 1)
            for i in range(NT):
                pool.affine_select(out=eye16[:, :], in_=eye16[:, :], compare_op=ALU.not_equal, fill=1.0,
                                   base=-GC * i, pattern=[[-1, GC]], channel_multiplier=1).then_inc(eye_made, 1)
                pool.wait_ge(eye_made, i + 1)
            pool.dma_start(bin_row[:, :], b_in[0:1, :].partition_broadcast(P)).then_inc(brow_loaded, 16)
            pool.dma_start(bdw_row[:, :], b_dw[0:1, 0:CQ].partition_broadcast(P)).then_inc(bdw_loaded, 16)
            pool.wait_ge(const_made, 6)

            def inv_rms(j):
                two = slice(2 * j, 2 * j + 2)
                pool.wait_ge(ssx_done, 2 * j + 2)
                pool.tensor_scalar(tmp8[:, two], ssx[:, two], 1.0 / D, EPS, ALU.mult, ALU.add).then_inc(pool_chain, 1)
                pool.wait_ge(pool_chain, 5 + j)
                pool.tensor_tensor(rsx[:, two], tmp8[:, two], nhalf[:, 0:2], ALU.pow).then_inc(rsx_done, 1)

            inv_rms(0)
            for i in range(NT):
                pool.wait_ge(ht_done, i + 1)
                pool.tensor_tensor(hbuf[:, i % 2], hbuf[:, i % 2],
                                   a_sh[:, 0, :].unsqueeze(2).to_broadcast([P, KT, P]), ALU.add).then_inc(hs_done, 1)
                if i % 2 == 1 and i + 1 < NT:
                    inv_rms(i // 2 + 1)
            pool.wait_ge(hlo_done, NT)

            def make_m(q, g):
                if g < MSLOTS:
                    pool.wait_ge(conv_done, QG * q)
                else:
                    pool.wait_ge(conv_done, QG * q + g - MSLOTS + 1)
                pool.tensor_tensor(mx_hi[:, g % MSLOTS],
                                   taps_hi[:, g, :].bitcast(F32).rearrange("p (d i) -> p d i", d=ND).unsqueeze(3)
                                   .to_broadcast([P, ND, NT, GC]),
                                   eye16[:, :].unsqueeze(1).unsqueeze(1).to_broadcast([P, ND, NT, GC]),
                                   ALU.mult).then_inc(mhi_done, 1)

            def quarter(q, last):
                pool.wait_ge(taps_loaded, 128 * q + 128)
                pool.wait_ge(mlo_done, QG * q)
                pool.tensor_tensor(taps_hi[:, :, :], taps_raw[:, :, :], ones[:, 0:1].unsqueeze(1).to_broadcast([P, QG, NM]),
                                   ALU.mult).then_inc(taps_split, 1)
                pool.wait_ge(taps_split, 2 * q + 1)
                pool.tensor_tensor(taps_lo[:, :, :], taps_raw[:, :, :], taps_hi[:, :, :].bitcast(F32),
                                   ALU.subtract).then_inc(taps_split, 1)
                for g in range(QG):
                    make_m(q, g)
                    if g == 8 and not last:
                        pool.wait_ge(pre_done, 8 * q + 8)
                        pool.dma_start(bin_row[:, :],
                                       b_in[bass.ds(q + 1, 1), :].partition_broadcast(P)).then_inc(brow_loaded, 16)
                if not last:
                    pool.wait_ge(v_done, QB * q + QB)
                    pool.dma_start(bdw_row[:, :],
                                   b_dw[0:1, bass.ds((q + 1) * CQ, CQ)].partition_broadcast(P)).then_inc(bdw_loaded, 16)

            with pool.Fori(0, NQ - 1) as q:
                quarter(q, False)
            quarter(NQ - 1, True)

            def lnr_of(i, b):
                pool.wait_ge(mv_done, i + 1)
                pool.tensor_tensor(lnr[:, b, 0:1], mv[:, b, 1:2], epsc[:, :], ALU.add).then_inc(lnv_done, 1)
                pool.wait_ge(lnv_done, i + 1)
                pool.tensor_tensor(lnr[:, b, 1:2], lnr[:, b, 0:1], nhalf[:, 0:1], ALU.pow).then_inc(lnr_done, 1)

            def factor(i, b, s3, summed, mid, done):
                pool.wait_ge(summed, i + 1)
                pool.tensor_tensor(s3[:, b, 1:2], s3[:, b, 0:1], epsc[:, :], ALU.add).then_inc(mid, 1)
                pool.wait_ge(mid, i + 1)
                pool.tensor_tensor(s3[:, b, 2:3], s3[:, b, 1:2], nhalf[:, 0:1], ALU.pow).then_inc(done, 1)

            def step(i, b, last):
                if not last:
                    lnr_of(i + 1, 1 - b)
                factor(i, b, sy, sqy_done, sym_done, ry_done)
                factor(i, b, sx, sqx_done, sxm_done, rx_done)
                pool.wait_ge(hg_done, i + 1)
                pool.tensor_tensor(h2[:, b, :], h2[:, b, :], rows[:, 2, :], ALU.add).then_inc(h2_done, 1)

            lnr_of(0, 0)
            pool.wait_ge(rows_done, 4)
            step(0, 0, False)
            with pool.Fori(0, NT // 2 - 1) as t:
                step(2 * t + 1, 1, False)
                step(2 * t + 2, 0, False)
            step(NT - 1, 1, True)
            pool.wait_ge(v_done, NQ * QB)
            pool.memset(tri[:, :], 1.0).then_inc(pool_chain, 1)
            pool.memset(le16[:, :, :], 1.0).then_inc(pool_chain, 1)
            pool.memset(lt4[:, :, :], 1.0).then_inc(pool_chain, 1)
            for j in range(NG):
                pool.memset(desc4[:, j:j + 1], float(NG - j)).then_inc(rconst, 1)
            pool.wait_ge(pool_chain, 4 + NT // 2 + 3)
            pool.affine_select(out=tri[:, :], in_=tri[:, :], compare_op=ALU.is_ge, fill=0.0, base=-1,
                               pattern=[[1, P]], channel_multiplier=-1).then_inc(rconst, 1)
            pool.affine_select(out=le16[:, :, :], in_=le16[:, :, :], compare_op=ALU.is_ge, fill=0.0, base=0,
                               pattern=[[1, NE], [-1, NE]], channel_multiplier=0).then_inc(rconst, 1)
            pool.affine_select(out=lt4[:, :, :], in_=lt4[:, :, :], compare_op=ALU.is_ge, fill=0.0, base=-1,
                               pattern=[[1, EG], [-1, EG]], channel_multiplier=0).then_inc(rconst, 1)
            pool.iota(iota[:, :], pattern=[[1, P]], base=0, channel_multiplier=0,
                      allow_small_or_imprecise_dtypes=True).then_inc(rconst, 1)
            pool.iota(tok1[:, :], pattern=[[S, 2], [1, NT]], base=1, channel_multiplier=NT,
                      allow_small_or_imprecise_dtypes=True).then_inc(rconst, 1)

            pool.wait_ge(tables, 1)
            last_st = pool.value_load(counts[0:1, 0:1], min_val=0, max_val=NST - 1)
            st = last_st + 1

            def low(idx, q, e, k, down):
                pool.wait_ge(pr_hi_done, idx + 1)
                if down:
                    pool.tensor_tensor(pr_lo[:, 3, :], raw_d[:, bass.ds(q, 1), k, :].rearrange("p o n -> p (o n)"),
                                       pr_hi[:, 3, :].bitcast(F32), ALU.subtract).then_inc(pr_lo_pool, 1)
                    return None
                return pool.tensor_tensor(pr_lo[:, 3, :].rearrange("p (g n) -> p g n", g=2),
                                          raw_gu[:, bass.ds(q, 1), :, k, :].rearrange("p o g n -> p (o g) n"),
                                          pr_hi[:, 3, :].bitcast(F32).rearrange("p (g n) -> p g n", g=2), ALU.subtract)

            def settle():
                pool.tensor_tensor(gap_p[:, :], epsc[:, :], epsc[:, :], ALU.add)

            def gather(s, b, nxt):
                if nxt is not None:
                    pool.wait_ge(xt_tr, nxt)
                col_ = src[:, bass.ds(2 * s + b, 1)]
                pool.tensor_tensor(ic[:, b:b + 1], col_, zero_i[:, :], ALU.add).then_inc(ic_done[b], 1)
                n = s + 1 if b == 0 else gathered_b[0] + 1
                pool.wait_ge(ic_done[b], n)
                settle()
                pool.indirect_dma_start(xg[:, b, :], None, h2_rows,
                                        bass.IndirectOffsetOnAxis(ap=ic[:, b:b + 1].bitcast(U32), axis=0)).then_inc(gath[b], 16)

            def scatter(b, slot, tiles, before, n):
                pool.wait_ge(y0_done, tiles)
                pool.wait_ge(y1_done, tiles)
                pool.wait_ge(scat[b], 16 * before)
                col_ = dest[:, bass.ds(slot, 1)]
                pool.tensor_tensor(ic[:, 2 + b:3 + b], col_, zero_i[:, :], ALU.add).then_inc(ic_done[2 + b], 1)
                pool.wait_ge(ic_done[2 + b], n)
                settle()
                pool.indirect_dma_start(y_rows, bass.IndirectOffsetOnAxis(ap=ic[:, 2 + b:3 + b].bitcast(U32), axis=0),
                                        ys[:, b, :], None, bounds_check=2 * S - 1, oob_is_err=False
                                        ).then_inc(scat[b], 16)

            def scatter_both(w_s, hb, nb, tiles):
                before = w_s + 0
                n = w_s + 1
                scatter(0, 2 * w_s, tiles + 1, before, n)
                with pool.If(hb > 0):
                    n = nb + 1
                    scatter(1, 2 * w_s + 1, tiles + 2, nb, n)

            gathered_b = [0]
            w = Step(pool, 0)
            gather(0, 0, None)
            with pool.If(w.h > 0):
                gather(0, 1, None)
            low(3, 0, 0, 3, False).then_inc(pr_lo_pool, 1)
            gather(1, 0, w.cn)
            gathered_b = [w.h]
            with pool.If(w.hn > 0):
                gather(1, 1, w.cn)
            low(7, 0, 0, 7, False).then_inc(pr_lo_pool, 2)
            low(15, w.en & 1, 0, 3, False).then_inc(pr_lo_pool, 1)
            with pool.Fori(1, NST) as s:
                with pool.If(s < st):
                    w = Step(pool, s)
                    gathered_b = [w.nbn]
                    with pool.If(s + 1 < st):
                        gather(s + 1, 0, w.cn)
                        pool.wait_ge(tables, 1)
                    with pool.Else():
                        pool.wait_ge(tables, 1)
                    with pool.If(w.hn > 0):
                        gather(s + 1, 1, w.cn)
                    low(12 * s + 7, w.e & 1, 0, 7, False).then_inc(pr_lo_pool, 1)
                    low(12 * s + 11, w.ep & 1, 0, 3, True)
                    with pool.If(s + 1 < st):
                        low(12 * s + 15, w.en & 1, 0, 3, False).then_inc(pr_lo_pool, 1)
                    with pool.Else():
                        pool.wait_ge(tables, 1)
                    scatter_both(s - 1, w.hp, w.nbp, w.cp)
                    pool.wait_ge(tables, 1)
                pool.wait_ge(tables, 1)
            w = Step(pool, last_st)
            low(12 * st + 3, (NE - 1) % 2, 0, 3, True)
            scatter_both(last_st, w.h, w.nb, w.c)
            pool.wait_ge(scat[0], 16 * st)
            pool.wait_ge(scat[1], 16 * w.nbn)
            pool.tensor_tensor(tmp8[:, 0:1], epsc[:, :], epsc[:, :], ALU.add).then_inc(all_scattered, 1)
            for i in range(NT):
                pool.wait_ge(sqf_done, i + 1)
                pool.tensor_tensor(sf[:, 1, i:i + 1], sf[:, 0, i:i + 1], epsc[:, :], ALU.add).then_inc(sfm_done, 1)
                pool.wait_ge(sfm_done, i + 1)
                pool.tensor_tensor(sf[:, 2, i:i + 1], sf[:, 1, i:i + 1], nhalf[:, 0:1], ALU.pow).then_inc(rf_done, 1)
                if i >= 1:
                    pool.wait_ge(fg_done, i)
                    pool.tensor_tensor(x1[:, i - 1, :], x1[:, i - 1, :], fb[:, (i - 1) % 2, :], ALU.add).then_inc(o_done, 1)
            pool.wait_ge(fg_done, NT)
            pool.tensor_tensor(x1[:, NT - 1, :], x1[:, NT - 1, :], fb[:, (NT - 1) % 2, :], ALU.add).then_inc(o_done, 1)

        @block.scalar
        def _(act):
            act.wait_ge(cols_loaded, 16 * 8)
            act.activation(silc[:, 0, :], col[:, 0, :], ACT.Sigmoid).then_inc(sigc_done, 1)

            def square_sum(i):
                act.wait_ge(x_loaded[i // 2], 16)
                if i > 0:
                    act.wait_ge(ssx_done, i)
                act.activation(junk[:, :], xv[:, i, :], ACT.Square, accum_out=ssx[:, i:i + 1]).then_inc(ssx_done, 1)

            square_sum(0)
            square_sum(1)

            def split_hi(q, k, first):
                act.wait_ge(stage_loaded[k // 2], 16 * (q + 1))
                if not first:
                    if k < 3:
                        act.wait_ge(wi_used, 3 * q + k - 2)
                    else:
                        act.wait_ge(win_tile, NT * q)
                act.activation(wi_hi[:, 2 * k:2 * k + 2, :],
                               stage[:, k // 2, 1024 * (k % 2):1024 * (k % 2) + 1024].rearrange("p (k n) -> p k n", k=2),
                               ACT.Copy).then_inc(wi_hi_done, 1)

            def split_wout(k):
                act.wait_ge(stage_loaded[(k // 2) % 2], 16 * (NQ + 1 + k // 4))
                act.wait_ge(win_tile, NQ * NT)
                act.activation(sp_hi[:, k, :], stage[:, (k // 2) % 2, 1024 * (k % 2):1024 * (k % 2) + 1024],
                               ACT.Copy).then_inc(wo_hi_done, 1)

            for i in range(NT):
                act.wait_ge(hs_done, i + 1)
                act.activation(sp_hi[:, :, P * i:P * i + P], hbuf[:, i % 2], ACT.Copy).then_inc(hhi_done, 1)
                if i < 2:
                    split_hi(0, 2 * i, True)
                    split_hi(0, 2 * i + 1, True)
                if i % 2 == 1 and i + 1 < NT:
                    square_sum(i + 1)
                    square_sum(i + 2)

            def ut(q, b):
                act.wait_ge(ut_tr, QB * q + b + 1)
                if b < 2:
                    act.wait_ge(conv_done, QG * q)
                else:
                    act.wait_ge(conv_done, QG * q + BG * (b - 1))
                act.activation(ut_hi[:, b % 2, :, PAD:PAD + P],
                               ps[:, UT[b % 2], :].rearrange("p (g a) -> p g a", g=BG), ACT.Copy).then_inc(uthi_done, 1)

            def quarter(q, last):
                for i in range(NT):
                    act.wait_ge(pre_done, NT * q + i + 1)
                    act.activation(pre[:, i % 2, CQ:], pre[:, i % 2, CQ:], ACT.Sigmoid).then_inc(sig_done, 1)
                split = (lambda k: split_wout(k)) if last else (lambda k: split_hi(q + 1, k, False))
                ut(q, 0)
                ut(q, 1)
                split(0)
                split(1)
                ut(q, 2)
                split(2)
                ut(q, 3)
                split(3)

            act.wait_ge(const_made, 6)
            with act.Fori(0, NQ - 1) as q:
                quarter(q, False)
            quarter(NQ - 1, True)
            for k in range(4, KT):
                split_wout(k)
            act.wait_ge(v_done, NQ * QB)
            for j in range(4):
                act.wait_ge(brow_tr, j + 1)
                dst = rows[:, j, :] if j < 3 else h2[:, 0, :]
                b0 = (PY, PH)[j % 2]
                act.activation(dst, ps[:, b0:b0 + 2, :].rearrange("p b n -> p (b n)"), ACT.Copy).then_inc(rows_done, 1)

            def silu_tile(i, b):
                act.wait_ge(zt_done, i + 1)
                act.wait_ge(sl_done, i)
                for k in range(KT):
                    last = act.activation(s_full[:, k, :], ps[:, PZ + k // 4, P * (k % 4):P * (k % 4) + P], ACT.Silu,
                                          bias=col[:, 6, k:k + 1], scale=col[:, 5, k:k + 1])
                last.then_inc(s_done, 1)
                act.wait_ge(s_done, i + 1)
                if not (type(i) is int and i < 2):
                    act.wait_ge(yh_done, 2 * i - 2)
                act.activation(s_hi[:, b], s_full[:, :, :], ACT.Copy).then_inc(sh_done, 1)

            def h2t_copy(i):
                act.wait_ge(h2_tr, i + 1)
                act.wait_ge(rt_done, i)
                act.activation(h2t[:, :, :], ps[:, PH:PH + 2, :].rearrange("p b (k a) -> p (b k) a", a=P),
                               ACT.Copy).then_inc(h2t_done, 1)

            def step(i, b, first, last):
                if not last:
                    silu_tile(i + 1, 1 - b)
                if not first:
                    h2t_copy(i - 1)
                act.wait_ge(yb_done, 2 * i + 2)
                act.wait_ge(sqx_done, i)
                act.activation(junk2[:, :], yb[:, b, :], ACT.Square, scale=D ** -0.5,
                               accum_out=sy[:, b, 0:1]).then_inc(sqy_done, 1)
                act.wait_ge(x1_done, i + 1)
                act.wait_ge(sqy_done, i + 1)
                act.activation(junk2[:, :], x1[:, bass.ds(i, 1), :], ACT.Square, scale=D ** -0.5,
                               accum_out=sx[:, b, 0:1]).then_inc(sqx_done, 1)

            act.wait_ge(diag_done, 4)
            act.wait_ge(brow_tr, 4)
            silu_tile(0, 0)
            act.wait_ge(wo_lo_done, KT)
            step(0, 0, True, False)
            with act.Fori(0, NT // 2 - 1) as t:
                step(2 * t + 1, 1, False, False)
                step(2 * t + 2, 0, False, False)
            step(NT - 1, 1, False, True)
            h2t_copy(NT - 1)
            act.wait_ge(log_done, NT)
            act.activation(aff[:, :, :], logits[:, :, :], ACT.Sigmoid).then_inc(aff_done, 1)

            def landed(j, e):
                act.wait_ge(raw_loaded[0][j], 16 * ((e >> 1) + 1))
                if not (type(e) is int and e == 0):
                    act.wait_ge(raw_loaded[1][j], 16 * ((e + 1) >> 1))

            def high(idx, slot_, q, k, down, e, free):
                if free is not None:
                    act.wait_ge(pr_used, free)
                if down:
                    if k % 2 == 0:
                        landed(4 + k // 2, e)
                    act.activation(pr_hi[:, slot_, :], raw_d[:, bass.ds(q, 1), k, :].rearrange("p o n -> p (o n)"),
                                   ACT.Copy).then_inc(pr_hi_done, 1)
                    return
                if k % 4 == 0:
                    landed(2 * (k // 4), e)
                    landed(2 * (k // 4) + 1, e)
                act.activation(pr_hi[:, slot_, :].rearrange("p (g n) -> p g n", g=2),
                               raw_gu[:, bass.ds(q, 1), :, k, :].rearrange("p o g n -> p (o g) n"),
                               ACT.Copy).then_inc(pr_hi_done, 5 if (type(idx) is int and idx == 7) else 1)

            def x_hi(b, n):
                act.wait_ge(xt_tr, n + 1)
                act.activation(xt_hi[:, b], ps[:, TR:TR + 2, :].rearrange("p b (k a) -> p (b k) a", a=P),
                               ACT.Copy).then_inc(xth_done, 1)

            def silu(b, used, n, freed):
                act.wait_ge(pr_used, used)
                act.wait_ge(he_tr, freed)
                act.activation(he[:, b, :], ps[:, 2 * b, :], ACT.Silu).then_inc(sil_done, 1)

            def y_0(b, n, scattered):
                act.wait_ge(d0_done, n + 1)
                act.wait_ge(scat[b], 16 * scattered)
                act.activation(ys[:, b, 0:512], ps[:, DN, :], ACT.Copy).then_inc(y0_done, 1)

            def he_hi(b, n):
                act.wait_ge(he_tr, n + 1)
                act.activation(het_hi[:, b], ps[:, TR + b, :].rearrange("p (k a) -> p k a", a=P),
                               ACT.Copy).then_inc(heth_done, 1)

            act.wait_ge(rt_done, NT)
            act.wait_ge(h2_done, NT)
            for k in range(4):
                high(k, k, 0, k, False, 0, None)
            act.wait_ge(tables, 1)
            last_st = act.value_load(counts[0:1, 0:1], min_val=0, max_val=NST - 1)
            st = last_st + 1
            w = Step(act, 0)
            x_hi(0, 0)
            with act.If(w.h > 0):
                x_hi(1, 1)
            for k in range(4, KT):
                high(k, k % 4, 0, k, False, 0, k - 3)
            silu(0, 8, 0, 0)
            x_hi(0, w.cn)
            with act.If(w.h > 0):
                silu(1, 8, 1, 0)
            with act.If(w.hn > 0):
                x_hi(1, w.cn + 1)
            for k in range(4):
                high(12 + k, k, w.en & 1, k, False, w.en, 9 + k)
            he_hi(0, 0)
            with act.If(w.h > 0):
                he_hi(1, 1)
            with act.Fori(1, NST) as s:
                with act.If(s < st):
                    w = Step(act, s)
                    more = s + 1 < st
                    q = w.e & 1
                    for k in range(4, KT):
                        high(12 * s + k, k % 4, q, k, False, w.e, 12 * s + k - 3)
                    qp = w.ep & 1
                    for k in range(3):
                        high(12 * s + 8 + k, k, qp, k, True, w.ep, 12 * s + 5 + k)
                    silu(0, 12 * s + 8, w.c, w.c)
                    with act.If(more):
                        x_hi(0, w.cn)
                    with act.Else():
                        act.wait_ge(tables, 1)
                    high(12 * s + 11, 3, qp, 3, True, w.ep, 12 * s + 8)
                    with act.If(w.h > 0):
                        silu(1, 12 * s + 8, w.c + 1, w.c)
                    with act.If(w.hp > 0):
                        y_0(0, w.cp, s - 1)
                    with act.If(w.hn > 0):
                        x_hi(1, w.cn + 1)
                    with act.If(more):
                        qn = w.en & 1
                        for k in range(4):
                            high(12 * s + 12 + k, k, qn, k, False, w.en, 12 * s + 9 + k)
                    with act.Else():
                        act.wait_ge(tables, 1)
                    with act.If(w.hp > 0):
                        y_0(1, w.cp + 1, w.nbp)
                    with act.Else():
                        y_0(0, w.cp, s - 1)
                    he_hi(0, w.c)
                    with act.If(w.h > 0):
                        he_hi(1, w.c + 1)
                    act.wait_ge(tables, 1)
                act.wait_ge(tables, 1)
            w = Step(act, last_st)
            for k in range(FT):
                high(12 * st + k, k, (NE - 1) % 2, k, True, NE - 1, 12 * last_st + 9 + k)
            with act.If(w.h > 0):
                y_0(0, w.c, last_st)
                y_0(1, w.c + 1, w.nb)
            with act.Else():
                y_0(0, w.c, last_st)
            for i in range(NT):
                act.wait_ge(yl[i // 2], 32)
                if i >= 2:
                    act.wait_ge(o_done, i - 1)
                act.activation(fb[:, i % 2, :], y_all[:, 0, i, :], ACT.Copy, scale=gates[:, 0, i:i + 1]).then_inc(fa_done, 1)
                act.wait_ge(f_done, i + 1)
                act.wait_ge(sqf_done, i)
                act.activation(junk3[:, :], fb[:, i % 2, :], ACT.Square, scale=D ** -0.5,
                               accum_out=sf[:, 0, i:i + 1]).then_inc(sqf_done, 1)

        @block.vector
        def _(dve):
            dve.wait_ge(cols_loaded, 16 * 8)
            dve.wait_ge(sigc_done, 1)
            dve.tensor_tensor(silc[:, 1, :], silc[:, 0, :], col[:, 0, :], ALU.mult).then_inc(silc_done, 1)

            def normalise(i):
                dve.wait_ge(rsx_done, i // 2 + 1)
                dve.tensor_scalar(xv[:, i, :], xv[:, i, :], rsx[:, i:i + 1], None, ALU.mult).then_inc(xn_done, 1)

            normalise(0)
            normalise(1)
            dve.wait_ge(ada1_mod, 1)
            dve.tensor_tensor(a_sh[:, :, :], ps[:, MODB, 0:2 * KT].rearrange("p (s k) -> p s k", s=2),
                              bada[:, 0:2, :], ALU.add).then_inc(mod1_done, 1)
            dve.wait_ge(mod1_done, 1)
            dve.scalar_tensor_tensor(out=a_sh[:, 1, :], in0=a_sh[:, 1, :], scalar=1.0, in1=col[:, 1, :],
                                     op0=ALU.add, op1=ALU.mult).then_inc(mod1_done, 1)
            dve.wait_ge(mod1_done, 2)

            def split_lo(q, k):
                dve.wait_ge(wi_hi_done, 4 * q + k + 1)
                dve.tensor_tensor(wi_lo[:, 2 * k:2 * k + 2, :],
                                  stage[:, k // 2, 1024 * (k % 2):1024 * (k % 2) + 1024].rearrange("p (k n) -> p k n", k=2),
                                  wi_hi[:, 2 * k:2 * k + 2, :].bitcast(F32), ALU.subtract).then_inc(wi_lo_done, 1)

            def split_wout(k):
                dve.wait_ge(wo_hi_done, k + 1)
                dve.tensor_tensor(sp_lo[:, k, :], stage[:, (k // 2) % 2, 1024 * (k % 2):1024 * (k % 2) + 1024],
                                  sp_hi[:, k, :].bitcast(F32), ALU.subtract).then_inc(wo_lo_done, 1)

            def gained(i):
                dve.wait_ge(xt_done, i + 1)
                if i >= 2:
                    dve.wait_ge(hhi_done, i - 1)
                    dve.wait_ge(hlo_done, i - 1)
                b0 = UT[0] if i % 2 == 0 else CV[0]
                dve.tensor_tensor(hbuf[:, i % 2], ps[:, b0:b0 + 2, :].rearrange("p b (k a) -> p (b k) a", a=P),
                                  a_sh[:, 1, :].unsqueeze(2).to_broadcast([P, KT, P]), ALU.mult).then_inc(ht_done, 1)

            def h_lo(i):
                dve.wait_ge(hhi_done, i + 1)
                dve.tensor_tensor(sp_lo[:, :, P * i:P * i + P], hbuf[:, i % 2],
                                  sp_hi[:, :, P * i:P * i + P].bitcast(F32), ALU.subtract).then_inc(hlo_done, 1)

            for i in range(0, NT, 2):
                gained(i)
                gained(i + 1)
                for j in range(2):
                    h_lo(i + j)
                    if i == 0:
                        split_lo(0, 2 * j)
                        split_lo(0, 2 * j + 1)
                if i + 2 < NT:
                    normalise(i + 2)
                    normalise(i + 3)
            dve.wait_ge(hlo_done, NT)
            dve.wait_ge(const_made, 6)
            dve.wait_ge(eye_made, NT)

            def make_m(q, g):
                if g < MSLOTS:
                    dve.wait_ge(conv_done, QG * q)
                else:
                    dve.wait_ge(conv_done, QG * q + g - MSLOTS + 1)
                dve.tensor_tensor(mx_lo[:, g % MSLOTS],
                                  taps_lo[:, g, :].bitcast(F32).rearrange("p (d i) -> p d i", d=ND).unsqueeze(3)
                                  .to_broadcast([P, ND, NT, GC]),
                                  eye16[:, :].unsqueeze(1).unsqueeze(1).to_broadcast([P, ND, NT, GC]),
                                  ALU.mult).then_inc(mlo_done, 1)

            def ut(q, b):
                dve.wait_ge(uthi_done, QB * q + b + 1)
                dve.tensor_tensor(ut_lo[:, b % 2, :, PAD:PAD + P],
                                  ps[:, UT[b % 2], :].rearrange("p (g a) -> p g a", g=BG),
                                  ut_hi[:, b % 2, :, PAD:PAD + P].bitcast(F32), ALU.subtract).then_inc(utlo_done, 1)

            def gate(q, i):
                dve.wait_ge(sig_done, NT * q + i + 1)
                dve.tensor_tensor(u[:, :, GC * i:GC * i + GC], pre[:, i % 2, 0:CQ].rearrange("p (g c) -> p g c", c=GC),
                                  pre[:, i % 2, CQ:].rearrange("p (g c) -> p g c", c=GC),
                                  ALU.mult).then_inc(u_done, 1)

            def quarter(q, last):
                dve.wait_ge(ut_tr, QB * q)
                dve.wait_ge(brow_loaded, 16 * q + 16)
                for i in range(NT):
                    dve.wait_ge(win_tile, NT * q + i + 1)
                    dve.wait_ge(u_done, NT * q + max(i - 1, 0))
                    dve.tensor_tensor(pre[:, i % 2, :], ps[:, WI[i % 3], :], bin_row[:, :],
                                      ALU.add).then_inc(pre_done, 1)
                    if i >= 1:
                        gate(q, i - 1)
                    dve.wait_ge(ada_loaded[i % 2], 64 * q + 16 * (i // 2) + 16)
                    if i == 0:
                        dve.wait_ge(acc_col, q)
                        dve.tensor_scalar(acc[:, :], ada_stage[:, 0, :], silc[:, 1, 0:1], None,
                                          ALU.mult).then_inc(acc_done, 1)
                    else:
                        dve.wait_ge(acc_done, KT * q + i)
                        dve.scalar_tensor_tensor(out=acc[:, :], in0=ada_stage[:, i % 2, :], scalar=silc[:, 1, i:i + 1],
                                                 in1=acc[:, :], op0=ALU.mult, op1=ALU.add).then_inc(acc_done, 1)
                    if i < MSLOTS:
                        if i == 0:
                            dve.wait_ge(taps_split, 2 * q + 2)
                        make_m(q, i)
                gate(q, NT - 1)
                split = split_wout if last else (lambda k: split_lo(q + 1, k))
                ut(q, 0)
                ut(q, 1)
                dve.wait_ge(acc_col, q + 1)
                dve.tensor_tensor(modc[:, bass.ds(q, 1), :], ps[:, MODB, 16:16 + KT].unsqueeze(1),
                                  bada[:, bass.ds(q + 2, 1), :], ALU.add).then_inc(modc_done, 1)
                dve.wait_ge(bdw_loaded, 16 * q + 16)
                for b in range(QB):
                    if b + 1 < QB:
                        for g in range(BG):
                            make_m(q, BG * (b + 1) + g)
                    split(b)
                    dve.wait_ge(conv_done, QG * q + BG * (b + 1))
                    dve.tensor_tensor(
                        xv[:, :, bass.ds(q * CQ + BG * GC * b, BG * GC)].rearrange("p i (g c) -> p g i c", g=BG),
                        ps[:, CV[b % 2], :].rearrange("p (g i c) -> p g i c", g=BG, i=NT),
                        bdw_row[:, BG * GC * b:BG * GC * (b + 1)].rearrange("p (g c) -> p g c", g=BG).unsqueeze(2)
                        .to_broadcast([P, BG, NT, GC]), ALU.add).then_inc(v_done, 1)
                    if b + 2 < QB:
                        ut(q, b + 2)

            with dve.Fori(0, NQ - 1) as q:
                quarter(q, False)
            quarter(NQ - 1, True)
            dve.wait_ge(modc_done, NQ)
            dve.tensor_tensor(vcol[:, 0, :], modc[:, 0, :], col[:, 2, :], ALU.mult).then_inc(vcol_done, 1)
            dve.scalar_tensor_tensor(out=vcol[:, 1, :], in0=modc[:, 2, :], scalar=1.0, in1=col[:, 3, :],
                                     op0=ALU.add, op1=ALU.mult).then_inc(vcol_done, 1)
            dve.tensor_tensor(vcol[:, 2, :], modc[:, 3, :], col[:, 4, :], ALU.mult).then_inc(vcol_done, 1)
            dve.wait_ge(vcol_done, 3)
            dve.wait_ge(v_done, NQ * QB)
            for j, cc in enumerate((vcol[:, 0, :], vcol[:, 1, :], modc[:, 1, :], vcol[:, 2, :])):
                if j >= 2:
                    dve.wait_ge(brow_tr, j - 1)
                dve.tensor_tensor(diag[j % 2][:, :, :], ident[:, :].unsqueeze(2).to_broadcast([P, P, KT]),
                                  cc.unsqueeze(1).to_broadcast([P, P, KT]), ALU.mult).then_inc(diag_done, 1)

            def normalised(i, b, first):
                vi = xv[:, bass.ds(i, 1), :].rearrange("p o d -> p (o d)")
                if not first:
                    dve.wait_ge(mv_done, i)
                dve.bn_stats(stats[:, 0, :], vi[:, 0:512])
                dve.bn_stats(stats[:, 1, :], vi[:, 512:1024]).then_inc(stats_done, 1)
                dve.wait_ge(stats_done, i + 1)
                if not first:
                    dve.wait_ge(z_done, i)
                dve.memset(gap[:, :], 0.0)
                dve.bn_aggr(mv[:, b, :], stats[:, :, :]).then_inc(mv_done, 1)
                dve.wait_ge(lnr_done, i + 1)
                dve.wait_ge(mv_done, i + 1)
                if not first:
                    dve.wait_ge(zt_done, i)
                dve.tensor_scalar(zb[:, :], vi, mv[:, b, 0:1], lnr[:, b, 1:2],
                                  ALU.subtract, ALU.mult).then_inc(z_done, 1)

            def s_low(i, b, first):
                dve.wait_ge(sh_done, i + 1)
                if not first:
                    dve.wait_ge(yh_done, 2 * i - 2)
                dve.tensor_tensor(s_lo[:, b], s_full[:, :, :], s_hi[:, b].bitcast(F32), ALU.subtract).then_inc(sl_done, 1)

            def y_half(i, b, h):
                dve.wait_ge(yh_done, 2 * i + h + 1)
                cols = slice(512 * h, 512 * h + 512)
                dve.tensor_tensor(yb[:, b, cols], ps[:, PY + h, :], bout_row[:, cols], ALU.add).then_inc(yb_done, 1)

            def logits_of(i):
                dve.wait_ge(rt_done, i + 1)
                dve.tensor_copy(logits[:, bass.ds(i, 1), :], ps[:, PR, 0:NE].unsqueeze(1)).then_inc(log_done, 1)

            def step(i, b, first, last):
                if not last:
                    normalised(i + 1, 1 - b, False)
                y_half(i, b, 0)
                if not last:
                    s_low(i + 1, 1 - b, first)
                y_half(i, b, 1)
                dve.wait_ge(ry_done, i + 1)
                dve.scalar_tensor_tensor(out=yb[:, b, :], in0=yb[:, b, :], scalar=sy[:, b, 2:3], in1=rows[:, 0, :],
                                         op0=ALU.mult, op1=ALU.mult).then_inc(t_done, 1)
                dve.wait_ge(t_done, i + 1)
                xi = x1[:, bass.ds(i, 1), :].rearrange("p o d -> p (o d)")
                dve.wait_ge(xr_loaded[b], 16 * ((i - b) // 2) + 16)
                dve.tensor_tensor(xi, yb[:, b, :], xr[:, b, :], ALU.add).then_inc(x1_done, 1)
                if not first:
                    logits_of(i - 1)
                dve.wait_ge(rx_done, i + 1)
                if first:
                    dve.wait_ge(g3_stored, 16)
                elif not (type(i) is int and i < 2):
                    dve.wait_ge(h2_stored[b], 16 * ((i - b) // 2))
                    dve.wait_ge(h2_tr, i - 1)
                dve.scalar_tensor_tensor(out=h2[:, b, :], in0=xi, scalar=sx[:, b, 2:3], in1=rows[:, 1, :],
                                         op0=ALU.mult, op1=ALU.mult).then_inc(hg_done, 1)

            normalised(0, 0, True)
            dve.wait_ge(sh_done, 1)
            dve.tensor_tensor(s_lo[:, 0], s_full[:, :, :], s_hi[:, 0].bitcast(F32), ALU.subtract).then_inc(sl_done, 1)
            for k in range(4, KT):
                split_wout(k)
            dve.wait_ge(bout_loaded, 16)
            step(0, 0, True, False)
            with dve.Fori(0, NT // 2 - 1) as t:
                step(2 * t + 1, 1, False, False)
                step(2 * t + 2, 0, False, False)
            step(NT - 1, 1, False, True)
            logits_of(NT - 1)
            chain = [0]

            def then(ins):
                ins.then_inc(route_chain, 1)
                chain[0] += 1
                dve.wait_ge(route_chain, chain[0])

            def tt(o, a, b, op):
                then(dve.tensor_tensor(o, a, b, op))

            def ts(o, a, x_, y_, op0, op1=None):
                if op1 is None:
                    then(dve.tensor_scalar(o, a, x_, None, op0))
                else:
                    then(dve.tensor_scalar(o, a, x_, y_, op0, op1))

            def total(o, a, op=ALU.add):
                then(dve.tensor_reduce(o, a, axis=AX_X, op=op))

            dve.wait_ge(aff_done, 1)
            dve.wait_ge(rconst, NG + 5)
            dve.wait_ge(rt_done, NT)
            dve.wait_ge(h2_done, NT)
            dve.wait_ge(h2_stored[0], 16 * (NT // 2))
            dve.wait_ge(h2_stored[1], 16 * (NT // 2))
            tt(sel[:, :, :], aff[:, :, :], rb_row[:, :].unsqueeze(1).to_broadcast([P, NT, NE]), ALU.add)
            s4 = sel[:, :, :].rearrange("p t (g h j) -> p (t g) h j", g=NG, h=2)
            tt(pair_max[:, :, :], s4[:, :, :, 0], s4[:, :, :, 1], ALU.max)
            tt(pair_min[:, :, :], s4[:, :, :, 0], s4[:, :, :, 1], ALU.min)

            def g6(j):
                return gs[:, j].rearrange("p t g -> p (t g)")

            tt(g6(0), pair_max[:, :, 0], pair_max[:, :, 1], ALU.max)
            tt(g6(1), pair_max[:, :, 0], pair_max[:, :, 1], ALU.min)
            tt(g6(2), pair_min[:, :, 0], pair_min[:, :, 1], ALU.max)
            tt(g6(1), g6(1), g6(2), ALU.max)
            tt(g6(0), g6(0), g6(1), ALU.add)
            total(gmax[:, 0, :], gs[:, 0], ALU.max)
            tt(gs[:, 3], gs[:, 0], gmax[:, 0, :].unsqueeze(2).to_broadcast([P, NT, NG]), ALU.is_ge)
            tt(gs[:, 3], gs[:, 3], desc4[:, :].unsqueeze(1).to_broadcast([P, NT, NG]), ALU.mult)
            total(gmax[:, 1, :], gs[:, 3], ALU.max)
            tt(gs[:, 4], gs[:, 3], gmax[:, 1, :].unsqueeze(2).to_broadcast([P, NT, NG]), ALU.is_equal)
            sg = sel[:, :, :].rearrange("p t (g j) -> p (t g) j", g=NG)
            inner = sg.unsqueeze(2).to_broadcast([P, NT * NG, EG, EG])
            outer = sg.unsqueeze(3).to_broadcast([P, NT * NG, EG, EG])
            tt(beats[:, 0], inner, outer, ALU.is_gt)
            tt(beats[:, 1], inner, outer, ALU.is_equal)
            tt(beats[:, 1], beats[:, 1], lt4[:, :, :].unsqueeze(1).to_broadcast([P, NT * NG, EG, EG]), ALU.mult)
            tt(beats[:, 0], beats[:, 0], beats[:, 1], ALU.add)
            total(rank[:, :, :].rearrange("p t (g j) -> p (t g) j", g=NG), beats[:, 0])
            for k in range(2):
                ts(mk[:, k], rank[:, :, :], float(k), None, ALU.is_equal)
                tt(mk[:, k].rearrange("p t (g j) -> p (t g) j", g=NG), mk[:, k].rearrange("p t (g j) -> p (t g) j", g=NG),
                   g6(4).unsqueeze(2).to_broadcast([P, NT * NG, EG]), ALU.mult)
            then(dve.memset(m9[:, NT, :], 0.0))
            tt(m9[:, 0:NT, :], mk[:, 0], mk[:, 1], ALU.add)
            marks["chosen"] = chain[0]
            for k in range(2):
                tt(prod[:, NT * k:NT * k + NT, :], mk[:, k], aff[:, :, :], ALU.mult)
            total(ak[:, :, :].rearrange("p k t -> p (k t)"), prod[:, :, :])
            tt(den[:, 0, :], ak[:, 0, :], ak[:, 1, :], ALU.add)
            then(dve.reciprocal(den[:, 1, :], den[:, 0, :]))
            tt(gates[:, :, :], ak[:, :, :], den[:, 1, :].unsqueeze(1).to_broadcast([P, 2, NT]), ALU.mult)
            dve.wait_ge(pos_done, 1)
            then(dve.tensor_copy(cnt[:, 0, :], ps[:, PZ, NT * NE:NT * NE + NE]))
            ts(cnt[:, 1, :], cnt[:, 0, :], float(ST_ROWS), None, ALU.is_gt)
            for j in (2, 3):
                then(dve.scalar_tensor_tensor(out=cnt[:, 1, :], in0=cnt[:, 0, :], scalar=float(j * ST_ROWS),
                                              in1=cnt[:, 1, :], op0=ALU.is_gt, op1=ALU.add))
            ts(cnt[:, 1, :], cnt[:, 1, :], 1.0, None, ALU.add)
            tt(prod16[:, :, :], le16[:, :, :], cnt[:, 1, :].unsqueeze(1).to_broadcast([P, NE, NE]), ALU.mult)
            total(cnt[:, 2, :], prod16[:, :, :])
            tt(cnt[:, 3, :], cnt[:, 2, :], cnt[:, 1, :], ALU.subtract)
            ts(cnt[:, 4, :], cnt[:, 3, :], float(ST_ROWS), None, ALU.mult)
            tt(cnt[:, 5, :], cnt[:, 4, :], cnt[:, 0, :], ALU.add)
            tt(pos[:, :, :], ps[:, PZ, 0:NT * NE].rearrange("p (t e) -> p t e", e=NE),
               cnt[:, 4, :].unsqueeze(1).to_broadcast([P, NT, NE]), ALU.add)
            for k in range(2):
                tt(prod[:, NT * k:NT * k + NT, :], mk[:, k], pos[:, :, :], ALU.mult)
            total(slot[:, :], prod[:, :, :])
            then(dve.tensor_copy(slot_i[:, 0, :], slot[:, :]))
            ts(slot_i[:, 1, :], slot_i[:, 0, :], 7, None, ALU.arith_shift_right)
            ts(slot_i[:, 2, :], slot_i[:, 0, :], P - 1, None, ALU.bitwise_and)
            then(dve.tensor_copy(slot_f[:, :, :], slot_i[:, 1:3, :]))
            tt(oh_p[:, :, :], iota[:, :].unsqueeze(1).to_broadcast([P, 2 * NT, P]),
               slot_f[:, 1, :].unsqueeze(2).to_broadcast([P, 2 * NT, P]), ALU.is_equal)
            tt(oh_t[:, :, :], iota[:, 0:2 * NSTC].unsqueeze(1).to_broadcast([P, 2 * NT, 2 * NSTC]),
               slot_f[:, 0, :].unsqueeze(2).to_broadcast([P, 2 * NT, 2 * NSTC]), ALU.is_equal)
            tt(oh_t[:, :, :], oh_t[:, :, :], tok1[:, :].unsqueeze(2).to_broadcast([P, 2 * NT, 2 * NSTC]), ALU.mult)
            marks["slots"] = chain[0]
            ts(start[:, 0, :], iota[:, 0:NSTC], float(ST_ROWS), None, ALU.mult)
            ts(start[:, 1, :], start[:, 0, :], float(P), None, ALU.add)
            sh3 = [P, NSTC, NE]
            srow = iota[:, 0:NSTC].unsqueeze(2).to_broadcast(sh3)
            tt(st_le[:, :, :], cnt[:, 2, :].unsqueeze(1).to_broadcast(sh3), srow, ALU.is_le)
            tt(st_in[:, :, :], cnt[:, 3, :].unsqueeze(1).to_broadcast(sh3), srow, ALU.is_le)
            tt(st_in[:, :, :], st_in[:, :, :], st_le[:, :, :], ALU.subtract)
            tt(st_ab[:, :, :], cnt[:, 5, :].unsqueeze(1).to_broadcast(sh3),
               start[:, 1, :].unsqueeze(2).to_broadcast(sh3), ALU.is_gt)
            tt(st_ab[:, :, :], st_ab[:, :, :], st_in[:, :, :], ALU.mult)
            then(dve.memset(e_of[:, :], 0.0))
            then(dve.memset(hb_of[:, :, :], 0.0))
            total(e_of[:, 1:NSTC + 1], st_le[:, :, :])
            total(hb_of[:, 0, 16:16 + NSTC], st_ab[:, :, :])
            then(dve.tensor_copy(word_f[:, 1, :], hb_of[:, 0, 16:16 + NSTC]))
            marks["hb"] = chain[0]
            then(dve.scalar_tensor_tensor(out=word_f[:, 0, :], in0=e_of[:, 1:NSTC + 1], scalar=32.0,
                                          in1=e_of[:, 0:NSTC], op0=ALU.mult, op1=ALU.add))
            for scale_, v in ((1024.0, e_of[:, 2:NSTC + 2]), (2.0 ** 15, hb_of[:, 0, 15:15 + NSTC]),
                              (2.0 ** 16, hb_of[:, 0, 16:16 + NSTC]), (2.0 ** 17, hb_of[:, 0, 17:17 + NSTC])):
                then(dve.scalar_tensor_tensor(out=word_f[:, 0, :], in0=v, scalar=scale_,
                                              in1=word_f[:, 0, :], op0=ALU.mult, op1=ALU.add))
            for j, d in enumerate((1, 2, 4, 8, 16)):
                tt(hb_of[:, (j + 1) % 2, 16:16 + NSTC], hb_of[:, j % 2, 16:16 + NSTC],
                   hb_of[:, j % 2, 16 - d:16 - d + NSTC], ALU.add)
            then(dve.scalar_tensor_tensor(out=word_f[:, 0, :], in0=hb_of[:, 1, 14:14 + NSTC], scalar=2.0 ** 18,
                                          in1=word_f[:, 0, :], op0=ALU.mult, op1=ALU.add))
            then(dve.tensor_copy(words[:, :], word_f[:, 0, :]))
            ts(ct_i[:, :], cnt[:, 2, :], -1.0, None, ALU.add)
            ts(counts[:, 0:1], cnt[:, 2, NE - 1:NE], -1.0, None, ALU.add)
            then(dve.tensor_copy(counts[:, 1:2], hb_of[:, 1, 15 + NSTC:16 + NSTC]))
            dve.wait_ge(slots_done, 1)
            ts(dest[:, :], ps[:, PZ + 1, 0:2 * NSTC], -1.0, None, ALU.add)
            ts(src[:, :], dest[:, :], S - 1, None, ALU.bitwise_and)
            then(dve.memset(gap[:, :], 0.0))
            dve.tensor_copy(gap[:, :], gmax[:, 0, 0:1]).then_inc(tables, 1)

            last_st = dve.value_load(counts[0:1, 0:1], min_val=0, max_val=NST - 1)
            st = last_st + 1

            def low(turn, slot_, q, k, down, inc):
                dve.wait_ge(pr_hi_done, 4 * turn + slot_ + 1)
                if down:
                    dve.tensor_tensor(pr_lo[:, slot_, :], raw_d[:, bass.ds(q, 1), k, :].rearrange("p o n -> p (o n)"),
                                      pr_hi[:, slot_, :].bitcast(F32), ALU.subtract).then_inc(pr_lo_dve, inc)
                else:
                    dve.tensor_tensor(pr_lo[:, slot_, :].rearrange("p (g n) -> p g n", g=2),
                                      raw_gu[:, bass.ds(q, 1), :, k, :].rearrange("p o g n -> p (o g) n"),
                                      pr_hi[:, slot_, :].bitcast(F32).rearrange("p (g n) -> p g n", g=2),
                                      ALU.subtract).then_inc(pr_lo_dve, inc)

            def x_lo(b, n):
                dve.wait_ge(xth_done, n + 1)
                dve.tensor_tensor(xt_lo[:, b], ps[:, TR:TR + 2, :].rearrange("p b (k a) -> p (b k) a", a=P),
                                  xt_hi[:, b].bitcast(F32), ALU.subtract).then_inc(xtl_done, 1)

            def times_up(b, n):
                dve.wait_ge(sil_done, n + 1)
                dve.tensor_tensor(he[:, b, :], he[:, b, :], ps[:, 2 * b + 1, :], ALU.mult).then_inc(he_done, 1)

            def y_1(b, sem_, n, scattered):
                dve.wait_ge(sem_, n)
                dve.wait_ge(scat[b], 16 * scattered)
                dve.tensor_copy(ys[:, b, 512:1024], ps[:, DN + 1, :]).then_inc(y1_done, 1)

            def he_lo(b, n):
                dve.wait_ge(heth_done, n + 1)
                dve.tensor_tensor(het_lo[:, b], ps[:, TR + b, :].rearrange("p (k a) -> p k a", a=P),
                                  het_hi[:, b].bitcast(F32), ALU.subtract).then_inc(hetl_done, 1)

            w = Step(dve, 0)
            for k in range(3):
                low(0, k, 0, k, False, 1)
            x_lo(0, 0)
            with dve.If(w.h > 0):
                x_lo(1, 1)
            for k in range(3):
                low(1, k, 0, k + 4, False, 4 if k == 2 else 1)
            times_up(0, 0)
            x_lo(0, w.cn)
            with dve.If(w.h > 0):
                times_up(1, 1)
            with dve.If(w.hn > 0):
                x_lo(1, w.cn + 1)
            for k in range(3):
                low(3, k, w.en & 1, k, False, 1)
            he_lo(0, 0)
            with dve.If(w.h > 0):
                he_lo(1, 1)
            with dve.Fori(1, NST) as s:
                with dve.If(s < st):
                    w = Step(dve, s)
                    more = s + 1 < st
                    q = w.e & 1
                    for k in range(3):
                        low(3 * s + 1, k, q, k + 4, False, 1)
                    qp = w.ep & 1
                    for k in range(3):
                        low(3 * s + 2, k, qp, k, True, 1)
                    times_up(0, w.c)
                    with dve.If(more):
                        x_lo(0, w.cn)
                    with dve.Else():
                        dve.wait_ge(tables, 1)
                    with dve.If(w.h > 0):
                        times_up(1, w.c + 1)
                    with dve.If(w.hp > 0):
                        y_1(0, d1_done, w.nbp + 1, s - 1)
                    with dve.If(w.hn > 0):
                        x_lo(1, w.cn + 1)
                    with dve.If(more):
                        qn = w.en & 1
                        for k in range(3):
                            low(3 * s + 3, k, qn, k, False, 1)
                    with dve.Else():
                        dve.wait_ge(tables, 1)
                    with dve.If(w.hp > 0):
                        y_1(1, pr_used, 12 * s + 12, w.nbp)
                    with dve.Else():
                        y_1(0, pr_used, 12 * s + 12, s - 1)
                    he_lo(0, w.c)
                    with dve.If(w.h > 0):
                        he_lo(1, w.c + 1)
                    dve.wait_ge(tables, 1)
                dve.wait_ge(tables, 1)
            w = Step(dve, last_st)
            for k in range(3):
                low(3 * st, k, (NE - 1) % 2, k, True, 1)
            with dve.If(w.h > 0):
                y_1(0, d1_done, w.nb + 1, last_st)
                y_1(1, pr_used, 12 * st + 4, w.nb)
            with dve.Else():
                y_1(0, pr_used, 12 * st + 4, last_st)
            dve.wait_ge(g3_loaded, 16)
            for i in range(NT):
                b = i % 2
                dve.wait_ge(fa_done, i + 1)
                dve.scalar_tensor_tensor(out=fb[:, b, :], in0=y_all[:, 1, i, :], scalar=gates[:, 1, i:i + 1],
                                         in1=fb[:, b, :], op0=ALU.mult, op1=ALU.add).then_inc(f_done, 1)
                dve.wait_ge(rf_done, i + 1)
                dve.scalar_tensor_tensor(out=fb[:, b, :], in0=fb[:, b, :], scalar=sf[:, 2, i:i + 1], in1=g3[:, :],
                                         op0=ALU.mult, op1=ALU.mult).then_inc(fg_done, 1)

        @block.tensor
        def _(pe):
            pe.wait_ge(const_made, 6)
            pe.wait_ge(silc_done, 1)
            for k in range(KT):
                pe.wait_ge(ada1_loaded[k // 2], 16)
                for s in range(2):
                    for j in range(KT):
                        last = pe.matmul(ps[:, MODB, KT * s + j:KT * s + j + 1],
                                         ada_first[:, k, bass.ds(D * s + j, P, step=KT)], silc[:, 1, k:k + 1],
                                         start=(k == 0 and s == 0 and j == 0), stop=(k == KT - 1),
                                         skip_group_check=True)
            last.then_inc(ada1_mod, 1)
            for i in range(NT):
                pe.wait_ge(xn_done, i + 1)
                if i >= 2:
                    pe.wait_ge(ht_done, i - 1)
                b0 = UT[0] if i % 2 == 0 else CV[0]
                for k in range(KT):
                    last = pe.transpose(ps[:, b0 + k // 4, P * (k % 4):P * (k % 4) + P],
                                        xv[:, i, bass.ds(k, P, step=KT)], ident[:, :])
                last.then_inc(xt_done, 1)

            def quarter(q):
                for i in range(NT):
                    pe.wait_ge(hlo_done, i + 1)
                    if i >= 3:
                        pe.wait_ge(pre_done, NT * q + i - 2)
                    o = ps[:, WI[i % 3], :]
                    for k in range(KT):
                        if i == 0 and k % 2 == 0:
                            pe.wait_ge(wi_lo_done, 4 * q + k // 2 + 1)
                        tok = slice(P * i, P * i + P)
                        pe.matmul(o, sp_hi[:, k, tok], wi_hi[:, k, :], start=(k == 0), stop=False)
                        pe.matmul(o, sp_hi[:, k, tok], wi_lo[:, k, :], start=False, stop=False)
                        last = pe.matmul(o, sp_lo[:, k, tok], wi_hi[:, k, :], start=False, stop=(k == KT - 1))
                        if i == NT - 1 and k % 2 == 1 and k < KT - 1:
                            last.then_inc(wi_used, 1)
                    last.then_inc(win_tile, 1)
                pe.wait_ge(acc_done, KT * q + KT)
                pe.wait_ge(modc_done, q)
                for j in range(KT):
                    last = pe.matmul(ps[:, MODB, 16 + j:17 + j], acc[:, bass.ds(j, P, step=KT)], ones[:, 0:1],
                                     start=(j == 0), stop=True, skip_group_check=True)
                last.then_inc(acc_col, 1)

                def turn(b):
                    if b == 0:
                        pe.wait_ge(u_done, NT * q + NT)
                    if b >= 2:
                        pe.wait_ge(utlo_done, QB * q + b - 1)
                    for g in range(BG):
                        last = pe.transpose(ps[:, UT[b % 2], P * g:P * g + P], u[:, BG * b + g, :], ident[:, :])
                    last.then_inc(ut_tr, 1)

                def conv(b):
                    pe.wait_ge(utlo_done, QB * q + b + 1)
                    if b < 2:
                        pe.wait_ge(v_done, QB * q)
                    else:
                        pe.wait_ge(v_done, QB * q + b - 1)
                    for g in range(BG):
                        n = BG * b + g
                        m = n % MSLOTS
                        pe.wait_ge(mhi_done, QG * q + n + 1)
                        pe.wait_ge(mlo_done, QG * q + n + 1)
                        o = ps[:, CV[b % 2], P * g:P * g + P]
                        for d in range(ND):
                            tok = slice(2 * PAD - d, 2 * PAD - d + P)
                            uh, ul = ut_hi[:, b % 2, g, tok], ut_lo[:, b % 2, g, tok]
                            mh = mx_hi[:, m, d].rearrange("p i c -> p (i c)")
                            ml = mx_lo[:, m, d].rearrange("p i c -> p (i c)")
                            pe.matmul(o, uh, mh, start=(d == 0), stop=False)
                            pe.matmul(o, uh, ml, start=False, stop=False)
                            last = pe.matmul(o, ul, mh, start=False, stop=(d == ND - 1))
                        last.then_inc(conv_done, 1)

                turn(0)
                turn(1)
                conv(0)
                turn(2)
                conv(1)
                turn(3)
                conv(2)
                conv(3)

            with pe.Fori(0, NQ) as q:
                quarter(q)

            for j in range(4):
                pe.wait_ge(diag_done, j + 1)
                if j >= 2:
                    pe.wait_ge(rows_done, j - 1)
                b0 = (PY, PH)[j % 2]
                for h in range(2):
                    last = pe.matmul(ps[:, b0 + h, :], ones[:, :],
                                     diag[j % 2][:, 64 * h:64 * h + 64, :].rearrange("p j k -> p (j k)"),
                                     start=True, stop=True)
                last.then_inc(brow_tr, 1)

            def turn_z(i):
                pe.wait_ge(z_done, i + 1)
                pe.wait_ge(s_done, i)
                for k in range(KT):
                    last = pe.transpose(ps[:, PZ + k // 4, P * (k % 4):P * (k % 4) + P],
                                        zb[:, bass.ds(k, P, step=KT)], ident[:, :])
                last.then_inc(zt_done, 1)

            def y_mm(i, b, h, ks):
                cols = slice(512 * h, 512 * h + 512)
                o = ps[:, PY + h, :]
                for k in ks:
                    if k == 0:
                        pe.wait_ge(sl_done, i + 1)
                        pe.wait_ge(yb_done, 2 * i)
                    pe.matmul(o, s_hi[:, b, k, :], sp_hi[:, k, cols], start=(k == 0), stop=False)
                    pe.matmul(o, s_hi[:, b, k, :], sp_lo[:, k, cols], start=False, stop=False)
                    last = pe.matmul(o, s_lo[:, b, k, :], sp_hi[:, k, cols], start=False, stop=(k == KT - 1))
                if ks[-1] == KT - 1:
                    last.then_inc(yh_done, 1)

            def turn_h2(i, b):
                pe.wait_ge(h2_done, i + 1)
                pe.wait_ge(h2t_done, i)
                for k in range(KT):
                    last = pe.transpose(ps[:, PH + k // 4, P * (k % 4):P * (k % 4) + P],
                                        h2[:, b, bass.ds(k, P, step=KT)], ident[:, :])
                last.then_inc(h2_tr, 1)

            def route(i):
                pe.wait_ge(h2t_done, i + 1)
                pe.wait_ge(log_done, i)
                for k in range(KT):
                    last = pe.matmul(ps[:, PR, 0:NE], h2t[:, k, :], rwt[:, k, :], start=(k == 0), stop=(k == KT - 1))
                last.then_inc(rt_done, 1)

            def step(i, b, first, last):
                y_mm(i, b, 0, list(range(KT)))
                if not last:
                    turn_z(i + 1)
                y_mm(i, b, 1, list(range(KT)))
                if not first:
                    turn_h2(i - 1, 1 - b)
                    route(i - 1)

            turn_z(0)
            pe.wait_ge(rw_loaded, 32)
            pe.wait_ge(rows_done, 4)
            pe.wait_ge(wo_lo_done, KT)
            step(0, 0, True, False)
            with pe.Fori(0, NT // 2 - 1) as t:
                step(2 * t + 1, 1, False, False)
                step(2 * t + 2, 0, False, False)
            step(NT - 1, 1, False, True)
            turn_h2(NT - 1, 1)
            route(NT - 1)
            pe.wait_ge(route_chain, marks["chosen"])
            pe.matmul(ps[:, PZ, 0:NE * (NT + 1)], tri[:, :], m9[:, :, :].rearrange("p t e -> p (t e)"),
                      start=True, stop=False, skip_group_check=True)
            for t in range(NT):
                last = pe.matmul(ps[:, PZ, NE * (t + 1):NE * (NT + 1)], ones[:, :],
                                 m9[:, t:t + 1, :].to_broadcast([P, NT - t, NE]),
                                 start=False, stop=(t == NT - 1), skip_group_check=True)
            last.then_inc(pos_done, 1)
            pe.wait_ge(route_chain, marks["slots"])
            for j in range(2 * NT):
                last = pe.matmul(ps[:, PZ + 1, 0:2 * NSTC], oh_p[:, j, :], oh_t[:, j, :],
                                 start=(j == 0), stop=(j == 2 * NT - 1))
            last.then_inc(slots_done, 1)

            pe.wait_ge(tables, 1)
            last_st = pe.value_load(counts[0:1, 0:1], min_val=0, max_val=NST - 1)
            st = last_st + 1

            def turn_x(b, n, held, landed):
                pe.wait_ge(gath[b], 16 * landed)
                pe.wait_ge(xtl_done, n)
                pe.wait_ge(hetl_done, held)
                for k in range(KT):
                    last = pe.transpose(ps[:, TR + k // 4, P * (k % 4):P * (k % 4) + P],
                                        xg[:, b, bass.ds(k, P, step=KT)], ident[:, :])
                last.then_inc(xt_tr, 1)

            def pair(turn, slot_):
                if slot_ < 3:
                    pe.wait_ge(pr_lo_dve, 3 * turn + slot_ + 1)
                else:
                    pe.wait_ge(pr_lo_pool, turn + 1)

            def gate_up(turn, c, cn, h, last_inc):
                pe.wait_ge(xtl_done, cn)
                pe.wait_ge(he_done, c)

                def tile(b, k):
                    sl = k % RING
                    g, up = ps[:, 2 * b, :], ps[:, 2 * b + 1, :]
                    first, end = k == 0, k == KT - 1
                    xh, xl = xt_hi[:, b, k, :], xt_lo[:, b, k, :]
                    pe.matmul(g, xh, pr_hi[:, sl, 0:F], start=first, stop=False)
                    pe.matmul(up, xh, pr_hi[:, sl, F:], start=first, stop=False)
                    pe.matmul(g, xh, pr_lo[:, sl, 0:F], start=False, stop=False)
                    pe.matmul(up, xh, pr_lo[:, sl, F:], start=False, stop=False)
                    pe.matmul(g, xl, pr_hi[:, sl, 0:F], start=False, stop=end)
                    return pe.matmul(up, xl, pr_hi[:, sl, F:], start=False, stop=end)

                def all_tiles(two):
                    for k in range(KT):
                        pair(turn + k // RING, k % RING)
                        last = tile(0, k)
                        if two:
                            last = tile(1, k)
                        last.then_inc(pr_used, last_inc if k == KT - 1 else 1)

                with pe.If(h > 0):
                    all_tiles(True)
                with pe.Else():
                    all_tiles(False)

            def down(b, turn, before, by_half):
                pe.wait_ge(y0_done, before)
                pe.wait_ge(y1_done, before)

                def part(k, h):
                    cols = slice(512 * h, 512 * h + 512)
                    o = ps[:, DN + h, :]
                    pe.matmul(o, het_hi[:, b, k, :], pr_hi[:, k, cols], start=(k == 0), stop=False)
                    pe.matmul(o, het_hi[:, b, k, :], pr_lo[:, k, cols], start=False, stop=False)
                    return pe.matmul(o, het_lo[:, b, k, :], pr_hi[:, k, cols], start=False, stop=(k == FT - 1))

                if by_half:
                    for h in range(2):
                        for k in range(FT):
                            if h == 0:
                                pair(turn, k)
                            last = part(k, h)
                        last.then_inc(d1_done if h else d0_done, 1)
                else:
                    for k in range(FT):
                        if b == 0:
                            pair(turn, k)
                        last = part(k, 0)
                        if k == FT - 1:
                            last.then_inc(d0_done, 1)
                        part(k, 1).then_inc(pr_used, 1)

            def turn_he(b, made, xs):
                pe.wait_ge(he_done, made)
                pe.wait_ge(xtl_done, xs)
                for k in range(FT):
                    last = pe.transpose(ps[:, TR + b, P * k:P * k + P], he[:, b, bass.ds(k, P, step=FT)], ident[:, :])
                last.then_inc(he_tr, 1)

            w = Step(pe, 0)
            turn_x(0, 0, 0, 1)
            with pe.If(w.h > 0):
                turn_x(1, 1, 0, 1)
            gate_up(0, w.c, w.cn, w.h, 5)
            turn_x(0, w.cn, 0, 2)
            with pe.If(w.hn > 0):
                turn_x(1, w.cn + 1, 0, w.h + 1)
            turn_he(0, 1, w.cn + 1 + w.hn)
            with pe.If(w.h > 0):
                turn_he(1, 2, w.cn + 1 + w.hn)
            with pe.Fori(1, NST) as s:
                with pe.If(s < st):
                    w = Step(pe, s)
                    more = s + 1 < st
                    gate_up(3 * s, w.c, w.cn, w.h, 1)
                    with pe.If(more):
                        turn_x(0, w.cn, w.c, s + 2)
                    with pe.Else():
                        pe.wait_ge(tables, 1)
                    pe.wait_ge(hetl_done, w.c)
                    with pe.If(w.hp > 0):
                        down(0, 3 * s + 2, w.cp, True)
                    with pe.Else():
                        down(0, 3 * s + 2, w.cp, False)
                    with pe.If(w.hn > 0):
                        turn_x(1, w.cn + 1, w.c, w.nbn + 1)
                    with pe.If(w.hp > 0):
                        down(1, 3 * s + 2, w.cp + 1, False)
                    xs = w.cn + w.hn + more
                    turn_he(0, w.c + 1, xs)
                    with pe.If(w.h > 0):
                        turn_he(1, w.c + 2, xs)
                    pe.wait_ge(tables, 1)
                pe.wait_ge(tables, 1)
            w = Step(pe, last_st)
            pe.wait_ge(hetl_done, w.cn)
            with pe.If(w.h > 0):
                down(0, 3 * st, w.c, True)
                down(1, 3 * st, w.c + 1, False)
            with pe.Else():
                down(0, 3 * st, w.c, False)


def kernel(**inputs):
    import numpy as _np
    import concourse.bacc as _bacc
    from concourse import mybir as _mybir
    from concourse.bass_utils import run_bass_kernel_spmd as _run

    a = {n: _np.ascontiguousarray(v) for n, v in inputs.items()}
    laid = {
        "x": a["x"], "c": a["c"], "w_ada": a["w_ada"], "b_ada": a["b_ada"],
        "g_mix_pre": a["g_mix_pre"], "g_mix_post": a["g_mix_post"],
        "g_ffn_pre": a["g_ffn_pre"], "g_ffn_post": a["g_ffn_post"],
        "w_in": a["conv_w_in"][0].reshape(P, KT, 2, NQ, CQ).transpose(3, 0, 1, 2, 4).reshape(NQ, P, KT * 2 * CQ),
        "b_in": a["conv_b_in"][0].reshape(2, NQ, CQ).transpose(1, 0, 2).reshape(NQ, 2 * CQ),
        "w_dw": a["conv_w_dw"][0][::-1].reshape(TAPS, NQ, QG, GC).transpose(1, 3, 2, 0),
        "b_dw": a["conv_b_dw"], "ln_g": a["conv_ln_g"], "ln_b": a["conv_ln_b"],
        "w_out": a["conv_w_out"], "b_out": a["conv_b_out"],
        "router_w": a["router_w"], "router_b": a["router_b"],
        "w_gate": a["exp_w_gate"], "w_up": a["exp_w_up"], "w_down": a["exp_w_down"],
    }
    nc = _bacc.Bacc("TRN2", target_bir_lowering=False, num_devices=1, dynamic_dma_scratch_size=8192)
    arrays, args = {}, []
    for name, v in laid.items():
        v = _np.ascontiguousarray(v)
        arrays[f"in_{name}"] = v
        args.append(nc.dram_tensor(f"in_{name}", v.shape, _mybir.dt.from_np(v.dtype), kind="ExternalInput").ap())
    args.append(nc.dram_tensor("out_0", (1, S, D), F32, kind="ExternalOutput").ap())
    dit_layer(nc, *args)
    r = _run(nc, [arrays], core_ids=[0])
    return r.results[0]["out_0"]
```

```python
from contextlib import ExitStack

import concourse.bass as bass
from concourse import mybir

F32 = mybir.dt.float32
F32R = mybir.dt.float32r
I32 = mybir.dt.int32
U32 = mybir.dt.uint32
ALU = mybir.AluOpType
ACT = mybir.ActivationFunctionType
AX_X = mybir.AxisListType.X

P = 128
D = 1024
S = 1024
NT = S // P
KT = D // P
F = 512
FT = F // P
NE = 16
NG = 4
EG = NE // NG
EPS = 1e-6

NQ = 4
CQ = D // NQ
TAPS = 31
GC = 16
QG = CQ // GC
BG = 4
QB = QG // BG
CG = 2
QH = QG // CG
ND = 5
NM = ND * NT
PAD = 2
MSLOTS = 4

ST_ROWS = 2 * P
NST = 23
NSTC = NST + 1
CHUNKS = 6
FB = 4
RING = 4
KB = 1024
ONE = 1
ONE_DMA = 16


def dit_layer(nc, x, c, w_ada, b_ada, g_mix_pre, g_mix_post, g_ffn_pre, g_ffn_post,
              w_in, b_in, w_dw, b_dw, ln_g, ln_b, w_out, b_out, router_w, router_b,
              w_gate, w_up, w_down, out):
    ctx = ExitStack()
    with ctx:
        def sem(name):
            return ctx.enter_context(nc.semaphore(name))

        limit = nc.sbuf_top
        base = (nc.sbuf_base + 31) // 32 * 32
        arena = ctx.enter_context(nc.sbuf_tensor("arena", [P, (limit - base - 64) // 4], F32))
        R0, R1, R2 = base, base + 96 * KB, base + 128 * KB
        top = [R2 + 84736]

        def at(name, shape, dt, offset):
            return nc.alloc_sbuf_tensor_at(name, shape, dt, offset=offset)

        def small(name, shape, dt=F32):
            n = 4
            for d in shape[1:]:
                n *= d
            t = at(name, shape, dt, top[0])
            top[0] += (n + 31) // 32 * 32
            assert top[0] <= limit, (name, top[0], limit)
            return t

        ada_first = at("ada_first", [P, KT, 2 * D], F32, R0)
        sp_hi = at("sp_hi", [P, KT, D], F32R, R0)
        sp_lo = at("sp_lo", [P, KT, D], F32R, R0 + 32 * KB)
        xv = at("xv", [P, NT, D], F32, R0 + 64 * KB)
        raw_gu = at("raw_gu", [P, 2, 2, KT, F], F32, R0)
        raw_d = at("raw_d", [P, 2, FT, D], F32, R0 + 64 * KB)
        wi_hi = at("wi_hi", [P, KT, 2 * CQ], F32R, R1)
        wi_lo = at("wi_lo", [P, KT, 2 * CQ], F32R, R1 + 16 * KB)
        x1 = at("x1", [P, NT, D], F32, R1)
        off = [R2]

        def seq(name, shape, dt):
            n = 4
            for d in shape[1:]:
                n *= d
            t = at(name, shape, dt, off[0])
            off[0] += (n + 31) // 32 * 32
            return t

        stage = seq("stage", [P, 2, 4096 // 2], F32)
        mx = seq("mx", [P, MSLOTS, ND, 2, P], F32R)
        u = seq("u", [P, QG, NT * GC], F32)
        ut_hi = seq("ut_hi", [P, 2, BG, P + 2 * PAD], F32R)
        ut_lo = seq("ut_lo", [P, 2, BG, P + 2 * PAD], F32R)
        taps_raw = seq("taps_raw", [P, QG, NM], F32)
        taps_hi = seq("taps_hi", [P, QG, NM], F32R)
        taps_lo = seq("taps_lo", [P, QG, NM], F32R)
        bin_row = seq("bin_row", [P, 2 * CQ], F32)
        bdw_row = seq("bdw_row", [P, CQ], F32)
        acc = seq("acc", [P, D], F32)
        ada_stage = seq("ada_stage", [P, 2, D], F32)
        pre = seq("pre", [P, 2, 2 * CQ], F32)
        junk = seq("junk", [P, D], F32)
        assert off[0] <= top[0]
        mod_row = at("mod_row", [P, 3, D], F32, R2 + 16 * KB)
        acc01 = at("acc01", [P, 2, D], F32, R2 + 36 * KB)
        off = [R2 + 16 * KB]
        s_full = seq("s_full", [P, KT, P], F32)
        s_hi = seq("s_hi", [P, 2, KT, P], F32R)
        s_lo = seq("s_lo", [P, 2, KT, P], F32R)
        zb = seq("zb", [P, D], F32)
        yb_at = off[0]
        yb = seq("yb", [P, 2, D], F32)
        xr = seq("xr", [P, 2, D], F32)
        h2_at = off[0]
        h2 = seq("h2", [P, 2, D], F32)
        bout_row = seq("bout_row", [P, D], F32)
        rows = seq("rows", [P, 3, D], F32)
        diag = [at("diag0", [P, P, KT], F32, yb_at + 4 * KB), at("diag1", [P, P, KT], F32, h2_at + 4 * KB)]
        junk2 = at("junk2", [P, D], F32, R2 + 12 * KB)
        h2t = at("h2t", [P, KT, P], F32, R2 + 8 * KB)
        assert off[0] <= top[0], (off[0], top[0])

        ident = small("ident", [P, P])
        col = small("col", [P, 8, KT])
        bada = small("bada", [P, 6, KT])
        modc = small("modc", [P, 4, KT])
        silc = small("silc", [P, 2, KT])
        eye16 = small("eye16", [P, GC])
        ones = small("ones", [P, P])
        nhalf = small("nhalf", [P, 8])
        epsc = small("epsc", [P, 1])
        gap = small("gap", [P, 1])
        zero_i = small("zero_i", [P, 1], I32)
        gap_p = small("gap_p", [P, 1])
        ssx = small("ssx", [P, NT])
        rsx = small("rsx", [P, NT])
        tmp8 = small("tmp8", [P, NT])
        stats = small("stats", [P, NT, 2, 6])
        mv = small("mv", [P, NT, 2])
        lnr = small("lnr", [P, 2, NT])
        sy = small("sy", [P, 2, 3])
        sx = small("sx", [P, 2, 3])
        vcol = small("vcol", [P, 3, KT])
        rwt = small("rwt", [P, KT, NE])
        rb_row = small("rb_row", [P, NE])
        logits = small("logits", [P, NT, NE])

        gates = small("gates", [P, 2, NT])
        words = small("words", [P, NSTC], I32)
        counts = small("counts", [P, 2], I32)
        ct_i = small("ct_i", [P, NE], I32)
        dest = small("dest", [P, 2 * NSTC], I32)
        src = small("src", [P, 2 * NSTC + 2], I32)
        ic = small("ic", [P, 4], I32)

        off = [R2 + 80 * KB]
        tri = seq("tri", [P, P], F32)
        iota = seq("iota", [P, P], F32)
        le16 = seq("le16", [P, NE, NE], F32)
        lt4 = seq("lt4", [P, EG, EG], F32)
        desc4 = seq("desc4", [P, NG], F32)
        tok1 = seq("tok1", [P, 2 * NT], F32)
        assert off[0] <= R2 + 84736
        off = [R2 + 40 * KB]
        aff = seq("aff", [P, NT, NE], F32)
        sel = seq("sel", [P, NT, NE], F32)
        pair_max = seq("pair_max", [P, NT * NG, 2], F32)
        pair_min = seq("pair_min", [P, NT * NG, 2], F32)
        gs = seq("gs", [P, 6, NT, NG], F32)
        gmax = seq("gmax", [P, 2, NT], F32)
        beats = seq("beats", [P, 2, NT * NG, EG, EG], F32)
        rank = seq("rank", [P, NT, NE], F32)
        mk = seq("mk", [P, 2, NT, NE], F32)
        m9 = seq("m9", [P, NT + 1, NE], F32)
        prod = seq("prod", [P, 2 * NT, NE], F32)
        ak = seq("ak", [P, 2, NT], F32)
        den = seq("den", [P, 2, NT], F32)
        pos = seq("pos", [P, NT, NE], F32)
        cnt = seq("cnt", [P, 6, NE], F32)
        prod16 = seq("prod16", [P, NE, NE], F32)
        slot = seq("slot", [P, 2 * NT], F32)
        slot_i = seq("slot_i", [P, 3, 2 * NT], I32)
        slot_f = seq("slot_f", [P, 2, 2 * NT], F32)
        st_le = seq("st_le", [P, NSTC, NE], F32)
        st_in = seq("st_in", [P, NSTC, NE], F32)
        st_ab = seq("st_ab", [P, NSTC, NE], F32)
        start = seq("start", [P, 2, NSTC], F32)
        e_of = seq("e_of", [P, NSTC + 2], F32)
        hb_of = seq("hb_of", [P, 2, 16 + NSTC + 1], F32)
        word_f = seq("word_f", [P, 2, NSTC], F32)
        oh_p = seq("oh_p", [P, 2 * NT, P], F32)
        oh_t = seq("oh_t", [P, 2 * NT, 2 * NSTC], F32)
        assert off[0] <= R2 + 76 * KB, off[0] - R2

        off = [R2]
        pr_hi = seq("pr_hi", [P, RING, D], F32R)
        pr_lo = seq("pr_lo", [P, RING, D], F32R)
        xg = seq("xg", [P, 2, D], F32)
        xt_hi = seq("xt_hi", [P, 2, KT, P], F32R)
        xt_lo = seq("xt_lo", [P, 2, KT, P], F32R)
        he = seq("he", [P, 2, F], F32)
        het_hi = seq("het_hi", [P, 2, FT, P], F32R)
        het_lo = seq("het_lo", [P, 2, FT, P], F32R)
        ys = seq("ys", [P, 2, D], F32)
        assert off[0] <= R2 + 80 * KB
        y_all = at("y_all", [P, 2, NT, D], F32, R0)
        g3 = at("g3", [P, D], F32, R0 + 64 * KB)
        fb = at("fb", [P, FB, D], F32, R0 + 68 * KB)
        junk3 = at("junk3", [P, D], F32, R0 + (68 + 4 * FB) * KB)
        sf = small("sf", [P, 3, NT])

        h2_rows = nc.dram_tensor("h2_rows", [S, D], F32).ap()
        y_rows = nc.dram_tensor("y_rows", [2 * S, D], F32).ap()
        first_rows = nc.dram_tensor("first_rows", [2, P], F32).ap()
        g3_rows = nc.dram_tensor("g3_rows", [P, D], F32).ap()

        ps = ctx.enter_context(nc.psum_tensor("ps", [P, 8, 512], F32))

        cols_loaded = sem("cols_loaded")
        x_loaded = [sem(f"x_loaded{j}") for j in range(4)]
        ada1_loaded = [sem(f"ada1_loaded{j}") for j in range(4)]
        stage_loaded = [sem(f"stage_loaded{j}") for j in range(2)]
        taps_loaded = sem("taps_loaded")
        brow_loaded = sem("brow_loaded")
        bdw_loaded = sem("bdw_loaded")
        ada_loaded = [sem(f"ada_loaded{j}") for j in range(2)]
        const_made = sem("const_made")
        eye_made = sem("eye_made")
        sigc_done = sem("sigc_done")
        silc_done = sem("silc_done")
        ssx_done = sem("ssx_done")
        pool_chain = sem("pool_chain")
        rsx_done = sem("rsx_done")
        xn_done = sem("xn_done")
        brow1_loaded = sem("brow1_loaded")
        acc1_done = sem("acc1_done")
        ada1_mod = sem("ada1_mod")
        mod1_done = sem("mod1_done")
        xt_done = sem("xt_done")
        hs_done = sem("hs_done")
        hhi_done = sem("hhi_done")
        hlo_done = sem("hlo_done")
        wi_hi_done = sem("wi_hi_done")
        wi_lo_done = sem("wi_lo_done")
        wi_used = sem("wi_used")
        win_tile = sem("win_tile")
        pre_done = sem("pre_done")
        sig_done = sem("sig_done")
        u_done = sem("u_done")
        acc_done = sem("acc_done")
        acc_col = sem("acc_col")
        modc_done = sem("modc_done")
        taps_split = sem("taps_split")
        mhi_done = sem("mhi_done")
        mlo_done = sem("mlo_done")
        ut_tr = sem("ut_tr")
        uthi_done = sem("uthi_done")
        utlo_done = sem("utlo_done")
        conv_done = sem("conv_done")
        vb_done = sem("vb_done")
        v_done = sem("v_done")
        wo_hi_done = sem("wo_hi_done")
        wo_lo_done = sem("wo_lo_done")
        xr_loaded = [sem(f"xr_loaded{j}") for j in range(2)]
        bout_loaded = sem("bout_loaded")
        rw_loaded = sem("rw_loaded")
        vcol_done = sem("vcol_done")
        diag_done = sem("diag_done")
        brow_tr = sem("brow_tr")
        rows_done = sem("rows_done")
        g3_stored = sem("g3_stored")
        stats_done = sem("stats_done")
        mv_done = sem("mv_done")
        lnr_done = sem("lnr_done")
        lnv_done = sem("lnv_done")
        sym_done = sem("sym_done")
        sxm_done = sem("sxm_done")
        z_done = sem("z_done")
        zt_done = sem("zt_done")
        s_done = sem("s_done")
        sh_done = sem("sh_done")
        sl_done = sem("sl_done")
        yh_done = sem("yh_done")
        yb_done = sem("yb_done")
        sqy_done = sem("sqy_done")
        ry_done = sem("ry_done")
        t_done = sem("t_done")
        x1_done = sem("x1_done")
        sqx_done = sem("sqx_done")
        rx_done = sem("rx_done")
        hg_done = sem("hg_done")
        h2_done = sem("h2_done")
        h2_stored = [sem(f"h2_stored{j}") for j in range(2)]
        h2_tr = sem("h2_tr")
        h2t_done = sem("h2t_done")
        rt_done = sem("rt_done")
        log_done = sem("log_done")

        rconst = sem("rconst")
        aff_done = sem("aff_done")
        route_chain = sem("route_chain")
        pos_done = sem("pos_done")
        slots_done = sem("slots_done")
        tables = sem("tables")
        raw_loaded = [[sem(f"raw_loaded{b}{j}") for j in range(CHUNKS)] for b in range(2)]
        ic_done = [sem(f"ic_done{j}") for j in range(4)]
        gath = [sem(f"gath{j}") for j in range(2)]
        scat = [sem(f"scat{j}") for j in range(2)]
        all_scattered = sem("all_scattered")
        xt_tr = sem("xt_tr")
        xth_done = sem("xth_done")
        xtl_done = sem("xtl_done")
        pr_hi_done = sem("pr_hi_done")
        pr_lo_dve = sem("pr_lo_dve")
        pr_lo_pool = sem("pr_lo_pool")
        pr_used = sem("pr_used")
        sil_done = sem("sil_done")
        he_done = sem("he_done")
        he_tr = sem("he_tr")
        heth_done = sem("heth_done")
        hetl_done = sem("hetl_done")
        d0_done = sem("d0_done")
        d1_done = sem("d1_done")
        y0_done = sem("y0_done")
        y1_done = sem("y1_done")
        yl = [sem(f"yl{j}") for j in range(4)]
        g3_loaded = sem("g3_loaded")
        fa_done = sem("fa_done")
        f_done = sem("f_done")
        sqf_done = sem("sqf_done")
        sfm_done = sem("sfm_done")
        rf_done = sem("rf_done")
        fg_done = sem("fg_done")
        o_done = sem("o_done")
        stored = sem("stored")

        block = ctx.enter_context(nc.Block())

        class Step:
            def __init__(self, eng, s):
                w = eng.value_load(words[0:1, bass.ds(s, 1)], min_val=0, max_val=(1 << 23) - 1)
                self.s = s
                self.ep, self.e, self.en = w & 31, (w >> 5) & 31, (w >> 10) & 31
                self.hp, self.h, self.hn = (w >> 15) & 1, (w >> 16) & 1, (w >> 17) & 1
                self.nbp = w >> 18
                self.nb = self.nbp + self.hp
                self.nbn = self.nb + self.h
                self.c = self.nb + s
                self.cn = self.c + self.h + 1
                if not (type(s) is int and s == 0):
                    self.cp = self.nbp + (s - 1)

        marks = {}
        WI = (0, 1, 2)
        UT = (3, 4)
        CV = (5, 6)
        MODB = 7
        DN, TR = 4, 6
        PZ, PY, PH, PR = 0, 2, 4, 6

        x_t = x.rearrange("b (a i) d -> (b a) i d", i=NT)
        w_ada_t = w_ada.rearrange("l (p k) n -> (l p) k n", k=KT)
        w_out_t = w_out.rearrange("l (p k) n -> (l p) k n", k=KT)

        @block.sync
        def _(sp):
            cols = ((c.rearrange("b n -> (b n)"), 0), (g_mix_pre.rearrange("b n -> (b n)"), 1),
                    (g_mix_post.rearrange("b n -> (b n)"), 2), (g_ffn_pre.rearrange("b n -> (b n)"), 3),
                    (g_ffn_post.rearrange("b n -> (b n)"), 4), (ln_g.rearrange("b n -> (b n)"), 5),
                    (ln_b.rearrange("b n -> (b n)"), 6))
            for src, j in cols:
                sp.dma_start(col[:, j, :], src.rearrange("(p k) -> p k", k=KT)).then_inc(cols_loaded, 16)
            sp.dma_start(bada[:, :, :], b_ada.rearrange("l (s p k) -> (l p) s k", s=6, k=KT)).then_inc(cols_loaded, 16)

            def load_x(j):
                sp.dma_start(xv[:, 2 * j:2 * j + 2, :], x_t[:, 2 * j:2 * j + 2, :]).then_inc(x_loaded[j], 16)

            def load_win(q, h):
                sp.dma_start(stage[:, h, :],
                             w_in[bass.ds(q, 1), :, 2048 * h:2048 * h + 2048].rearrange("q p n -> (q p) n")
                             ).then_inc(stage_loaded[h], 16)

            def load_taps(q):
                for i in range(NT):
                    sp.dma_start(taps_raw[GC * i:GC * i + GC, :, i + 1:i + 1 + TAPS],
                                 w_dw[bass.ds(q, 1)].rearrange("q c g t -> (q c) g t")).then_inc(taps_loaded, 16)

            load_x(0)
            for j in range(4):
                sp.dma_start(ada_first[:, 2 * j:2 * j + 2, :],
                             w_ada_t[:, 2 * j:2 * j + 2, 0:2 * D]).then_inc(ada1_loaded[j], 16)
                if j < 3:
                    load_x(j + 1)
                if j == 1:
                    sp.dma_start(mod_row[:, 0:2, :].rearrange("p s d -> p (s d)"),
                                 b_ada[0:1, 0:2 * D].partition_broadcast(P)).then_inc(brow1_loaded, 16)
                    sp.dma_start(mod_row[:, 2, :], g_mix_pre[0:1, :].partition_broadcast(P)).then_inc(brow1_loaded, 16)
            load_win(0, 0)
            load_win(0, 1)
            sp.dma_start(rwt[:, :, :], router_w.rearrange("(p k) e -> p k e", k=KT)).then_inc(rw_loaded, 16)
            sp.dma_start(rb_row[:, :], router_b.rearrange("(b n) -> b n", b=1).partition_broadcast(P)).then_inc(rw_loaded, 16)
            sp.wait_ge(const_made, 6)
            load_taps(0)

            def quarter(q, last):
                for h in range(2):
                    sp.wait_ge(wi_lo_done, 4 * q + 2 * h + 2)
                    if last:
                        sp.dma_start(stage[:, h, :].rearrange("p (k n) -> p k n", k=2), w_out_t[:, 2 * h:2 * h + 2, :]).then_inc(stage_loaded[h], 16)
                    else:
                        load_win(q + 1, h)
                for k in range(KT):
                    if k >= 2:
                        sp.wait_ge(acc_done, ONE + 8 * q + k - 1)
                    else:
                        sp.wait_ge(acc_done, ONE + 8 * q)
                    sp.dma_start(ada_stage[:, k % 2, :],
                                 w_ada_t[:, k, bass.ds((q + 2) * D, D)]).then_inc(ada_loaded[k % 2], 16)
                if not last:
                    sp.wait_ge(taps_split, 2 * q + 2)
                    load_taps(q + 1)

            with sp.Fori(0, NQ - 1) as q:
                quarter(q, False)
            quarter(NQ - 1, True)
            for h in range(2):
                sp.wait_ge(wo_lo_done, 2 * h + 2)
                sp.dma_start(stage[:, h, :].rearrange("p (k n) -> p k n", k=2),
                             w_out_t[:, 4 + 2 * h:6 + 2 * h, :]).then_inc(stage_loaded[h], 16)
            sp.wait_ge(v_done, ONE + NQ * QH)
            sp.dma_start(bout_row[:, :], b_out[0:1, :].partition_broadcast(P)).then_inc(bout_loaded, 16)

            h2_out = h2_rows.rearrange("(a i) d -> a i d", i=NT)

            def load_xr(i, b, first):
                if not first:
                    sp.wait_ge(x1_done, i - 1)
                sp.dma_start(xr[:, b, :], x_t[:, bass.ds(i, 1), :]).then_inc(xr_loaded[b], 16)

            def store_h2(i, b):
                sp.wait_ge(h2_done, i + 1)
                sp.dma_start(h2_out[:, bass.ds(i, 1), :], h2[:, b, :]).then_inc(h2_stored[b], 16)

            load_xr(0, 0, True)
            load_xr(1, 1, True)
            sp.wait_ge(rows_done, 4)
            sp.dma_start(g3_rows, h2[:, 0, :]).then_inc(g3_stored, 16)
            with sp.Fori(0, NT // 2 - 1) as t:
                for b in range(2):
                    load_xr(2 * t + 2 + b, b, False)
                    store_h2(2 * t + b, b)
            store_h2(NT - 2, 0)
            store_h2(NT - 1, 1)
            sp.wait_ge(yh_done, 2 * NT)
            sp.wait_ge(z_done, NT)

            def load_expert(t, b, ct):
                one = bass.ds(2 * t + b, 1)
                for j in range(CHUNKS):
                    if ct is not None and j == 0:
                        sp.wait_ge(pr_used, 12 * ct + 8)
                    if ct is not None and j == 4:
                        sp.wait_ge(pr_used, 12 * ct + 24)
                    if j in (2, 3, 5):
                        sp.wait_ge(raw_loaded[b][j - 2], ONE_DMA * b + 16 * t + 16)
                    elif j == 1 and b == 1:
                        sp.wait_ge(raw_loaded[0][5], 16 * t + 16)
                    elif j == 1 and ct is not None:
                        sp.wait_ge(raw_loaded[1][5], ONE_DMA + 16 * t)
                    if j < 4:
                        src_w = (w_gate, w_up)[j % 2]
                        ks = slice(4 * (j // 2), 4 * (j // 2) + 4)
                        sp.dma_start(raw_gu[:, b, j % 2, ks, :],
                                     src_w[0, one].rearrange("e (p k) n -> (e p) k n", k=KT)[:, ks, :]
                                     ).then_inc(raw_loaded[b][j], 16)
                    else:
                        ks = slice(2 * (j - 4), 2 * (j - 4) + 2)
                        sp.dma_start(raw_d[:, b, ks, :],
                                     w_down[0, one].rearrange("e (p k) n -> (e p) k n", k=FT)[:, ks, :]
                                     ).then_inc(raw_loaded[b][j], 16)

            load_expert(0, 0, None)
            load_expert(0, 1, None)
            sp.wait_ge(tables, 1)
            with sp.Fori(1, NE // 2) as t:
                for b in range(2):
                    load_expert(t, b, sp.value_load(ct_i[0:1, bass.ds(2 * t - 2 + b, 1)], min_val=0, max_val=NST - 1))

            last_st = sp.value_load(counts[0:1, 0:1], min_val=0, max_val=NST - 1)
            st = last_st + 1
            sp.wait_ge(pr_used, 12 * st + 4)
            sp.dma_start(g3[:, :], g3_rows).then_inc(g3_loaded, 16)
            sp.wait_ge(all_scattered, 1)
            y_in = y_rows.rearrange("(k a i) d -> a k i d", k=2, i=NT)
            for j in range(4):
                for k in range(2):
                    sp.dma_start(y_all[:, k, 2 * j:2 * j + 2, :], y_in[:, k, 2 * j:2 * j + 2, :]).then_inc(yl[j], 16)
            out_t = out.rearrange("b (a i) d -> (b a) i d", i=NT)
            for i in range(NT):
                sp.wait_ge(o_done, i + 1)
                sp.dma_start(out_t[:, i, :], x1[:, i, :]).then_inc(stored, 16)
            sp.wait_ge(h2_stored[0], ONE_DMA + 16 * (NT // 2))
            sp.wait_ge(h2_stored[1], ONE_DMA + 16 * (NT // 2))
            sp.wait_ge(stored, 16 * NT)

        @block.gpsimd
        def _(pool):
            for s_ in (acc_col, acc_done, conv_done, h2_tr, h2t_done, he_done, log_done, mlo_done, modc_done, rt_done, u_done, ut_tr, v_done, y0_done, y1_done):
                pool.sem_inc(s_, ONE)
            for s_ in h2_stored + raw_loaded[1]:
                pool.sem_inc(s_, ONE_DMA)
            pool.memset(ident[:, :], 0.0).then_inc(pool_chain, 1)
            pool.memset(eye16[:, :], 0.0).then_inc(pool_chain, 1)
            pool.memset(epsc[:, :], EPS).then_inc(pool_chain, 1)
            pool.memset(zero_i[:, :], 0).then_inc(pool_chain, 1)
            pool.memset(ones[:, :], 1.0).then_inc(const_made, 1)
            pool.memset(nhalf[:, :], -0.5).then_inc(const_made, 1)
            pool.memset(taps_raw[:, :, :], 0.0).then_inc(const_made, 1)
            pool.memset(ut_hi[:, :, :, :].bitcast(F32), 0.0).then_inc(const_made, 1)
            pool.memset(ut_lo[:, :, :, :].bitcast(F32), 0.0).then_inc(const_made, 1)
            pool.wait_ge(pool_chain, 4)
            pool.affine_select(out=ident[:, :], in_=ident[:, :], compare_op=ALU.not_equal, fill=1.0, base=0,
                               pattern=[[-1, P]], channel_multiplier=1).then_inc(const_made, 1)
            pool.wait_ge(const_made, 6)
            for b in range(2):
                pool.dma_start(first_rows[b:b + 1, :], ones[0:1, :]).then_inc(scat[b], 16)
            for i in range(NT):
                pool.affine_select(out=eye16[:, :], in_=eye16[:, :], compare_op=ALU.not_equal, fill=1.0,
                                   base=-GC * i, pattern=[[-1, GC]], channel_multiplier=1).then_inc(eye_made, 1)
                pool.wait_ge(eye_made, i + 1)
            pool.dma_start(bin_row[:, :], b_in[0:1, :].partition_broadcast(P)).then_inc(brow_loaded, 16)
            pool.dma_start(bdw_row[:, :], b_dw[0:1, 0:CQ].partition_broadcast(P)).then_inc(bdw_loaded, 16)
            pool.wait_ge(const_made, 6)

            def inv_rms(j):
                two = slice(2 * j, 2 * j + 2)
                pool.wait_ge(ssx_done, 2 * j + 2)
                pool.tensor_scalar(tmp8[:, two], ssx[:, two], 1.0 / D, EPS, ALU.mult, ALU.add).then_inc(pool_chain, 1)
                pool.wait_ge(pool_chain, 5 + j)
                pool.tensor_tensor(rsx[:, two], tmp8[:, two], nhalf[:, 0:2], ALU.pow).then_inc(rsx_done, 1)

            for i in range(NT):
                if i < 4:
                    inv_rms(i)
                pool.wait_ge(xn_done, i + 1)
                pool.wait_ge(mod1_done, 3)
                pool.tensor_tensor(xv[:, i, :], xv[:, i, :], mod_row[:, 0, :], ALU.add).then_inc(hs_done, 1)
            pool.wait_ge(hlo_done, NT)

            def make_m(q, g):
                if g < MSLOTS:
                    pool.wait_ge(conv_done, ONE + QG * q)
                else:
                    pool.wait_ge(conv_done, ONE + QG * q + g - MSLOTS + 1)
                pool.tensor_tensor(mx[:, g % MSLOTS, :, 0, :].rearrange("p d (i c) -> p d i c", i=NT),
                                   taps_hi[:, g, :].bitcast(F32).rearrange("p (d i) -> p d i", d=ND).unsqueeze(3)
                                   .to_broadcast([P, ND, NT, GC]),
                                   eye16[:, :].unsqueeze(1).unsqueeze(1).to_broadcast([P, ND, NT, GC]),
                                   ALU.mult).then_inc(mhi_done, 1)

            def quarter(q, last):
                pool.wait_ge(taps_loaded, 128 * q + 128)
                pool.wait_ge(mlo_done, ONE + QG * q)
                pool.tensor_tensor(taps_hi[:, :, :], taps_raw[:, :, :], ones[:, 0:1].unsqueeze(1).to_broadcast([P, QG, NM]),
                                   ALU.mult).then_inc(taps_split, 1)
                pool.wait_ge(taps_split, 2 * q + 1)
                pool.tensor_tensor(taps_lo[:, :, :], taps_raw[:, :, :], taps_hi[:, :, :].bitcast(F32),
                                   ALU.subtract).then_inc(taps_split, 1)
                for g in range(QG):
                    make_m(q, g)
                    if g == 8 and not last:
                        pool.wait_ge(pre_done, 8 * q + 8)
                        pool.dma_start(bin_row[:, :],
                                       b_in[bass.ds(q + 1, 1), :].partition_broadcast(P)).then_inc(brow_loaded, 16)
                if not last:
                    pool.wait_ge(v_done, ONE + QH * q + QH)
                    pool.dma_start(bdw_row[:, :],
                                   b_dw[0:1, bass.ds((q + 1) * CQ, CQ)].partition_broadcast(P)).then_inc(bdw_loaded, 16)

            with pool.Fori(0, NQ - 1) as q:
                quarter(q, False)
            quarter(NQ - 1, True)

            for j, ts_ in enumerate((slice(0, 2), slice(2, NT))):
                pool.wait_ge(mv_done, (2, NT)[j])
                pool.tensor_tensor(lnr[:, 0, ts_], mv[:, ts_, 1], epsc[:, :].to_broadcast([P, ts_.stop - ts_.start]),
                                   ALU.add).then_inc(lnv_done, 1)
                pool.wait_ge(lnv_done, j + 1)
                pool.tensor_tensor(lnr[:, 1, ts_], lnr[:, 0, ts_], nhalf[:, 0:ts_.stop - ts_.start],
                                   ALU.pow).then_inc(lnr_done, 1)

            def factor(i, b, s3, summed, mid, done):
                pool.wait_ge(summed, i + 1)
                pool.tensor_tensor(s3[:, b, 1:2], s3[:, b, 0:1], epsc[:, :], ALU.add).then_inc(mid, 1)
                pool.wait_ge(mid, i + 1)
                pool.tensor_tensor(s3[:, b, 2:3], s3[:, b, 1:2], nhalf[:, 0:1], ALU.pow).then_inc(done, 1)

            def step(i, b, last):
                factor(i, b, sy, sqy_done, sym_done, ry_done)
                factor(i, b, sx, sqx_done, sxm_done, rx_done)
                pool.wait_ge(hg_done, i + 1)
                pool.tensor_tensor(h2[:, b, :], h2[:, b, :], rows[:, 2, :], ALU.add).then_inc(h2_done, 1)

            pool.wait_ge(rows_done, 4)
            step(0, 0, False)
            with pool.Fori(0, NT // 2 - 1) as t:
                step(2 * t + 1, 1, False)
                step(2 * t + 2, 0, False)
            step(NT - 1, 1, True)
            pool.wait_ge(v_done, ONE + NQ * QH)
            pool.memset(tri[:, :], 1.0).then_inc(pool_chain, 1)
            pool.memset(le16[:, :, :], 1.0).then_inc(pool_chain, 1)
            pool.memset(lt4[:, :, :], 1.0).then_inc(pool_chain, 1)
            for j in range(NG):
                pool.memset(desc4[:, j:j + 1], float(NG - j)).then_inc(rconst, 1)
            pool.wait_ge(pool_chain, 4 + NT // 2 + 3)
            pool.affine_select(out=tri[:, :], in_=tri[:, :], compare_op=ALU.is_ge, fill=0.0, base=-1,
                               pattern=[[1, P]], channel_multiplier=-1).then_inc(rconst, 1)
            pool.affine_select(out=le16[:, :, :], in_=le16[:, :, :], compare_op=ALU.is_ge, fill=0.0, base=0,
                               pattern=[[1, NE], [-1, NE]], channel_multiplier=0).then_inc(rconst, 1)
            pool.affine_select(out=lt4[:, :, :], in_=lt4[:, :, :], compare_op=ALU.is_ge, fill=0.0, base=-1,
                               pattern=[[1, EG], [-1, EG]], channel_multiplier=0).then_inc(rconst, 1)
            pool.iota(iota[:, :], pattern=[[1, P]], base=0, channel_multiplier=0,
                      allow_small_or_imprecise_dtypes=True).then_inc(rconst, 1)
            pool.iota(tok1[:, :], pattern=[[S, 2], [1, NT]], base=1, channel_multiplier=NT,
                      allow_small_or_imprecise_dtypes=True).then_inc(rconst, 1)

            pool.wait_ge(tables, 1)
            last_st = pool.value_load(counts[0:1, 0:1], min_val=0, max_val=NST - 1)
            st = last_st + 1

            def low(idx, q, e, k, down):
                pool.wait_ge(pr_hi_done, idx + 1)
                if down:
                    pool.tensor_tensor(pr_lo[:, 3, :], raw_d[:, bass.ds(q, 1), k, :].rearrange("p o n -> p (o n)"),
                                       pr_hi[:, 3, :].bitcast(F32), ALU.subtract).then_inc(pr_lo_pool, 1)
                    return None
                return pool.tensor_tensor(pr_lo[:, 3, :].rearrange("p (g n) -> p g n", g=2),
                                          raw_gu[:, bass.ds(q, 1), :, k, :].rearrange("p o g n -> p (o g) n"),
                                          pr_hi[:, 3, :].bitcast(F32).rearrange("p (g n) -> p g n", g=2), ALU.subtract)

            def settle():
                pool.tensor_tensor(gap_p[:, :], epsc[:, :], epsc[:, :], ALU.add)

            def gather(s, b, turned, n):
                if turned is not None:
                    pool.wait_ge(xt_tr, turned)
                pool.tensor_tensor(ic[:, b:b + 1], src[:, bass.ds(2 * s + b, 1)], zero_i[:, :], ALU.add).then_inc(ic_done[b], 1)
                pool.wait_ge(ic_done[b], n)
                settle()
                pool.indirect_dma_start(xg[:, b, :], None, h2_rows,
                                        bass.IndirectOffsetOnAxis(ap=ic[:, b:b + 1].bitcast(U32), axis=0)).then_inc(gath[b], 16)

            def scatter(b, slot, tiles, before, n):
                pool.wait_ge(y0_done, ONE + tiles)
                pool.wait_ge(y1_done, ONE + tiles)
                pool.wait_ge(scat[b], ONE_DMA + 16 * before)
                col_ = dest[:, bass.ds(slot, 1)]
                pool.tensor_tensor(ic[:, 2 + b:3 + b], col_, zero_i[:, :], ALU.add).then_inc(ic_done[2 + b], 1)
                pool.wait_ge(ic_done[2 + b], n)
                settle()
                pool.indirect_dma_start(y_rows, bass.IndirectOffsetOnAxis(ap=ic[:, 2 + b:3 + b].bitcast(U32), axis=0),
                                        ys[:, b, :], None, bounds_check=2 * S - 1, oob_is_err=False
                                        ).then_inc(scat[b], 16)

            def scatter_both(w_s, hb, nb, tiles):
                before = w_s + 0
                n = w_s + 1
                scatter(0, 2 * w_s, tiles + 1, before, n)
                with pool.If(hb > 0):
                    n = nb + 1
                    scatter(1, 2 * w_s + 1, tiles + 2, nb, n)

            w = Step(pool, 0)
            gather(0, 0, None, 1)
            with pool.If(w.h > 0):
                gather(0, 1, None, 1)
            low(3, 0, 0, 3, False).then_inc(pr_lo_pool, 1)
            gather(1, 0, 1, 2)
            with pool.If(w.hn > 0):
                gather(1, 1, w.cn, w.h + 1)
            low(7, 0, 0, 7, False).then_inc(pr_lo_pool, 2)
            after = Step(pool, 1)
            gather(2, 0, w.cn + 1, 3)
            low(15, w.en & 1, 0, 3, False).then_inc(pr_lo_pool, 1)
            with pool.If(after.hn > 0):
                gather(2, 1, w.cn + 1 + w.hn, w.h + w.hn + 1)
            low(19, w.en & 1, 0, 7, False).then_inc(pr_lo_pool, 1)
            with pool.Fori(1, NST) as s:
                with pool.If(s < st):
                    w = Step(pool, s)
                    low(12 * s + 11, w.ep & 1, 0, 3, True)
                    with pool.If(s + 2 < st):
                        gather(s + 2, 0, w.cn + 1, s + 3)
                        pool.wait_ge(tables, 1)
                    with pool.Else():
                        pool.wait_ge(tables, 1)
                    with pool.If(s + 1 < st):
                        low(12 * s + 15, w.en & 1, 0, 3, False).then_inc(pr_lo_pool, 1)
                    with pool.Else():
                        pool.wait_ge(tables, 1)
                    w2 = pool.value_load(words[0:1, bass.ds(s + 1, 1)], min_val=0, max_val=(1 << 23) - 1)
                    with pool.If(((w2 >> 17) & 1) > 0):
                        gather(s + 2, 1, w.cn + 1 + w.hn, w.nbn + w.hn + 1)
                    scatter_both(s - 1, w.hp, w.nbp, w.cp)
                    with pool.If(s + 1 < st):
                        low(12 * s + 19, w.en & 1, 0, 7, False).then_inc(pr_lo_pool, 1)
                    with pool.Else():
                        pool.wait_ge(tables, 1)
                    pool.wait_ge(tables, 1)
                pool.wait_ge(tables, 1)
            w = Step(pool, last_st)
            low(12 * st + 3, (NE - 1) % 2, 0, 3, True)
            scatter_both(last_st, w.h, w.nb, w.c)
            pool.wait_ge(scat[0], ONE_DMA + 16 * st)
            pool.wait_ge(scat[1], ONE_DMA + 16 * w.nbn)
            pool.tensor_tensor(tmp8[:, 0:1], epsc[:, :], epsc[:, :], ALU.add).then_inc(all_scattered, 1)
            def residual(i):
                pool.wait_ge(fg_done, i + 1)
                pool.tensor_tensor(x1[:, i, :], x1[:, i, :], fb[:, i % FB, :], ALU.add).then_inc(o_done, 1)

            for i in range(NT):
                pool.wait_ge(sqf_done, i + 1)
                pool.tensor_tensor(sf[:, 1, i:i + 1], sf[:, 0, i:i + 1], epsc[:, :], ALU.add).then_inc(sfm_done, 1)
                pool.wait_ge(sfm_done, i + 1)
                pool.tensor_tensor(sf[:, 2, i:i + 1], sf[:, 1, i:i + 1], nhalf[:, 0:1], ALU.pow).then_inc(rf_done, 1)
                if i >= 1:
                    residual(i - 1)
            residual(NT - 1)

        @block.scalar
        def _(act):
            act.wait_ge(cols_loaded, 16 * 8)
            act.activation(silc[:, 0, :], col[:, 0, :], ACT.Sigmoid).then_inc(sigc_done, 1)

            def square_sum(i):
                act.wait_ge(x_loaded[i // 2], 16)
                if i > 0:
                    act.wait_ge(ssx_done, i)
                act.activation(junk[:, :], xv[:, i, :], ACT.Square, accum_out=ssx[:, i:i + 1]).then_inc(ssx_done, 1)

            for i in range(NT):
                square_sum(i)

            def split_hi(q, k, first):
                act.wait_ge(stage_loaded[k // 2], 16 * (q + 1))
                if not first:
                    if k < 3:
                        act.wait_ge(wi_used, 3 * q + k - 2)
                    else:
                        act.wait_ge(win_tile, NT * q)
                act.activation(wi_hi[:, 2 * k:2 * k + 2, :],
                               stage[:, k // 2, 1024 * (k % 2):1024 * (k % 2) + 1024].rearrange("p (k n) -> p k n", k=2),
                               ACT.Copy).then_inc(wi_hi_done, 1)

            def split_wout(k):
                act.wait_ge(stage_loaded[(k // 2) % 2], 16 * (NQ + 1 + k // 4))
                act.wait_ge(win_tile, NQ * NT)
                act.activation(sp_hi[:, k, :], stage[:, (k // 2) % 2, 1024 * (k % 2):1024 * (k % 2) + 1024],
                               ACT.Copy).then_inc(wo_hi_done, 1)

            for i in range(NT):
                act.wait_ge(xt_done, i + 1)
                b0 = UT[0] if i % 2 == 0 else CV[0]
                act.activation(sp_hi[:, :, P * i:P * i + P], ps[:, b0:b0 + 2, :].rearrange("p b (k a) -> p (b k) a", a=P),
                               ACT.Copy).then_inc(hhi_done, 1)
                if i < 2:
                    split_hi(0, 2 * i, True)
                    split_hi(0, 2 * i + 1, True)

            def ut(q, b):
                act.wait_ge(ut_tr, ONE + QB * q + b + 1)
                if b < 2:
                    act.wait_ge(conv_done, ONE + QG * q)
                else:
                    act.wait_ge(conv_done, ONE + QG * q + BG * (b - 1))
                act.activation(ut_hi[:, b % 2, :, PAD:PAD + P],
                               ps[:, UT[b % 2], :].rearrange("p (g a) -> p g a", g=BG), ACT.Copy).then_inc(uthi_done, 1)

            def quarter(q, last):
                for i in range(NT):
                    act.wait_ge(pre_done, NT * q + i + 1)
                    act.activation(pre[:, i % 2, CQ:], pre[:, i % 2, CQ:], ACT.Sigmoid).then_inc(sig_done, 1)
                split = (lambda k: split_wout(k)) if last else (lambda k: split_hi(q + 1, k, False))
                ut(q, 0)
                ut(q, 1)
                split(0)
                split(1)
                ut(q, 2)
                split(2)
                ut(q, 3)
                split(3)

            act.wait_ge(const_made, 6)
            with act.Fori(0, NQ - 1) as q:
                quarter(q, False)
            quarter(NQ - 1, True)
            for k in range(4, KT):
                split_wout(k)
            def silu_tile(i, b):
                act.wait_ge(zt_done, i + 1)
                act.wait_ge(sl_done, i)
                for k in range(KT):
                    last = act.activation(s_full[:, k, :], ps[:, PZ + k // 4, P * (k % 4):P * (k % 4) + P], ACT.Silu,
                                          bias=col[:, 6, k:k + 1], scale=col[:, 5, k:k + 1])
                last.then_inc(s_done, 1)
                act.wait_ge(s_done, i + 1)
                if not (type(i) is int and i < 2):
                    act.wait_ge(yh_done, 2 * i - 2)
                act.activation(s_hi[:, b], s_full[:, :, :], ACT.Copy).then_inc(sh_done, 1)

            def h2t_copy(i):
                act.wait_ge(h2_tr, ONE + i + 1)
                act.wait_ge(rt_done, ONE + i)
                act.activation(h2t[:, :, :], ps[:, PH:PH + 2, :].rearrange("p b (k a) -> p (b k) a", a=P),
                               ACT.Copy).then_inc(h2t_done, 1)

            def step(i, b, first, last):
                if not last:
                    silu_tile(i + 1, 1 - b)
                if not first:
                    h2t_copy(i - 1)
                act.wait_ge(yb_done, 2 * i + 2)
                act.wait_ge(sqx_done, i)
                act.activation(junk2[:, :], yb[:, b, :], ACT.Square, scale=D ** -0.5,
                               accum_out=sy[:, b, 0:1]).then_inc(sqy_done, 1)
                act.wait_ge(x1_done, i + 1)
                act.wait_ge(sqy_done, i + 1)
                act.activation(junk2[:, :], x1[:, bass.ds(i, 1), :], ACT.Square, scale=D ** -0.5,
                               accum_out=sx[:, b, 0:1]).then_inc(sqx_done, 1)

            act.wait_ge(v_done, ONE + NQ * QH)
            silu_tile(0, 0)
            for j in range(4):
                act.wait_ge(brow_tr, j + 1)
                dst = rows[:, j, :] if j < 3 else h2[:, 0, :]
                b0 = (PH, PR)[j % 2]
                act.activation(dst, ps[:, b0:b0 + 2, :].rearrange("p b n -> p (b n)"), ACT.Copy).then_inc(rows_done, 1)
            act.wait_ge(wo_lo_done, KT)
            step(0, 0, True, False)
            with act.Fori(0, NT // 2 - 1) as t:
                step(2 * t + 1, 1, False, False)
                step(2 * t + 2, 0, False, False)
            step(NT - 1, 1, False, True)
            h2t_copy(NT - 1)
            act.wait_ge(log_done, ONE + NT)
            act.activation(aff[:, :, :], logits[:, :, :], ACT.Sigmoid).then_inc(aff_done, 1)

            def landed(j, e):
                act.wait_ge(raw_loaded[0][j], 16 * ((e >> 1) + 1))
                if not (type(e) is int and e == 0):
                    act.wait_ge(raw_loaded[1][j], ONE_DMA + 16 * ((e + 1) >> 1))

            def high(idx, slot_, q, k, down, e, free):
                if free is not None:
                    act.wait_ge(pr_used, free)
                if down:
                    if k % 2 == 0:
                        landed(4 + k // 2, e)
                    act.activation(pr_hi[:, slot_, :], raw_d[:, bass.ds(q, 1), k, :].rearrange("p o n -> p (o n)"),
                                   ACT.Copy).then_inc(pr_hi_done, 1)
                    return
                if k % 4 == 0:
                    landed(2 * (k // 4), e)
                    landed(2 * (k // 4) + 1, e)
                act.activation(pr_hi[:, slot_, :].rearrange("p (g n) -> p g n", g=2),
                               raw_gu[:, bass.ds(q, 1), :, k, :].rearrange("p o g n -> p (o g) n"),
                               ACT.Copy).then_inc(pr_hi_done, 5 if (type(idx) is int and idx == 7) else 1)

            def x_hi(b, n):
                act.wait_ge(xt_tr, n + 1)
                act.activation(xt_hi[:, b], ps[:, TR:TR + 2, :].rearrange("p b (k a) -> p (b k) a", a=P),
                               ACT.Copy).then_inc(xth_done, 1)

            def silu(b, used, n, freed):
                act.wait_ge(pr_used, used)
                act.wait_ge(he_tr, freed)
                act.activation(he[:, b, :], ps[:, 2 * b, :], ACT.Silu).then_inc(sil_done, 1)

            def y_0(b, n, scattered):
                act.wait_ge(d0_done, n + 1)
                act.wait_ge(scat[b], ONE_DMA + 16 * scattered)
                act.activation(ys[:, b, 0:512], ps[:, DN, :], ACT.Copy).then_inc(y0_done, 1)

            def he_hi(b, n):
                act.wait_ge(he_tr, n + 1)
                act.activation(het_hi[:, b], ps[:, TR + b, :].rearrange("p (k a) -> p k a", a=P),
                               ACT.Copy).then_inc(heth_done, 1)

            act.wait_ge(rt_done, ONE + NT)
            act.wait_ge(h2_done, NT)
            for k in range(4):
                high(k, k, 0, k, False, 0, None)
            act.wait_ge(tables, 1)
            last_st = act.value_load(counts[0:1, 0:1], min_val=0, max_val=NST - 1)
            st = last_st + 1
            w = Step(act, 0)
            x_hi(0, 0)
            with act.If(w.h > 0):
                x_hi(1, 1)
            for k in range(4, KT):
                high(k, k % 4, 0, k, False, 0, k - 3)
            silu(0, 8, 0, 0)
            x_hi(0, w.cn)
            with act.If(w.h > 0):
                silu(1, 8, 1, 0)
            with act.If(w.hn > 0):
                x_hi(1, w.cn + 1)
            for k in range(4):
                high(12 + k, k, w.en & 1, k, False, w.en, 9 + k)
            he_hi(0, 0)
            with act.If(w.h > 0):
                he_hi(1, 1)
            for k in range(4, KT):
                high(12 + k, k % 4, w.en & 1, k, False, w.en, 9 + k)
            with act.Fori(1, NST) as s:
                with act.If(s < st):
                    w = Step(act, s)
                    more = s + 1 < st
                    qp = w.ep & 1
                    for k in range(FT):
                        high(12 * s + 8 + k, k, qp, k, True, w.ep, 12 * s + 5 + k)
                    silu(0, 12 * s + 8, w.c, w.c)
                    with act.If(more):
                        x_hi(0, w.cn)
                    with act.Else():
                        act.wait_ge(tables, 1)
                    with act.If(w.h > 0):
                        silu(1, 12 * s + 8, w.c + 1, w.c)
                    with act.If(w.hp > 0):
                        y_0(0, w.cp, s - 1)
                    with act.If(w.hn > 0):
                        x_hi(1, w.cn + 1)
                    with act.If(more):
                        qn = w.en & 1
                        for k in range(4):
                            high(12 * s + 12 + k, k, qn, k, False, w.en, 12 * s + 9 + k)
                    with act.Else():
                        act.wait_ge(tables, 1)
                    with act.If(w.hp > 0):
                        y_0(1, w.cp + 1, w.nbp)
                    with act.Else():
                        y_0(0, w.cp, s - 1)
                    he_hi(0, w.c)
                    with act.If(w.h > 0):
                        he_hi(1, w.c + 1)
                    with act.If(more):
                        qn = w.en & 1
                        for k in range(4, KT):
                            high(12 * s + 12 + k, k % 4, qn, k, False, w.en, 12 * s + 9 + k)
                    with act.Else():
                        act.wait_ge(tables, 1)
                    act.wait_ge(tables, 1)
                act.wait_ge(tables, 1)
            w = Step(act, last_st)
            for k in range(FT):
                high(12 * st + k, k, (NE - 1) % 2, k, True, NE - 1, 12 * last_st + 9 + k)
            with act.If(w.h > 0):
                y_0(0, w.c, last_st)
                y_0(1, w.c + 1, w.nb)
            with act.Else():
                y_0(0, w.c, last_st)
            def first_choice(i):
                act.wait_ge(yl[i // 2], 32)
                if i >= FB:
                    act.wait_ge(o_done, i - FB + 1)
                act.activation(fb[:, i % FB, :], y_all[:, 0, i, :], ACT.Copy, scale=gates[:, 0, i:i + 1]).then_inc(fa_done, 1)

            first_choice(0)
            for i in range(NT):
                if i + 1 < NT:
                    first_choice(i + 1)
                act.wait_ge(f_done, i + 1)
                act.wait_ge(sqf_done, i)
                act.activation(junk3[:, :], fb[:, i % FB, :], ACT.Square, scale=D ** -0.5,
                               accum_out=sf[:, 0, i:i + 1]).then_inc(sqf_done, 1)

        @block.vector
        def _(dve):
            dve.wait_ge(cols_loaded, 16 * 8)
            dve.wait_ge(sigc_done, 1)
            dve.tensor_tensor(silc[:, 1, :], silc[:, 0, :], col[:, 0, :], ALU.mult).then_inc(silc_done, 1)

            dve.wait_ge(silc_done, 1)
            both = acc01[:, :, :].rearrange("p s d -> p (s d)")
            for k in range(KT):
                dve.wait_ge(ada1_loaded[k // 2], 16)
                if k == 0:
                    dve.tensor_scalar(both, ada_first[:, k, :], silc[:, 1, k:k + 1], None, ALU.mult).then_inc(acc1_done, 1)
                else:
                    dve.wait_ge(acc1_done, k)
                    dve.scalar_tensor_tensor(out=both, in0=ada_first[:, k, :], scalar=silc[:, 1, k:k + 1],
                                             in1=both, op0=ALU.mult, op1=ALU.add).then_inc(acc1_done, 1)
            dve.wait_ge(brow1_loaded, 32)
            dve.wait_ge(ada1_mod, 1)
            dve.tensor_tensor(mod_row[:, 1, :], ps[:, 2:4, :].rearrange("p b n -> p (b n)"), mod_row[:, 1, :],
                              ALU.add).then_inc(mod1_done, 1)
            dve.wait_ge(mod1_done, 1)
            dve.scalar_tensor_tensor(out=mod_row[:, 1, :], in0=mod_row[:, 1, :], scalar=1.0, in1=mod_row[:, 2, :],
                                     op0=ALU.add, op1=ALU.mult).then_inc(mod1_done, 1)
            dve.wait_ge(ada1_mod, 2)
            dve.tensor_tensor(mod_row[:, 0, :], ps[:, 0:2, :].rearrange("p b n -> p (b n)"), mod_row[:, 0, :],
                              ALU.add).then_inc(mod1_done, 1)
            dve.wait_ge(mod1_done, 3)

            def split_lo(q, k):
                dve.wait_ge(wi_hi_done, 4 * q + k + 1)
                dve.tensor_tensor(wi_lo[:, 2 * k:2 * k + 2, :],
                                  stage[:, k // 2, 1024 * (k % 2):1024 * (k % 2) + 1024].rearrange("p (k n) -> p k n", k=2),
                                  wi_hi[:, 2 * k:2 * k + 2, :].bitcast(F32), ALU.subtract).then_inc(wi_lo_done, 1)

            def split_wout(k):
                dve.wait_ge(wo_hi_done, k + 1)
                dve.tensor_tensor(sp_lo[:, k, :], stage[:, (k // 2) % 2, 1024 * (k % 2):1024 * (k % 2) + 1024],
                                  sp_hi[:, k, :].bitcast(F32), ALU.subtract).then_inc(wo_lo_done, 1)

            def gained(i):
                dve.wait_ge(rsx_done, i // 2 + 1)
                dve.scalar_tensor_tensor(out=xv[:, i, :], in0=xv[:, i, :], scalar=rsx[:, i:i + 1], in1=mod_row[:, 1, :],
                                         op0=ALU.mult, op1=ALU.mult).then_inc(xn_done, 1)

            def h_lo(i):
                dve.wait_ge(hhi_done, i + 1)
                b0 = UT[0] if i % 2 == 0 else CV[0]
                dve.tensor_tensor(sp_lo[:, :, P * i:P * i + P], ps[:, b0:b0 + 2, :].rearrange("p b (k a) -> p (b k) a", a=P),
                                  sp_hi[:, :, P * i:P * i + P].bitcast(F32), ALU.subtract).then_inc(hlo_done, 1)

            gained(0)
            gained(1)
            gained(2)
            for i in range(NT):
                h_lo(i)
                if i < 2:
                    split_lo(0, 2 * i)
                    split_lo(0, 2 * i + 1)
                if i + 3 < NT:
                    gained(i + 3)
            dve.wait_ge(hlo_done, NT)
            dve.wait_ge(const_made, 6)
            dve.wait_ge(eye_made, NT)

            def make_m(q, g):
                if g < MSLOTS:
                    dve.wait_ge(conv_done, ONE + QG * q)
                else:
                    dve.wait_ge(conv_done, ONE + QG * q + g - MSLOTS + 1)
                dve.tensor_tensor(mx[:, g % MSLOTS, :, 1, :].rearrange("p d (i c) -> p d i c", i=NT),
                                  taps_lo[:, g, :].bitcast(F32).rearrange("p (d i) -> p d i", d=ND).unsqueeze(3)
                                  .to_broadcast([P, ND, NT, GC]),
                                  eye16[:, :].unsqueeze(1).unsqueeze(1).to_broadcast([P, ND, NT, GC]),
                                  ALU.mult).then_inc(mlo_done, 1)

            def ut(q, b):
                dve.wait_ge(uthi_done, QB * q + b + 1)
                dve.tensor_tensor(ut_lo[:, b % 2, :, PAD:PAD + P],
                                  ps[:, UT[b % 2], :].rearrange("p (g a) -> p g a", g=BG),
                                  ut_hi[:, b % 2, :, PAD:PAD + P].bitcast(F32), ALU.subtract).then_inc(utlo_done, 1)

            def gate(q, i):
                dve.wait_ge(sig_done, NT * q + i + 1)
                dve.tensor_tensor(u[:, :, GC * i:GC * i + GC], pre[:, i % 2, 0:CQ].rearrange("p (g c) -> p g c", c=GC),
                                  pre[:, i % 2, CQ:].rearrange("p (g c) -> p g c", c=GC),
                                  ALU.mult).then_inc(u_done, 1)

            def quarter(q, last):
                dve.wait_ge(ut_tr, ONE + QB * q)
                dve.wait_ge(brow_loaded, 16 * q + 16)
                for i in range(NT):
                    dve.wait_ge(win_tile, NT * q + i + 1)
                    dve.wait_ge(u_done, ONE + NT * q + max(i - 1, 0))
                    dve.tensor_tensor(pre[:, i % 2, :], ps[:, WI[i % 3], :], bin_row[:, :],
                                      ALU.add).then_inc(pre_done, 1)
                    if i >= 1:
                        gate(q, i - 1)
                    dve.wait_ge(ada_loaded[i % 2], 64 * q + 16 * (i // 2) + 16)
                    if i == 0:
                        dve.wait_ge(acc_col, ONE + q)
                        dve.tensor_scalar(acc[:, :], ada_stage[:, 0, :], silc[:, 1, 0:1], None,
                                          ALU.mult).then_inc(acc_done, 1)
                    else:
                        dve.wait_ge(acc_done, ONE + KT * q + i)
                        dve.scalar_tensor_tensor(out=acc[:, :], in0=ada_stage[:, i % 2, :], scalar=silc[:, 1, i:i + 1],
                                                 in1=acc[:, :], op0=ALU.mult, op1=ALU.add).then_inc(acc_done, 1)
                    if i < MSLOTS:
                        if i == 0:
                            dve.wait_ge(taps_split, 2 * q + 2)
                        make_m(q, i)
                gate(q, NT - 1)
                split = split_wout if last else (lambda k: split_lo(q + 1, k))
                ut(q, 0)
                ut(q, 1)
                dve.wait_ge(acc_col, ONE + q + 1)
                dve.tensor_tensor(modc[:, bass.ds(q, 1), :], ps[:, MODB, 16:16 + KT].unsqueeze(1),
                                  bada[:, bass.ds(q + 2, 1), :], ALU.add).then_inc(modc_done, 1)
                dve.wait_ge(bdw_loaded, 16 * q + 16)
                for b in range(QB):
                    for h in (2 * b, 2 * b + 1):
                        if b + 1 < QB:
                            for g in range(CG):
                                make_m(q, CG * h + BG + g)
                        vo = xv[:, :, bass.ds(q * CQ + CG * GC * h, CG * GC)].rearrange("p i (g c) -> p g i c", g=CG)
                        vp = ps[:, CV[h % 2], :].rearrange("p (g s i c) -> p g s i c", g=CG, s=2, i=NT)
                        dve.wait_ge(conv_done, ONE + QG * q + CG * (h + 1))
                        dve.tensor_tensor(vo, vp[:, :, 1], bdw_row[:, CG * GC * h:CG * GC * (h + 1)]
                                          .rearrange("p (g c) -> p g c", g=CG).unsqueeze(2)
                                          .to_broadcast([P, CG, NT, GC]), ALU.add).then_inc(vb_done, 1)
                        dve.wait_ge(vb_done, QH * q + h + 1)
                        dve.tensor_tensor(vo, vp[:, :, 0], vo, ALU.add).then_inc(v_done, 1)
                    split(b)
                    if b + 2 < QB:
                        ut(q, b + 2)

            with dve.Fori(0, NQ - 1) as q:
                quarter(q, False)
            quarter(NQ - 1, True)
            dve.wait_ge(modc_done, ONE + NQ)
            dve.tensor_tensor(vcol[:, 0, :], modc[:, 0, :], col[:, 2, :], ALU.mult).then_inc(vcol_done, 1)
            dve.scalar_tensor_tensor(out=vcol[:, 1, :], in0=modc[:, 2, :], scalar=1.0, in1=col[:, 3, :],
                                     op0=ALU.add, op1=ALU.mult).then_inc(vcol_done, 1)
            dve.tensor_tensor(vcol[:, 2, :], modc[:, 3, :], col[:, 4, :], ALU.mult).then_inc(vcol_done, 1)
            dve.wait_ge(vcol_done, 3)

            def diagonal(j):
                if j >= 2:
                    dve.wait_ge(brow_tr, j - 1)
                cc = (vcol[:, 0, :], vcol[:, 1, :], modc[:, 1, :], vcol[:, 2, :])[j]
                dve.tensor_tensor(diag[j % 2][:, :, :], ident[:, :].unsqueeze(2).to_broadcast([P, P, KT]),
                                  cc.unsqueeze(1).to_broadcast([P, P, KT]), ALU.mult).then_inc(diag_done, 1)

            def moments(i):
                dve.bn_stats(stats[:, i, 0, :], xv[:, i, 0:512]).then_inc(stats_done, 1)
                dve.bn_stats(stats[:, i, 1, :], xv[:, i, 512:1024]).then_inc(stats_done, 1)
                dve.wait_ge(stats_done, 2 * i + 2)
                dve.bn_aggr(mv[:, i, :], stats[:, i]).then_inc(mv_done, 1)

            def normalised(i, first):
                if not first:
                    dve.wait_ge(zt_done, i)
                dve.tensor_scalar(zb[:, :], xv[:, bass.ds(i, 1), :].rearrange("p o d -> p (o d)"),
                                  mv[:, bass.ds(i, 1), 0:1].rearrange("p o j -> p (o j)"),
                                  lnr[:, 1, bass.ds(i, 1)], ALU.subtract, ALU.mult).then_inc(z_done, 1)

            def s_low(i, b, first):
                dve.wait_ge(sh_done, i + 1)
                if not first:
                    dve.wait_ge(yh_done, 2 * i - 2)
                dve.tensor_tensor(s_lo[:, b], s_full[:, :, :], s_hi[:, b].bitcast(F32), ALU.subtract).then_inc(sl_done, 1)

            def y_half(i, b, h):
                dve.wait_ge(yh_done, 2 * i + h + 1)
                cols = slice(512 * h, 512 * h + 512)
                dve.tensor_tensor(yb[:, b, cols], ps[:, PY + h, :], bout_row[:, cols], ALU.add).then_inc(yb_done, 1)

            def logits_of(i):
                dve.wait_ge(rt_done, ONE + i + 1)
                dve.tensor_copy(logits[:, bass.ds(i, 1), :], ps[:, PR, 0:NE].unsqueeze(1)).then_inc(log_done, 1)

            def gained(i, b):
                dve.wait_ge(rx_done, i + 1)
                if type(i) is int and i == 0:
                    dve.wait_ge(g3_stored, 16)
                elif not (type(i) is int and i == 1):
                    dve.wait_ge(h2_stored[b], ONE_DMA + 16 * ((i - b) // 2))
                    dve.wait_ge(h2_tr, ONE + i - 1)
                dve.scalar_tensor_tensor(out=h2[:, b, :], in0=x1[:, bass.ds(i, 1), :].rearrange("p o d -> p (o d)"),
                                         scalar=sx[:, b, 2:3], in1=rows[:, 1, :],
                                         op0=ALU.mult, op1=ALU.mult).then_inc(hg_done, 1)

            def step(i, b, first, last):
                if not last and not first:
                    normalised(i + 1, False)
                if not first:
                    gained(i - 1, 1 - b)
                y_half(i, b, 0)
                if not last:
                    s_low(i + 1, 1 - b, first)
                y_half(i, b, 1)
                dve.wait_ge(ry_done, i + 1)
                dve.scalar_tensor_tensor(out=yb[:, b, :], in0=yb[:, b, :], scalar=sy[:, b, 2:3], in1=rows[:, 0, :],
                                         op0=ALU.mult, op1=ALU.mult).then_inc(t_done, 1)
                dve.wait_ge(t_done, i + 1)
                xi = x1[:, bass.ds(i, 1), :].rearrange("p o d -> p (o d)")
                dve.wait_ge(xr_loaded[b], 16 * ((i - b) // 2) + 16)
                dve.tensor_tensor(xi, yb[:, b, :], xr[:, b, :], ALU.add).then_inc(x1_done, 1)
                if not first:
                    logits_of(i - 1)

            dve.wait_ge(v_done, ONE + NQ * QH)
            moments(0)
            moments(1)
            split_wout(4)
            dve.wait_ge(lnr_done, 1)
            dve.wait_ge(mv_done, 2)
            normalised(0, True)
            for k in range(5, KT):
                split_wout(k)
            diagonal(0)
            diagonal(1)
            dve.wait_ge(sh_done, 1)
            dve.tensor_tensor(s_lo[:, 0], s_full[:, :, :], s_hi[:, 0].bitcast(F32), ALU.subtract).then_inc(sl_done, 1)
            normalised(1, False)
            diagonal(2)
            diagonal(3)
            for i in range(2, NT):
                moments(i)
            dve.wait_ge(lnr_done, 2)
            dve.wait_ge(mv_done, NT)
            dve.wait_ge(bout_loaded, 16)
            step(0, 0, True, False)
            step(1, 1, False, False)
            with dve.Fori(1, NT // 2 - 1) as t:
                step(2 * t, 0, False, False)
                step(2 * t + 1, 1, False, False)
            step(NT - 2, 0, False, False)
            step(NT - 1, 1, False, True)
            gained(NT - 1, 1)
            logits_of(NT - 1)
            def low(turn, slot_, q, k, down, inc):
                dve.wait_ge(pr_hi_done, 4 * turn + slot_ + 1)
                if down:
                    dve.tensor_tensor(pr_lo[:, slot_, :], raw_d[:, bass.ds(q, 1), k, :].rearrange("p o n -> p (o n)"),
                                      pr_hi[:, slot_, :].bitcast(F32), ALU.subtract).then_inc(pr_lo_dve, inc)
                else:
                    dve.tensor_tensor(pr_lo[:, slot_, :].rearrange("p (g n) -> p g n", g=2),
                                      raw_gu[:, bass.ds(q, 1), :, k, :].rearrange("p o g n -> p (o g) n"),
                                      pr_hi[:, slot_, :].bitcast(F32).rearrange("p (g n) -> p g n", g=2),
                                      ALU.subtract).then_inc(pr_lo_dve, inc)

            chain = [0]

            def then(ins):
                ins.then_inc(route_chain, 1)
                chain[0] += 1
                dve.wait_ge(route_chain, chain[0])

            def tt(o, a, b, op):
                then(dve.tensor_tensor(o, a, b, op))

            def ts(o, a, x_, y_, op0, op1=None):
                if op1 is None:
                    then(dve.tensor_scalar(o, a, x_, None, op0))
                else:
                    then(dve.tensor_scalar(o, a, x_, y_, op0, op1))

            def total(o, a, op=ALU.add):
                then(dve.tensor_reduce(o, a, axis=AX_X, op=op))

            dve.wait_ge(aff_done, 1)
            dve.wait_ge(rconst, NG + 5)
            dve.wait_ge(rt_done, ONE + NT)
            dve.wait_ge(h2_done, NT)
            dve.wait_ge(h2_stored[0], ONE_DMA + 16 * (NT // 2))
            dve.wait_ge(h2_stored[1], ONE_DMA + 16 * (NT // 2))
            tt(sel[:, :, :], aff[:, :, :], rb_row[:, :].unsqueeze(1).to_broadcast([P, NT, NE]), ALU.add)
            s4 = sel[:, :, :].rearrange("p t (g h j) -> p (t g) h j", g=NG, h=2)
            tt(pair_max[:, :, :], s4[:, :, :, 0], s4[:, :, :, 1], ALU.max)
            tt(pair_min[:, :, :], s4[:, :, :, 0], s4[:, :, :, 1], ALU.min)

            def g6(j):
                return gs[:, j].rearrange("p t g -> p (t g)")

            tt(g6(0), pair_max[:, :, 0], pair_max[:, :, 1], ALU.max)
            tt(g6(1), pair_max[:, :, 0], pair_max[:, :, 1], ALU.min)
            tt(g6(2), pair_min[:, :, 0], pair_min[:, :, 1], ALU.max)
            tt(g6(1), g6(1), g6(2), ALU.max)
            tt(g6(0), g6(0), g6(1), ALU.add)
            total(gmax[:, 0, :], gs[:, 0], ALU.max)
            tt(gs[:, 3], gs[:, 0], gmax[:, 0, :].unsqueeze(2).to_broadcast([P, NT, NG]), ALU.is_ge)
            tt(gs[:, 3], gs[:, 3], desc4[:, :].unsqueeze(1).to_broadcast([P, NT, NG]), ALU.mult)
            total(gmax[:, 1, :], gs[:, 3], ALU.max)
            tt(gs[:, 4], gs[:, 3], gmax[:, 1, :].unsqueeze(2).to_broadcast([P, NT, NG]), ALU.is_equal)
            sg = sel[:, :, :].rearrange("p t (g j) -> p (t g) j", g=NG)
            inner = sg.unsqueeze(2).to_broadcast([P, NT * NG, EG, EG])
            outer = sg.unsqueeze(3).to_broadcast([P, NT * NG, EG, EG])
            tt(beats[:, 0], inner, outer, ALU.is_gt)
            tt(beats[:, 1], inner, outer, ALU.is_equal)
            tt(beats[:, 1], beats[:, 1], lt4[:, :, :].unsqueeze(1).to_broadcast([P, NT * NG, EG, EG]), ALU.mult)
            tt(beats[:, 0], beats[:, 0], beats[:, 1], ALU.add)
            total(rank[:, :, :].rearrange("p t (g j) -> p (t g) j", g=NG), beats[:, 0])
            for k in range(2):
                ts(mk[:, k], rank[:, :, :], float(k), None, ALU.is_equal)
                tt(mk[:, k].rearrange("p t (g j) -> p (t g) j", g=NG), mk[:, k].rearrange("p t (g j) -> p (t g) j", g=NG),
                   g6(4).unsqueeze(2).to_broadcast([P, NT * NG, EG]), ALU.mult)
            then(dve.memset(m9[:, NT, :], 0.0))
            tt(m9[:, 0:NT, :], mk[:, 0], mk[:, 1], ALU.add)
            marks["chosen"] = chain[0]
            for k in range(2):
                tt(prod[:, NT * k:NT * k + NT, :], mk[:, k], aff[:, :, :], ALU.mult)
            total(ak[:, :, :].rearrange("p k t -> p (k t)"), prod[:, :, :])
            tt(den[:, 0, :], ak[:, 0, :], ak[:, 1, :], ALU.add)
            then(dve.reciprocal(den[:, 1, :], den[:, 0, :]))
            tt(gates[:, :, :], ak[:, :, :], den[:, 1, :].unsqueeze(1).to_broadcast([P, 2, NT]), ALU.mult)
            dve.wait_ge(pos_done, 1)
            then(dve.tensor_copy(cnt[:, 0, :], ps[:, PZ, NT * NE:NT * NE + NE]))
            ts(cnt[:, 1, :], cnt[:, 0, :], float(ST_ROWS), None, ALU.is_gt)
            for j in (2, 3):
                then(dve.scalar_tensor_tensor(out=cnt[:, 1, :], in0=cnt[:, 0, :], scalar=float(j * ST_ROWS),
                                              in1=cnt[:, 1, :], op0=ALU.is_gt, op1=ALU.add))
            ts(cnt[:, 1, :], cnt[:, 1, :], 1.0, None, ALU.add)
            tt(prod16[:, :, :], le16[:, :, :], cnt[:, 1, :].unsqueeze(1).to_broadcast([P, NE, NE]), ALU.mult)
            total(cnt[:, 2, :], prod16[:, :, :])
            tt(cnt[:, 3, :], cnt[:, 2, :], cnt[:, 1, :], ALU.subtract)
            ts(cnt[:, 4, :], cnt[:, 3, :], float(ST_ROWS), None, ALU.mult)
            tt(cnt[:, 5, :], cnt[:, 4, :], cnt[:, 0, :], ALU.add)
            tt(pos[:, :, :], ps[:, PZ, 0:NT * NE].rearrange("p (t e) -> p t e", e=NE),
               cnt[:, 4, :].unsqueeze(1).to_broadcast([P, NT, NE]), ALU.add)
            for k in range(2):
                tt(prod[:, NT * k:NT * k + NT, :], mk[:, k], pos[:, :, :], ALU.mult)
            total(slot[:, :], prod[:, :, :])
            then(dve.tensor_copy(slot_i[:, 0, :], slot[:, :]))
            ts(slot_i[:, 1, :], slot_i[:, 0, :], 7, None, ALU.arith_shift_right)
            ts(slot_i[:, 2, :], slot_i[:, 0, :], P - 1, None, ALU.bitwise_and)
            then(dve.tensor_copy(slot_f[:, :, :], slot_i[:, 1:3, :]))
            tt(oh_p[:, :, :], iota[:, :].unsqueeze(1).to_broadcast([P, 2 * NT, P]),
               slot_f[:, 1, :].unsqueeze(2).to_broadcast([P, 2 * NT, P]), ALU.is_equal)
            tt(oh_t[:, :, :], iota[:, 0:2 * NSTC].unsqueeze(1).to_broadcast([P, 2 * NT, 2 * NSTC]),
               slot_f[:, 0, :].unsqueeze(2).to_broadcast([P, 2 * NT, 2 * NSTC]), ALU.is_equal)
            tt(oh_t[:, :, :], oh_t[:, :, :], tok1[:, :].unsqueeze(2).to_broadcast([P, 2 * NT, 2 * NSTC]), ALU.mult)
            marks["slots"] = chain[0]
            ts(start[:, 0, :], iota[:, 0:NSTC], float(ST_ROWS), None, ALU.mult)
            ts(start[:, 1, :], start[:, 0, :], float(P), None, ALU.add)
            sh3 = [P, NSTC, NE]
            srow = iota[:, 0:NSTC].unsqueeze(2).to_broadcast(sh3)
            tt(st_le[:, :, :], cnt[:, 2, :].unsqueeze(1).to_broadcast(sh3), srow, ALU.is_le)
            tt(st_in[:, :, :], cnt[:, 3, :].unsqueeze(1).to_broadcast(sh3), srow, ALU.is_le)
            tt(st_in[:, :, :], st_in[:, :, :], st_le[:, :, :], ALU.subtract)
            tt(st_ab[:, :, :], cnt[:, 5, :].unsqueeze(1).to_broadcast(sh3),
               start[:, 1, :].unsqueeze(2).to_broadcast(sh3), ALU.is_gt)
            tt(st_ab[:, :, :], st_ab[:, :, :], st_in[:, :, :], ALU.mult)
            then(dve.memset(e_of[:, :], 0.0))
            then(dve.memset(hb_of[:, :, :], 0.0))
            total(e_of[:, 1:NSTC + 1], st_le[:, :, :])
            total(hb_of[:, 0, 16:16 + NSTC], st_ab[:, :, :])
            then(dve.tensor_copy(word_f[:, 1, :], hb_of[:, 0, 16:16 + NSTC]))
            marks["hb"] = chain[0]
            then(dve.scalar_tensor_tensor(out=word_f[:, 0, :], in0=e_of[:, 1:NSTC + 1], scalar=32.0,
                                          in1=e_of[:, 0:NSTC], op0=ALU.mult, op1=ALU.add))
            for scale_, v in ((1024.0, e_of[:, 2:NSTC + 2]), (2.0 ** 15, hb_of[:, 0, 15:15 + NSTC]),
                              (2.0 ** 16, hb_of[:, 0, 16:16 + NSTC]), (2.0 ** 17, hb_of[:, 0, 17:17 + NSTC])):
                then(dve.scalar_tensor_tensor(out=word_f[:, 0, :], in0=v, scalar=scale_,
                                              in1=word_f[:, 0, :], op0=ALU.mult, op1=ALU.add))
            for j, d in enumerate((1, 2, 4, 8, 16)):
                tt(hb_of[:, (j + 1) % 2, 16:16 + NSTC], hb_of[:, j % 2, 16:16 + NSTC],
                   hb_of[:, j % 2, 16 - d:16 - d + NSTC], ALU.add)
            then(dve.scalar_tensor_tensor(out=word_f[:, 0, :], in0=hb_of[:, 1, 14:14 + NSTC], scalar=2.0 ** 18,
                                          in1=word_f[:, 0, :], op0=ALU.mult, op1=ALU.add))
            then(dve.tensor_copy(words[:, :], word_f[:, 0, :]))
            ts(ct_i[:, :], cnt[:, 2, :], -1.0, None, ALU.add)
            ts(counts[:, 0:1], cnt[:, 2, NE - 1:NE], -1.0, None, ALU.add)
            then(dve.tensor_copy(counts[:, 1:2], hb_of[:, 1, 15 + NSTC:16 + NSTC]))
            for k in range(3):
                low(0, k, 0, k, False, 1)
            dve.wait_ge(slots_done, 1)
            ts(dest[:, :], ps[:, PZ + 1, 0:2 * NSTC], -1.0, None, ALU.add)
            ts(src[:, 0:2 * NSTC], dest[:, :], S - 1, None, ALU.bitwise_and)
            then(dve.memset(gap[:, :], 0.0))
            dve.tensor_copy(gap[:, :], gmax[:, 0, 0:1]).then_inc(tables, 1)

            last_st = dve.value_load(counts[0:1, 0:1], min_val=0, max_val=NST - 1)
            st = last_st + 1

            def x_lo(b, n):
                dve.wait_ge(xth_done, n + 1)
                dve.tensor_tensor(xt_lo[:, b], ps[:, TR:TR + 2, :].rearrange("p b (k a) -> p (b k) a", a=P),
                                  xt_hi[:, b].bitcast(F32), ALU.subtract).then_inc(xtl_done, 1)

            def times_up(b, n):
                dve.wait_ge(sil_done, n + 1)
                dve.tensor_tensor(he[:, b, :], he[:, b, :], ps[:, 2 * b + 1, :], ALU.mult).then_inc(he_done, 1)

            def y_1(b, sem_, n, scattered):
                dve.wait_ge(sem_, n)
                dve.wait_ge(scat[b], ONE_DMA + 16 * scattered)
                dve.tensor_copy(ys[:, b, 512:1024], ps[:, DN + 1, :]).then_inc(y1_done, 1)

            def he_lo(b, n):
                dve.wait_ge(heth_done, n + 1)
                dve.tensor_tensor(het_lo[:, b], ps[:, TR + b, :].rearrange("p (k a) -> p k a", a=P),
                                  het_hi[:, b].bitcast(F32), ALU.subtract).then_inc(hetl_done, 1)

            w = Step(dve, 0)
            x_lo(0, 0)
            with dve.If(w.h > 0):
                x_lo(1, 1)
            for k in range(3):
                low(1, k, 0, k + 4, False, 4 if k == 2 else 1)
            times_up(0, 0)
            x_lo(0, w.cn)
            with dve.If(w.h > 0):
                times_up(1, 1)
            with dve.If(w.hn > 0):
                x_lo(1, w.cn + 1)
            for k in range(3):
                low(3, k, w.en & 1, k, False, 1)
            he_lo(0, 0)
            with dve.If(w.h > 0):
                he_lo(1, 1)
            for k in range(3):
                low(4, k, w.en & 1, k + 4, False, 1)
            with dve.Fori(1, NST) as s:
                with dve.If(s < st):
                    w = Step(dve, s)
                    more = s + 1 < st
                    qp = w.ep & 1
                    for k in range(3):
                        low(3 * s + 2, k, qp, k, True, 1)
                    times_up(0, w.c)
                    with dve.If(more):
                        x_lo(0, w.cn)
                    with dve.Else():
                        dve.wait_ge(tables, 1)
                    with dve.If(w.h > 0):
                        times_up(1, w.c + 1)
                    with dve.If(w.hp > 0):
                        y_1(0, d1_done, w.nbp + 1, s - 1)
                    with dve.If(w.hn > 0):
                        x_lo(1, w.cn + 1)
                    with dve.If(more):
                        qn = w.en & 1
                        for k in range(3):
                            low(3 * s + 3, k, qn, k, False, 1)
                    with dve.Else():
                        dve.wait_ge(tables, 1)
                    with dve.If(w.hp > 0):
                        y_1(1, pr_used, 12 * s + 12, w.nbp)
                    with dve.Else():
                        y_1(0, pr_used, 12 * s + 12, s - 1)
                    he_lo(0, w.c)
                    with dve.If(w.h > 0):
                        he_lo(1, w.c + 1)
                    with dve.If(more):
                        qn = w.en & 1
                        for k in range(3):
                            low(3 * s + 4, k, qn, k + 4, False, 1)
                    with dve.Else():
                        dve.wait_ge(tables, 1)
                    dve.wait_ge(tables, 1)
                dve.wait_ge(tables, 1)
            w = Step(dve, last_st)
            for k in range(3):
                low(3 * st, k, (NE - 1) % 2, k, True, 1)
            with dve.If(w.h > 0):
                y_1(0, d1_done, w.nb + 1, last_st)
                y_1(1, pr_used, 12 * st + 4, w.nb)
            with dve.Else():
                y_1(0, pr_used, 12 * st + 4, last_st)
            dve.wait_ge(g3_loaded, 16)

            def scaled(i):
                dve.wait_ge(rf_done, i + 1)
                dve.scalar_tensor_tensor(out=fb[:, i % FB, :], in0=fb[:, i % FB, :], scalar=sf[:, 2, i:i + 1], in1=g3[:, :],
                                         op0=ALU.mult, op1=ALU.mult).then_inc(fg_done, 1)

            for i in range(NT):
                dve.wait_ge(fa_done, i + 1)
                dve.scalar_tensor_tensor(out=fb[:, i % FB, :], in0=y_all[:, 1, i, :], scalar=gates[:, 1, i:i + 1],
                                         in1=fb[:, i % FB, :], op0=ALU.mult, op1=ALU.add).then_inc(f_done, 1)
                if i >= 1:
                    scaled(i - 1)
            scaled(NT - 1)

        @block.tensor
        def _(pe):
            pe.wait_ge(const_made, 6)
            pe.wait_ge(acc1_done, KT)
            for sec in (1, 0):
                for h in range(2):
                    last = pe.matmul(ps[:, 2 * sec + h, :], ones[:, :], acc01[:, sec, 512 * h:512 * h + 512],
                                     start=True, stop=True)
                last.then_inc(ada1_mod, 1)
            pe.wait_ge(mod1_done, 3)
            for i in range(NT):
                pe.wait_ge(hs_done, i + 1)
                if i >= 2:
                    pe.wait_ge(hlo_done, i - 1)
                b0 = UT[0] if i % 2 == 0 else CV[0]
                for k in range(KT):
                    last = pe.transpose(ps[:, b0 + k // 4, P * (k % 4):P * (k % 4) + P],
                                        xv[:, i, bass.ds(k, P, step=KT)], ident[:, :])
                last.then_inc(xt_done, 1)

            def quarter(q):
                for i in range(NT):
                    pe.wait_ge(hlo_done, i + 1)
                    if i >= 3:
                        pe.wait_ge(pre_done, NT * q + i - 2)
                    o = ps[:, WI[i % 3], :]
                    for k in range(KT):
                        if i == 0 and k % 2 == 0:
                            pe.wait_ge(wi_lo_done, 4 * q + k // 2 + 1)
                        tok = slice(P * i, P * i + P)
                        pe.matmul(o, sp_hi[:, k, tok], wi_hi[:, k, :], start=(k == 0), stop=False)
                        pe.matmul(o, sp_hi[:, k, tok], wi_lo[:, k, :], start=False, stop=False)
                        last = pe.matmul(o, sp_lo[:, k, tok], wi_hi[:, k, :], start=False, stop=(k == KT - 1))
                        if i == NT - 1 and k % 2 == 1 and k < KT - 1:
                            last.then_inc(wi_used, 1)
                    last.then_inc(win_tile, 1)
                pe.wait_ge(acc_done, ONE + KT * q + KT)
                pe.wait_ge(modc_done, ONE + q)
                for j in range(KT):
                    last = pe.matmul(ps[:, MODB, 16 + j:17 + j], acc[:, bass.ds(j, P, step=KT)], ones[:, 0:1],
                                     start=(j == 0), stop=True, skip_group_check=True)
                last.then_inc(acc_col, 1)

                def turn(b):
                    if b == 0:
                        pe.wait_ge(u_done, ONE + NT * q + NT)
                    if b >= 2:
                        pe.wait_ge(utlo_done, QB * q + b - 1)
                    for g in range(BG):
                        last = pe.transpose(ps[:, UT[b % 2], P * g:P * g + P], u[:, BG * b + g, :], ident[:, :])
                    last.then_inc(ut_tr, 1)

                def conv(b):
                    pe.wait_ge(utlo_done, QB * q + b + 1)
                    for g in range(BG):
                        n = BG * b + g
                        m = n % MSLOTS
                        h = n // CG
                        if g % CG == 0:
                            pe.wait_ge(v_done, ONE + QH * q + max(h - 1, 0))
                        pe.wait_ge(mhi_done, QG * q + n + 1)
                        pe.wait_ge(mlo_done, ONE + QG * q + n + 1)
                        o = ps[:, CV[h % 2], 2 * P * (g % CG):2 * P * (g % CG) + 2 * P]
                        for d in range(ND):
                            tok = slice(2 * PAD - d, 2 * PAD - d + P)
                            uh, ul = ut_hi[:, b % 2, g, tok], ut_lo[:, b % 2, g, tok]
                            pe.matmul(o, uh, mx[:, m, d].rearrange("p s n -> p (s n)"), start=(d == 0), stop=False,
                                      skip_group_check=True)
                            last = pe.matmul(o[:, 0:P], ul, mx[:, m, d, 0, :], start=False, stop=(d == ND - 1),
                                             skip_group_check=True)
                        last.then_inc(conv_done, 1)

                turn(0)
                turn(1)
                conv(0)
                turn(2)
                conv(1)
                turn(3)
                conv(2)
                conv(3)

            with pe.Fori(0, NQ) as q:
                quarter(q)

            def turn_z(i):
                pe.wait_ge(z_done, i + 1)
                pe.wait_ge(s_done, i)
                for k in range(KT):
                    last = pe.transpose(ps[:, PZ + k // 4, P * (k % 4):P * (k % 4) + P],
                                        zb[:, bass.ds(k, P, step=KT)], ident[:, :])
                last.then_inc(zt_done, 1)

            def y_mm(i, b, h, ks, first=False):
                cols = slice(512 * h, 512 * h + 512)
                o = ps[:, PY + h, :]
                for k in ks:
                    if k == 0:
                        pe.wait_ge(sl_done, i + 1)
                        pe.wait_ge(yb_done, 2 * i)
                    if first and h == 0 and k >= 4:
                        pe.wait_ge(wo_lo_done, k + 1)
                    pe.matmul(o, s_hi[:, b, k, :], sp_hi[:, k, cols], start=(k == 0), stop=False)
                    pe.matmul(o, s_hi[:, b, k, :], sp_lo[:, k, cols], start=False, stop=False)
                    last = pe.matmul(o, s_lo[:, b, k, :], sp_hi[:, k, cols], start=False, stop=(k == KT - 1))
                if ks[-1] == KT - 1:
                    last.then_inc(yh_done, 1)

            def turn_h2(i, b):
                pe.wait_ge(h2_done, i + 1)
                pe.wait_ge(h2t_done, ONE + i)
                for k in range(KT):
                    last = pe.transpose(ps[:, PH + k // 4, P * (k % 4):P * (k % 4) + P],
                                        h2[:, b, bass.ds(k, P, step=KT)], ident[:, :])
                last.then_inc(h2_tr, 1)

            def route(i):
                pe.wait_ge(h2t_done, ONE + i + 1)
                pe.wait_ge(log_done, ONE + i)
                for k in range(KT):
                    last = pe.matmul(ps[:, PR, 0:NE], h2t[:, k, :], rwt[:, k, :], start=(k == 0), stop=(k == KT - 1))
                last.then_inc(rt_done, 1)

            def step(i, b, first, last):
                y_mm(i, b, 0, list(range(KT)), first)
                if not last:
                    turn_z(i + 1)
                y_mm(i, b, 1, [0, 1, 2, 3, 4, 5])
                if not first:
                    turn_h2(i - 1, 1 - b)
                y_mm(i, b, 1, [6, 7])
                if not first:
                    route(i - 1)

            turn_z(0)
            for j in range(4):
                pe.wait_ge(diag_done, j + 1)
                if j >= 2:
                    pe.wait_ge(rows_done, j - 1)
                if j == 1:
                    pe.wait_ge(modc_done, ONE + NQ)
                b0 = (PH, PR)[j % 2]
                for h in range(2):
                    last = pe.matmul(ps[:, b0 + h, :], ones[:, :],
                                     diag[j % 2][:, 64 * h:64 * h + 64, :].rearrange("p j k -> p (j k)"),
                                     start=True, stop=True)
                last.then_inc(brow_tr, 1)
            pe.wait_ge(rw_loaded, 32)
            pe.wait_ge(wo_lo_done, 4)
            step(0, 0, True, False)
            with pe.Fori(0, NT // 2 - 1) as t:
                step(2 * t + 1, 1, False, False)
                step(2 * t + 2, 0, False, False)
            step(NT - 1, 1, False, True)
            turn_h2(NT - 1, 1)
            route(NT - 1)
            pe.wait_ge(route_chain, marks["chosen"])
            pe.matmul(ps[:, PZ, 0:NE * (NT + 1)], tri[:, :], m9[:, :, :].rearrange("p t e -> p (t e)"),
                      start=True, stop=False, skip_group_check=True)
            for t in range(NT):
                last = pe.matmul(ps[:, PZ, NE * (t + 1):NE * (NT + 1)], ones[:, :],
                                 m9[:, t:t + 1, :].to_broadcast([P, NT - t, NE]),
                                 start=False, stop=(t == NT - 1), skip_group_check=True)
            last.then_inc(pos_done, 1)
            pe.wait_ge(route_chain, marks["slots"])
            for j in range(2 * NT):
                last = pe.matmul(ps[:, PZ + 1, 0:2 * NSTC], oh_p[:, j, :], oh_t[:, j, :],
                                 start=(j == 0), stop=(j == 2 * NT - 1))
            last.then_inc(slots_done, 1)

            pe.wait_ge(tables, 1)
            last_st = pe.value_load(counts[0:1, 0:1], min_val=0, max_val=NST - 1)
            st = last_st + 1

            def turn_x(b, n, held, landed):
                pe.wait_ge(gath[b], 16 * landed)
                pe.wait_ge(xtl_done, n)
                pe.wait_ge(hetl_done, held)
                for k in range(KT):
                    last = pe.transpose(ps[:, TR + k // 4, P * (k % 4):P * (k % 4) + P],
                                        xg[:, b, bass.ds(k, P, step=KT)], ident[:, :])
                last.then_inc(xt_tr, 1)

            def pair(turn, slot_):
                if slot_ < 3:
                    pe.wait_ge(pr_lo_dve, 3 * turn + slot_ + 1)
                else:
                    pe.wait_ge(pr_lo_pool, turn + 1)

            def gate_up(turn, c, cn, h, last_inc):
                pe.wait_ge(xtl_done, cn)
                pe.wait_ge(he_done, ONE + c)

                def tile(b, k):
                    sl = k % RING
                    g, up = ps[:, 2 * b, :], ps[:, 2 * b + 1, :]
                    first, end = k == 0, k == KT - 1
                    xh, xl = xt_hi[:, b, k, :], xt_lo[:, b, k, :]
                    pe.matmul(g, xh, pr_hi[:, sl, 0:F], start=first, stop=False)
                    pe.matmul(up, xh, pr_hi[:, sl, F:], start=first, stop=False)
                    pe.matmul(g, xh, pr_lo[:, sl, 0:F], start=False, stop=False)
                    pe.matmul(up, xh, pr_lo[:, sl, F:], start=False, stop=False)
                    pe.matmul(g, xl, pr_hi[:, sl, 0:F], start=False, stop=end)
                    return pe.matmul(up, xl, pr_hi[:, sl, F:], start=False, stop=end)

                def all_tiles(two):
                    for k in range(KT):
                        pair(turn + k // RING, k % RING)
                        last = tile(0, k)
                        if two:
                            last = tile(1, k)
                        last.then_inc(pr_used, last_inc if k == KT - 1 else 1)

                with pe.If(h > 0):
                    all_tiles(True)
                with pe.Else():
                    all_tiles(False)

            def part(b, k, h):
                cols = slice(512 * h, 512 * h + 512)
                o = ps[:, DN + h, :]
                pe.matmul(o, het_hi[:, b, k, :], pr_hi[:, k, cols], start=(k == 0), stop=False)
                pe.matmul(o, het_hi[:, b, k, :], pr_lo[:, k, cols], start=False, stop=False)
                return pe.matmul(o, het_lo[:, b, k, :], pr_hi[:, k, cols], start=False, stop=(k == FT - 1))

            def down_halves(turn, before):
                pe.wait_ge(y0_done, ONE + before)
                pe.wait_ge(y1_done, ONE + before)
                for h in range(2):
                    for k in range(FT):
                        if h == 0:
                            pair(turn, k)
                        last = part(0, k, h)
                    last.then_inc(d1_done if h else d0_done, 1)

            def down_tiles(b, turn, before, ks):
                if ks[0] == 0:
                    pe.wait_ge(y0_done, ONE + before)
                    pe.wait_ge(y1_done, ONE + before)
                for k in ks:
                    if b == 0:
                        pair(turn, k)
                    last = part(b, k, 0)
                    if k == FT - 1:
                        last.then_inc(d0_done, 1)
                    part(b, k, 1).then_inc(pr_used, 1)

            def turn_he(b, made, xs):
                pe.wait_ge(he_done, ONE + made)
                pe.wait_ge(xtl_done, xs)
                for k in range(FT):
                    last = pe.transpose(ps[:, TR + b, P * k:P * k + P], he[:, b, bass.ds(k, P, step=FT)], ident[:, :])
                last.then_inc(he_tr, 1)

            w = Step(pe, 0)
            turn_x(0, 0, 0, 1)
            with pe.If(w.h > 0):
                turn_x(1, 1, 0, 1)
            gate_up(0, w.c, w.cn, w.h, 5)
            turn_x(0, w.cn, 0, 2)
            with pe.If(w.hn > 0):
                turn_x(1, w.cn + 1, 0, w.h + 1)
            turn_he(0, 1, w.cn + 1 + w.hn)
            with pe.If(w.h > 0):
                turn_he(1, 2, w.cn + 1 + w.hn)
            with pe.Fori(1, NST) as s:
                with pe.If(s < st):
                    w = Step(pe, s)
                    more = s + 1 < st
                    gate_up(3 * s, w.c, w.cn, w.h, 1)
                    with pe.If(more):
                        turn_x(0, w.cn, w.c, s + 2)
                    with pe.Else():
                        pe.wait_ge(tables, 1)
                    pe.wait_ge(hetl_done, w.c)
                    with pe.If(w.hp > 0):
                        down_halves(3 * s + 2, w.cp)
                        with pe.If(w.hn > 0):
                            turn_x(1, w.cn + 1, w.c, w.nbn + 1)
                        down_tiles(1, 3 * s + 2, w.cp + 1, (0, 1, 2, 3))
                    with pe.Else():
                        down_tiles(0, 3 * s + 2, w.cp, (0, 1))
                        with pe.If(w.hn > 0):
                            turn_x(1, w.cn + 1, w.c, w.nbn + 1)
                        down_tiles(0, 3 * s + 2, w.cp, (2, 3))
                    xs = w.cn + w.hn + more
                    turn_he(0, w.c + 1, xs)
                    with pe.If(w.h > 0):
                        turn_he(1, w.c + 2, xs)
                    pe.wait_ge(tables, 1)
                pe.wait_ge(tables, 1)
            w = Step(pe, last_st)
            pe.wait_ge(hetl_done, w.cn)
            with pe.If(w.h > 0):
                down_halves(3 * st, w.c)
                down_tiles(1, 3 * st, w.c + 1, (0, 1, 2, 3))
            with pe.Else():
                down_tiles(0, 3 * st, w.c, (0, 1, 2, 3))


def kernel(**inputs):
    import numpy as _np
    import concourse.bacc as _bacc
    from concourse import mybir as _mybir
    from concourse.bass_utils import run_bass_kernel_spmd as _run

    a = {n: _np.ascontiguousarray(v) for n, v in inputs.items()}
    laid = {
        "x": a["x"], "c": a["c"], "w_ada": a["w_ada"], "b_ada": a["b_ada"],
        "g_mix_pre": a["g_mix_pre"], "g_mix_post": a["g_mix_post"],
        "g_ffn_pre": a["g_ffn_pre"], "g_ffn_post": a["g_ffn_post"],
        "w_in": a["conv_w_in"][0].reshape(P, KT, 2, NQ, CQ).transpose(3, 0, 1, 2, 4).reshape(NQ, P, KT * 2 * CQ),
        "b_in": a["conv_b_in"][0].reshape(2, NQ, CQ).transpose(1, 0, 2).reshape(NQ, 2 * CQ),
        "w_dw": a["conv_w_dw"][0][::-1].reshape(TAPS, NQ, QG, GC).transpose(1, 3, 2, 0),
        "b_dw": a["conv_b_dw"], "ln_g": a["conv_ln_g"], "ln_b": a["conv_ln_b"],
        "w_out": a["conv_w_out"], "b_out": a["conv_b_out"],
        "router_w": a["router_w"], "router_b": a["router_b"],
        "w_gate": a["exp_w_gate"], "w_up": a["exp_w_up"], "w_down": a["exp_w_down"],
    }
    nc = _bacc.Bacc("TRN2", target_bir_lowering=False, num_devices=1, dynamic_dma_scratch_size=8192)
    arrays, args = {}, []
    for name, v in laid.items():
        v = _np.ascontiguousarray(v)
        arrays[f"in_{name}"] = v
        args.append(nc.dram_tensor(f"in_{name}", v.shape, _mybir.dt.from_np(v.dtype), kind="ExternalInput").ap())
    args.append(nc.dram_tensor("out_0", (1, S, D), F32, kind="ExternalOutput").ap())
    dit_layer(nc, *args)
    r = _run(nc, [arrays], core_ids=[0])
    return r.results[0]["out_0"]
```

```python
from contextlib import ExitStack

import concourse.bass as bass
from concourse import mybir

F32 = mybir.dt.float32
F32R = mybir.dt.float32r
I32 = mybir.dt.int32
U32 = mybir.dt.uint32
ALU = mybir.AluOpType
ACT = mybir.ActivationFunctionType
AX_X = mybir.AxisListType.X

P = 128
D = 1024
S = 1024
NT = S // P
KT = D // P
F = 512
FT = F // P
NE = 16
NG = 4
EG = NE // NG
EPS = 1e-6

NQ = 4
CQ = D // NQ
TAPS = 31
GC = 16
QG = CQ // GC
BG = 4
QB = QG // BG
CG = 2
QH = QG // CG
ND = 5
NM = ND * NT
PAD = 2
MSLOTS = 4

ST_ROWS = 2 * P
NST = 23
NSTC = NST + 1
CHUNKS = 6
FB = 4
RING = 4
KB = 1024
ONE = 1
ONE_DMA = 16
DVE_RESIDUAL = (0, 3, 6, 7)


def dit_layer(nc, x, c, w_ada, b_ada, g_mix_pre, g_mix_post, g_ffn_pre, g_ffn_post,
              w_in, b_in, w_dw, b_dw, ln_g, ln_b, w_out, b_out, router_w, router_b,
              w_gate, w_up, w_down, out):
    ctx = ExitStack()
    with ctx:
        def sem(name):
            return ctx.enter_context(nc.semaphore(name))

        limit = nc.sbuf_top
        base = (nc.sbuf_base + 31) // 32 * 32
        arena = ctx.enter_context(nc.sbuf_tensor("arena", [P, (limit - base - 64) // 4], F32))
        R0, R1, R2 = base, base + 96 * KB, base + 128 * KB
        top = [R2 + 84736]

        def at(name, shape, dt, offset):
            return nc.alloc_sbuf_tensor_at(name, shape, dt, offset=offset)

        def small(name, shape, dt=F32):
            n = 4
            for d in shape[1:]:
                n *= d
            t = at(name, shape, dt, top[0])
            top[0] += (n + 31) // 32 * 32
            assert top[0] <= limit, (name, top[0], limit)
            return t

        ada_first = at("ada_first", [P, KT, 2 * D], F32, R0)
        sp_hi = at("sp_hi", [P, KT, D], F32R, R0)
        sp_lo = at("sp_lo", [P, KT, D], F32R, R0 + 32 * KB)
        xv = at("xv", [P, NT, D], F32, R0 + 64 * KB)
        raw_gu = at("raw_gu", [P, 2, 2, KT, F], F32, R0)
        raw_d = at("raw_d", [P, 2, FT, D], F32, R0 + 64 * KB)
        wi_hi = at("wi_hi", [P, KT, 2 * CQ], F32R, R1)
        wi_lo = at("wi_lo", [P, KT, 2 * CQ], F32R, R1 + 16 * KB)
        x1 = at("x1", [P, NT, D], F32, R1)
        off = [R2]

        def seq(name, shape, dt):
            n = 4
            for d in shape[1:]:
                n *= d
            t = at(name, shape, dt, off[0])
            off[0] += (n + 31) // 32 * 32
            return t

        stage = seq("stage", [P, 2, 4096 // 2], F32)
        mx = seq("mx", [P, MSLOTS, ND, 2, P], F32R)
        u = seq("u", [P, QG, NT * GC], F32)
        ut_hi = seq("ut_hi", [P, 2, BG, P + 2 * PAD], F32R)
        ut_lo = seq("ut_lo", [P, 2, BG, P + 2 * PAD], F32R)
        taps_raw = seq("taps_raw", [P, QG, NM], F32)
        taps_hi = seq("taps_hi", [P, QG, NM], F32R)
        taps_lo = seq("taps_lo", [P, QG, NM], F32R)
        bin_row = seq("bin_row", [P, 2 * CQ], F32)
        bdw_row = seq("bdw_row", [P, CQ], F32)
        acc = seq("acc", [P, D], F32)
        ada_stage = seq("ada_stage", [P, 2, D], F32)
        pre = seq("pre", [P, 2, 2 * CQ], F32)
        junk = seq("junk", [P, D], F32)
        assert off[0] <= top[0]
        mod_row = at("mod_row", [P, 3, D], F32, R2 + 16 * KB)
        acc01 = at("acc01", [P, 2, D], F32, R2 + 36 * KB)
        off = [R2 + 16 * KB]
        s_full = seq("s_full", [P, KT, P], F32)
        s_hi = seq("s_hi", [P, 2, KT, P], F32R)
        s_lo = seq("s_lo", [P, 2, KT, P], F32R)
        zb = seq("zb", [P, D], F32)
        yb = seq("yb", [P, 2, D], F32)
        xr = seq("xr", [P, 2, D], F32)
        h2 = seq("h2", [P, 2, D], F32)
        bout_row = seq("bout_row", [P, D], F32)
        rows = seq("rows", [P, 3, D], F32)
        diag = at("diag", [P, 4, P, KT], F32, R1 + 16 * KB)
        junk2 = at("junk2", [P, D], F32, R2 + 12 * KB)
        h2t = at("h2t", [P, KT, P], F32, R2 + 8 * KB)
        assert off[0] <= top[0], (off[0], top[0])

        ident = small("ident", [P, P])
        col = small("col", [P, 8, KT])
        bada = small("bada", [P, 6, KT])
        modc = small("modc", [P, 4, KT])
        silc = small("silc", [P, 2, KT])
        eye16 = small("eye16", [P, GC])
        ones = small("ones", [P, P])
        nhalf = small("nhalf", [P, 8])
        epsc = small("epsc", [P, 1])
        gap = small("gap", [P, 1])
        zero_i = small("zero_i", [P, 1], I32)
        gap_p = small("gap_p", [P, 1])
        ssx = small("ssx", [P, NT])
        rsx = small("rsx", [P, NT])
        tmp8 = small("tmp8", [P, NT])
        stats = small("stats", [P, NT, 2, 6])
        mv = small("mv", [P, NT, 2])
        lnr = small("lnr", [P, 2, NT])
        sy = small("sy", [P, 2, 3])
        sx = small("sx", [P, 2, 3])
        vcol = small("vcol", [P, 3, KT])
        rwt = small("rwt", [P, KT, NE])
        rb_row = small("rb_row", [P, NE])
        logits = small("logits", [P, NT, NE])

        gates = small("gates", [P, 2, NT])
        words = small("words", [P, NSTC], I32)
        counts = small("counts", [P, 2], I32)
        ct_i = small("ct_i", [P, NE], I32)
        dest = small("dest", [P, 2 * NSTC], I32)
        src = small("src", [P, 2 * NSTC + 2], I32)
        ic = small("ic", [P, 4], I32)

        off = [R2 + 80 * KB]
        ones_r = seq("ones_r", [P, P], F32R)
        tri = seq("tri", [P, P], F32R)
        iota = seq("iota", [P, P], F32)
        le16 = seq("le16", [P, NE, NE], F32)
        lt4 = seq("lt4", [P, EG, EG], F32)
        desc4 = seq("desc4", [P, NG], F32)
        tok1 = seq("tok1", [P, 2 * NT], F32)
        assert off[0] <= R2 + 84736
        off = [R2 + 40 * KB]
        aff = seq("aff", [P, NT, NE], F32)
        sel = seq("sel", [P, NT, NE], F32)
        pair_max = seq("pair_max", [P, NT * NG, 2], F32)
        pair_min = seq("pair_min", [P, NT * NG, 2], F32)
        gs = seq("gs", [P, 6, NT, NG], F32)
        gmax = seq("gmax", [P, 2, NT], F32)
        beats = seq("beats", [P, 2, NT, EG, EG], F32)
        of4 = seq("of4", [P, NT, NG, EG], F32)
        four = seq("four", [P, NT, EG], F32)
        is_k = seq("is_k", [P, 2, NT, EG], F32)
        rank = seq("rank", [P, NT, EG], F32)
        mk = seq("mk", [P, 2, NT, NE], F32)
        m9 = seq("m9", [P, NT + 1, NE], F32R)
        prod = seq("prod", [P, 2 * NT, NE], F32)
        ak = seq("ak", [P, 2, NT], F32)
        den = seq("den", [P, 2, NT], F32)
        pos = seq("pos", [P, NT, NE], F32)
        cnt = seq("cnt", [P, 6, NE], F32)
        prod16 = seq("prod16", [P, NE, NE], F32)
        slot = seq("slot", [P, 2 * NT], F32)
        slot_i = seq("slot_i", [P, 3, 2 * NT], I32)
        slot_f = seq("slot_f", [P, 2, 2 * NT], F32)
        st_le = seq("st_le", [P, NSTC, NE], F32)
        st_in = seq("st_in", [P, NSTC, NE], F32)
        st_ab = seq("st_ab", [P, NSTC, NE], F32)
        start = seq("start", [P, 2, NSTC], F32)
        e_of = seq("e_of", [P, NSTC + 2], F32)
        hb_of = seq("hb_of", [P, 2, 16 + NSTC + 1], F32)
        word_f = seq("word_f", [P, 2, NSTC], F32)
        oh_p = seq("oh_p", [P, 2 * NT, P], F32R)
        oh_t = seq("oh_t", [P, 2 * NT, 2 * NSTC], F32R)
        assert off[0] <= R2 + 76 * KB, off[0] - R2

        off = [R2]
        pr_hi = seq("pr_hi", [P, RING, D], F32R)
        pr_lo = seq("pr_lo", [P, RING, D], F32R)
        xg = seq("xg", [P, 2, D], F32)
        xt_hi = seq("xt_hi", [P, 2, KT, P], F32R)
        xt_lo = seq("xt_lo", [P, 2, KT, P], F32R)
        he = seq("he", [P, 2, F], F32)
        het_hi = seq("het_hi", [P, 2, FT, P], F32R)
        het_lo = seq("het_lo", [P, 2, FT, P], F32R)
        ys = seq("ys", [P, 2, D], F32)
        assert off[0] <= R2 + 80 * KB
        y_all = at("y_all", [P, 2, NT, D], F32, R0)
        g3 = at("g3", [P, D], F32, R0 + 64 * KB)
        fb = at("fb", [P, FB, D], F32, R0 + 68 * KB)
        junk3 = at("junk3", [P, D], F32, R0 + (68 + 4 * FB) * KB)
        sf = small("sf", [P, 3, NT])

        h2_rows = nc.dram_tensor("h2_rows", [S, D], F32).ap()
        y_rows = nc.dram_tensor("y_rows", [2 * S, D], F32).ap()
        first_rows = nc.dram_tensor("first_rows", [2, P], F32).ap()
        g3_rows = nc.dram_tensor("g3_rows", [P, D], F32).ap()

        ps = ctx.enter_context(nc.psum_tensor("ps", [P, 8, 512], F32))

        cols_loaded = sem("cols_loaded")
        x_loaded = [sem(f"x_loaded{j}") for j in range(4)]
        ada1_loaded = [sem(f"ada1_loaded{j}") for j in range(5)]
        stage_loaded = [sem(f"stage_loaded{j}") for j in range(2)]
        taps_loaded = sem("taps_loaded")
        brow_loaded = sem("brow_loaded")
        bdw_loaded = sem("bdw_loaded")
        ada_loaded = [sem(f"ada_loaded{j}") for j in range(2)]
        const_made = sem("const_made")
        eye_made = sem("eye_made")
        sigc_done = sem("sigc_done")
        silc_done = sem("silc_done")
        ssx_done = sem("ssx_done")
        pool_chain = sem("pool_chain")
        rsx_done = sem("rsx_done")
        xn_done = sem("xn_done")
        brow1_loaded = sem("brow1_loaded")
        bias_done = sem("bias_done")
        acc1_done = sem("acc1_done")
        ada1_mod = sem("ada1_mod")
        mod1_done = sem("mod1_done")
        shift_row = sem("shift_row")
        xt_done = sem("xt_done")
        hs_done = sem("hs_done")
        hhi_done = sem("hhi_done")
        hlo_done = sem("hlo_done")
        wi_hi_done = sem("wi_hi_done")
        wi_lo_done = sem("wi_lo_done")
        wi_used = sem("wi_used")
        win_tile = sem("win_tile")
        pre_done = sem("pre_done")
        sig_done = sem("sig_done")
        u_done = sem("u_done")
        acc_done = sem("acc_done")
        acc_col = sem("acc_col")
        modc_done = sem("modc_done")
        taps_split = sem("taps_split")
        mhi_done = sem("mhi_done")
        mlo_done = sem("mlo_done")
        ut_tr = sem("ut_tr")
        uthi_done = sem("uthi_done")
        utlo_done = sem("utlo_done")
        conv_done = sem("conv_done")
        vb_done = sem("vb_done")
        v_done = sem("v_done")
        wo_hi_done = sem("wo_hi_done")
        wo_lo_done = [sem(f"wo_lo_done{j}") for j in range(2)]
        xr_loaded = [sem(f"xr_loaded{j}") for j in range(2)]
        bout_loaded = sem("bout_loaded")
        rw_loaded = sem("rw_loaded")
        vcol_done = sem("vcol_done")
        diag_done = sem("diag_done")
        brow_tr = sem("brow_tr")
        rows_done = sem("rows_done")
        g3_stored = sem("g3_stored")
        stats_done = sem("stats_done")
        mv_done = sem("mv_done")
        lnr_done = sem("lnr_done")
        lnv_done = sem("lnv_done")
        sym_done = sem("sym_done")
        sxm_done = sem("sxm_done")
        z_done = sem("z_done")
        zt_done = sem("zt_done")
        s_done = sem("s_done")
        sh_done = sem("sh_done")
        sl_done = sem("sl_done")
        yh_done = sem("yh_done")
        yb_done = sem("yb_done")
        sqy_done = sem("sqy_done")
        ry_done = sem("ry_done")
        t_done = sem("t_done")
        x1_done = sem("x1_done")
        sqx_done = sem("sqx_done")
        rx_done = sem("rx_done")
        hg_done = sem("hg_done")
        h2_done = sem("h2_done")
        h2_stored = [sem(f"h2_stored{j}") for j in range(2)]
        h2_tr = sem("h2_tr")
        h2t_done = sem("h2t_done")
        rt_done = sem("rt_done")
        log_done = sem("log_done")

        rconst = sem("rconst")
        aff_done = sem("aff_done")
        route_chain = sem("route_chain")
        pos_done = sem("pos_done")
        slots_done = sem("slots_done")
        src_made = sem("src_made")
        tables = sem("tables")
        raw_loaded = [[sem(f"raw_loaded{b}{j}") for j in range(CHUNKS)] for b in range(2)]
        ic_done = [sem(f"ic_done{j}") for j in range(4)]
        gath = [sem(f"gath{j}") for j in range(2)]
        scat = [sem(f"scat{j}") for j in range(2)]
        all_scattered = sem("all_scattered")
        xt_tr = sem("xt_tr")
        xth_done = sem("xth_done")
        xtl_done = sem("xtl_done")
        pr_hi_done = sem("pr_hi_done")
        pr_lo_dve = sem("pr_lo_dve")
        pr_lo_pool = sem("pr_lo_pool")
        pr_used = sem("pr_used")
        sil_done = sem("sil_done")
        he_done = sem("he_done")
        he_tr = sem("he_tr")
        heth_done = sem("heth_done")
        hetl_done = sem("hetl_done")
        d0_done = sem("d0_done")
        d1_done = sem("d1_done")
        y0_done = sem("y0_done")
        y1_done = sem("y1_done")
        yl = [sem(f"yl{j}") for j in range(4)]
        g3_loaded = sem("g3_loaded")
        fa_done = sem("fa_done")
        f_done = sem("f_done")
        sqf_done = sem("sqf_done")
        sfm_done = sem("sfm_done")
        rf_done = sem("rf_done")
        fg_done = sem("fg_done")
        o_done = [sem(f"o_done{j}") for j in range(2)]

        def out_of(i):
            by_dve = i in DVE_RESIDUAL
            return o_done[by_dve], len([j for j in range(i + 1) if (j in DVE_RESIDUAL) == by_dve])

        stored = sem("stored")

        block = ctx.enter_context(nc.Block())

        class Step:
            def __init__(self, eng, s):
                w = eng.value_load(words[0:1, bass.ds(s, 1)], min_val=0, max_val=(1 << 23) - 1)
                self.s = s
                self.ep, self.e, self.en = w & 31, (w >> 5) & 31, (w >> 10) & 31
                self.hp, self.h, self.hn = (w >> 15) & 1, (w >> 16) & 1, (w >> 17) & 1
                self.nbp = w >> 18
                self.nb = self.nbp + self.hp
                self.nbn = self.nb + self.h
                self.c = self.nb + s
                self.cn = self.c + self.h + 1
                if not (type(s) is int and s == 0):
                    self.cp = self.nbp + (s - 1)

        marks = {}
        WI = (0, 1, 2)
        UT = (3, 4)
        CV = (5, 6)
        MODB = 7
        DN, TR = 4, 6
        PZ, PY, PH, PR = 0, 2, 4, 6

        x_t = x.rearrange("b (a i) d -> (b a) i d", i=NT)
        w_ada_t = w_ada.rearrange("l (p k) n -> (l p) k n", k=KT)
        w_out_t = w_out.rearrange("l (p k) n -> (l p) k n", k=KT)

        @block.sync
        def _(sp):
            cols = ((c.rearrange("b n -> (b n)"), 0), (g_mix_pre.rearrange("b n -> (b n)"), 1),
                    (g_mix_post.rearrange("b n -> (b n)"), 2), (g_ffn_pre.rearrange("b n -> (b n)"), 3),
                    (g_ffn_post.rearrange("b n -> (b n)"), 4), (ln_g.rearrange("b n -> (b n)"), 5),
                    (ln_b.rearrange("b n -> (b n)"), 6))
            for src, j in cols:
                sp.dma_start(col[:, j, :], src.rearrange("(p k) -> p k", k=KT)).then_inc(cols_loaded, 16)
            sp.dma_start(bada[:, :, :], b_ada.rearrange("l (s p k) -> (l p) s k", s=6, k=KT)).then_inc(cols_loaded, 16)

            def load_x(j):
                sp.dma_start(xv[:, 2 * j:2 * j + 2, :], x_t[:, 2 * j:2 * j + 2, :]).then_inc(x_loaded[j], 16)

            def load_win(q, h):
                sp.dma_start(stage[:, h, :],
                             w_in[bass.ds(q, 1), :, 2048 * h:2048 * h + 2048].rearrange("q p n -> (q p) n")
                             ).then_inc(stage_loaded[h], 16)

            def load_taps(q):
                for i in range(NT):
                    sp.dma_start(taps_raw[GC * i:GC * i + GC, :, i + 1:i + 1 + TAPS],
                                 w_dw[bass.ds(q, 1)].rearrange("q c g t -> (q c) g t")).then_inc(taps_loaded, 16)

            load_x(0)
            for j in range(4):
                if j < 3:
                    sp.dma_start(ada_first[:, 2 * j:2 * j + 2, :],
                                 w_ada_t[:, 2 * j:2 * j + 2, 0:2 * D]).then_inc(ada1_loaded[j], 16)
                    load_x(j + 1)
                else:
                    for k in (KT - 2, KT - 1):
                        sp.dma_start(ada_first[:, k, :], w_ada_t[:, k, 0:2 * D]).then_inc(ada1_loaded[k - 3], 16)
                if j == 0:
                    sp.dma_start(mod_row[0:1, 0:2, :].rearrange("p s d -> p (s d)"),
                                 b_ada[0:1, 0:2 * D]).then_inc(brow1_loaded, 16)
                    sp.dma_start(mod_row[:, 2, :], g_mix_pre[0:1, :].partition_broadcast(P)).then_inc(brow1_loaded, 16)
            load_win(0, 0)
            load_win(0, 1)
            sp.dma_start(rwt[:, :, :], router_w.rearrange("(p k) e -> p k e", k=KT)).then_inc(rw_loaded, 16)
            sp.dma_start(rb_row[:, :], router_b.rearrange("(b n) -> b n", b=1).partition_broadcast(P)).then_inc(rw_loaded, 16)
            sp.wait_ge(const_made, 6)
            load_taps(0)

            def quarter(q, last):
                for h in range(2):
                    sp.wait_ge(wi_lo_done, 4 * q + (2 * h + 2))
                    if last:
                        sp.dma_start(stage[:, h, :].rearrange("p (k n) -> p k n", k=2), w_out_t[:, 2 * h:2 * h + 2, :]).then_inc(stage_loaded[h], 16)
                    else:
                        load_win(q + 1, h)
                for k in range(KT):
                    if k >= 2:
                        sp.wait_ge(acc_done, 8 * q + (ONE + k - 1))
                    else:
                        sp.wait_ge(acc_done, ONE + 8 * q)
                    sp.dma_start(ada_stage[:, k % 2, :],
                                 w_ada_t[:, k, bass.ds((q + 2) * D, D)]).then_inc(ada_loaded[k % 2], 16)
                if not last:
                    sp.wait_ge(taps_split, 2 * q + 2)
                    load_taps(q + 1)

            with sp.Fori(0, NQ - 1) as q:
                quarter(q, False)
            quarter(NQ - 1, True)
            for h in range(2):
                sp.wait_ge(wo_lo_done[h], 2)
                sp.dma_start(stage[:, h, :].rearrange("p (k n) -> p k n", k=2),
                             w_out_t[:, 4 + 2 * h:6 + 2 * h, :]).then_inc(stage_loaded[h], 16)
            sp.wait_ge(v_done, ONE + NQ * QH)
            sp.dma_start(bout_row[:, :], b_out[0:1, :].partition_broadcast(P)).then_inc(bout_loaded, 16)

            h2_out = h2_rows.rearrange("(a i) d -> a i d", i=NT)

            def load_xr(i, b, first):
                if not first:
                    sp.wait_ge(x1_done, i - 1)
                sp.dma_start(xr[:, b, :], x_t[:, bass.ds(i, 1), :]).then_inc(xr_loaded[b], 16)

            def store_h2(i, b):
                sp.wait_ge(h2_done, i + 1)
                sp.dma_start(h2_out[:, bass.ds(i, 1), :], h2[:, b, :]).then_inc(h2_stored[b], 16)

            load_xr(0, 0, True)
            load_xr(1, 1, True)
            sp.wait_ge(rows_done, 4)
            sp.dma_start(g3_rows, h2[:, 0, :]).then_inc(g3_stored, 16)
            with sp.Fori(0, NT // 2 - 1) as t:
                for b in range(2):
                    load_xr(2 * t + 2 + b, b, False)
                    store_h2(2 * t + b, b)

            def load_down(b, h, one):
                ks = slice(FT // 2 * h, FT // 2 * (h + 1))
                sp.dma_start(raw_d[:, b, ks, :], w_down[0, one].rearrange("e (p k) n -> (e p) k n", k=FT)[:, ks, :]
                             ).then_inc(raw_loaded[b][4 + h], 16)

            for b, h in ((0, 0), (0, 1), (1, 0)):
                sp.wait_ge(z_done, 4 * b + 2 * h + 2)
                load_down(b, h, bass.ds(b, 1))
            store_h2(NT - 2, 0)
            sp.wait_ge(z_done, NT)
            load_down(1, 1, bass.ds(1, 1))
            store_h2(NT - 1, 1)
            sp.wait_ge(yh_done, 2 * NT)

            def load_gate_up(t, b, ct):
                one = bass.ds(2 * t + b, 1)
                for j in range(4):
                    if ct is not None and j in (0, 2):
                        sp.wait_ge(pr_used, 12 * ct + (4 + 2 * j))
                    if ct is not None and j == 1:
                        sp.wait_ge(raw_loaded[b][5], ONE_DMA * b + 16 * t)
                    if ct is None and j == 1 and b == 1:
                        sp.wait_ge(raw_loaded[0][3], 16)
                    if j == 3 or (j == 2 and ct is None):
                        sp.wait_ge(raw_loaded[b][j - 2], ONE_DMA * b + 16 * t + 16)
                    src_w = (w_gate, w_up)[j % 2]
                    ks = slice(4 * (j // 2), 4 * (j // 2) + 4)
                    sp.dma_start(raw_gu[:, b, j % 2, ks, :],
                                 src_w[0, one].rearrange("e (p k) n -> (e p) k n", k=KT)[:, ks, :]
                                 ).then_inc(raw_loaded[b][j], 16)

            def load_down_after(t, b, ct, tg, bg):
                for h in range(2):
                    if h == 0:
                        sp.wait_ge(pr_used, 12 * ct + 24)
                    elif tg is not None:
                        sp.wait_ge(raw_loaded[bg][3], ONE_DMA * bg + 16 * tg + 16)
                    load_down(b, h, bass.ds(2 * t + b, 1))

            def ct_of(e):
                return sp.value_load(ct_i[0:1, bass.ds(e, 1)], min_val=0, max_val=NST - 1)

            load_gate_up(0, 0, None)
            load_gate_up(0, 1, None)
            sp.wait_ge(tables, 1)
            load_gate_up(1, 0, ct_of(0))
            with sp.Fori(1, NE // 2 - 1) as t:
                odd = ct_of(2 * t - 1)
                load_gate_up(t, 1, odd)
                load_down_after(t, 0, ct_of(2 * t - 2), t, 1)
                load_gate_up(t + 1, 0, ct_of(2 * t))
                load_down_after(t, 1, odd, t + 1, 0)
            t = NE // 2 - 1
            odd = ct_of(2 * t - 1)
            load_gate_up(t, 1, odd)
            load_down_after(t, 0, ct_of(2 * t - 2), t, 1)
            load_down_after(t, 1, odd, None, None)

            last_st = sp.value_load(counts[0:1, 0:1], min_val=0, max_val=NST - 1)
            st = last_st + 1
            sp.wait_ge(pr_used, 12 * st + 4)
            sp.dma_start(g3[:, :], g3_rows).then_inc(g3_loaded, 16)
            sp.wait_ge(all_scattered, 1)
            y_in = y_rows.rearrange("(k a i) d -> a k i d", k=2, i=NT)
            for j in range(4):
                for k in range(2):
                    sp.dma_start(y_all[:, k, 2 * j:2 * j + 2, :], y_in[:, k, 2 * j:2 * j + 2, :]).then_inc(yl[j], 16)
            out_t = out.rearrange("b (a i) d -> (b a) i d", i=NT)
            for i in range(NT):
                made, n_made = out_of(i)
                sp.wait_ge(made, n_made)
                sp.dma_start(out_t[:, i, :], x1[:, i, :]).then_inc(stored, 16)
            sp.wait_ge(h2_stored[0], ONE_DMA + 16 * (NT // 2))
            sp.wait_ge(h2_stored[1], ONE_DMA + 16 * (NT // 2))
            sp.wait_ge(stored, 16 * NT)

        @block.gpsimd
        def _(pool):
            for s_ in (acc_col, acc_done, conv_done, h2_tr, h2t_done, he_done, log_done, mlo_done, modc_done, rt_done, u_done, ut_tr, v_done, y0_done, y1_done):
                pool.sem_inc(s_, ONE)
            for s_ in h2_stored + raw_loaded[1]:
                pool.sem_inc(s_, ONE_DMA)
            pool.memset(ident[:, :], 0.0).then_inc(pool_chain, 1)
            pool.memset(eye16[:, :], 0.0).then_inc(pool_chain, 1)
            pool.memset(epsc[:, :], EPS).then_inc(pool_chain, 1)
            pool.memset(zero_i[:, :], 0).then_inc(pool_chain, 1)
            pool.memset(ones[:, :], 1.0).then_inc(const_made, 1)
            pool.memset(nhalf[:, :], -0.5).then_inc(const_made, 1)
            pool.memset(taps_raw[:, :, :], 0.0).then_inc(const_made, 1)
            pool.memset(ut_hi[:, :, :, :].bitcast(F32), 0.0).then_inc(const_made, 1)
            pool.memset(ut_lo[:, :, :, :].bitcast(F32), 0.0).then_inc(const_made, 1)
            pool.wait_ge(pool_chain, 4)
            pool.affine_select(out=ident[:, :], in_=ident[:, :], compare_op=ALU.not_equal, fill=1.0, base=0,
                               pattern=[[-1, P]], channel_multiplier=1).then_inc(const_made, 1)
            pool.wait_ge(const_made, 6)
            for b in range(2):
                pool.dma_start(first_rows[b:b + 1, :], ones[0:1, :]).then_inc(scat[b], 16)
            for i in range(NT):
                pool.affine_select(out=eye16[:, :], in_=eye16[:, :], compare_op=ALU.not_equal, fill=1.0,
                                   base=-GC * i, pattern=[[-1, GC]], channel_multiplier=1).then_inc(eye_made, 1)
                pool.wait_ge(eye_made, i + 1)
            pool.dma_start(bin_row[:, :], b_in[0:1, :].partition_broadcast(P)).then_inc(brow_loaded, 16)
            pool.dma_start(bdw_row[:, :], b_dw[0:1, 0:CQ].partition_broadcast(P)).then_inc(bdw_loaded, 16)
            pool.wait_ge(const_made, 6)

            def inv_rms(j):
                two = slice(2 * j, 2 * j + 2)
                pool.wait_ge(ssx_done, 2 * j + 2)
                pool.tensor_scalar(tmp8[:, two], ssx[:, two], 1.0 / D, EPS, ALU.mult, ALU.add).then_inc(pool_chain, 1)
                pool.wait_ge(pool_chain, 5 + j)
                pool.tensor_tensor(rsx[:, two], tmp8[:, two], nhalf[:, 0:2], ALU.pow).then_inc(rsx_done, 1)

            for j in range(NT // 2):
                inv_rms(j)
            pool.wait_ge(shift_row, 1)
            pool.wait_ge(hs_done, 1)
            for i in range(1, NT):
                pool.wait_ge(xn_done, i + 1)
                pool.tensor_tensor(xv[:, i, :], xv[:, i, :], mod_row[:, 0, :], ALU.add).then_inc(hs_done, 1)
            pool.wait_ge(hlo_done, NT)

            def make_m(q, g):
                if g < MSLOTS:
                    pool.wait_ge(conv_done, ONE + QG * q)
                else:
                    pool.wait_ge(conv_done, QG * q + (ONE + g - MSLOTS + 1))
                pool.tensor_tensor(mx[:, g % MSLOTS, :, 0, :].rearrange("p d (i c) -> p d i c", i=NT),
                                   taps_hi[:, g, :].bitcast(F32).rearrange("p (d i) -> p d i", d=ND).unsqueeze(3)
                                   .to_broadcast([P, ND, NT, GC]),
                                   eye16[:, :].unsqueeze(1).unsqueeze(1).to_broadcast([P, ND, NT, GC]),
                                   ALU.mult).then_inc(mhi_done, 1)

            def quarter(q, last):
                pool.wait_ge(taps_loaded, 128 * q + 128)
                pool.wait_ge(mlo_done, ONE + QG * q)
                pool.tensor_tensor(taps_hi[:, :, :], taps_raw[:, :, :], ones[:, 0:1].unsqueeze(1).to_broadcast([P, QG, NM]),
                                   ALU.mult).then_inc(taps_split, 1)
                pool.wait_ge(taps_split, 2 * q + 1)
                pool.tensor_tensor(taps_lo[:, :, :], taps_raw[:, :, :], taps_hi[:, :, :].bitcast(F32),
                                   ALU.subtract).then_inc(taps_split, 1)
                for g in range(QG):
                    make_m(q, g)
                    if g == 8 and not last:
                        pool.wait_ge(pre_done, 8 * q + 8)
                        pool.dma_start(bin_row[:, :],
                                       b_in[bass.ds(q + 1, 1), :].partition_broadcast(P)).then_inc(brow_loaded, 16)
                if not last:
                    pool.wait_ge(v_done, QH * q + (ONE + QH))
                    pool.dma_start(bdw_row[:, :],
                                   b_dw[0:1, bass.ds((q + 1) * CQ, CQ)].partition_broadcast(P)).then_inc(bdw_loaded, 16)

            with pool.Fori(0, NQ - 1) as q:
                quarter(q, False)
            quarter(NQ - 1, True)

            def split_wout(k):
                pool.wait_ge(wo_hi_done, k + 1)
                pool.tensor_tensor(sp_lo[:, k, :], stage[:, 1, 1024 * (k % 2):1024 * (k % 2) + 1024],
                                   sp_hi[:, k, :].bitcast(F32), ALU.subtract).then_inc(wo_lo_done[1], 1)

            def diagonal(j):
                if j == 0:
                    pool.wait_ge(win_tile, NQ * NT)
                    pool.wait_ge(modc_done, ONE + NQ)
                    pool.wait_ge(vcol_done, 3)
                cc = (vcol[:, 0, :], vcol[:, 1, :], modc[:, 1, :], vcol[:, 2, :])[j]
                pool.tensor_tensor(diag[:, j], ident[:, :].unsqueeze(2).to_broadcast([P, P, KT]),
                                   cc.unsqueeze(1).to_broadcast([P, P, KT]), ALU.mult).then_inc(diag_done, 1)

            split_wout(2)
            split_wout(3)
            diagonal(0)
            diagonal(1)
            for j, ts_ in enumerate((slice(0, 1), slice(1, NT))):
                if j == 1:
                    diagonal(2)
                    diagonal(3)
                    split_wout(6)
                    split_wout(7)
                pool.wait_ge(mv_done, (1, NT)[j])
                pool.tensor_tensor(lnr[:, 0, ts_], mv[:, ts_, 1], epsc[:, :].to_broadcast([P, ts_.stop - ts_.start]),
                                   ALU.add).then_inc(lnv_done, 1)
                pool.wait_ge(lnv_done, j + 1)
                pool.tensor_tensor(lnr[:, 1, ts_], lnr[:, 0, ts_], nhalf[:, 0:ts_.stop - ts_.start],
                                   ALU.pow).then_inc(lnr_done, 1)

            def factor(i, b, s3, summed, mid, done):
                pool.wait_ge(summed, i + 1)
                pool.tensor_tensor(s3[:, b, 1:2], s3[:, b, 0:1], epsc[:, :], ALU.add).then_inc(mid, 1)
                pool.wait_ge(mid, i + 1)
                pool.tensor_tensor(s3[:, b, 2:3], s3[:, b, 1:2], nhalf[:, 0:1], ALU.pow).then_inc(done, 1)

            def step(i, b, last):
                factor(i, b, sy, sqy_done, sym_done, ry_done)
                factor(i, b, sx, sqx_done, sxm_done, rx_done)
                if not last:
                    pool.wait_ge(hg_done, i + 1)
                    pool.tensor_tensor(h2[:, b, :], h2[:, b, :], rows[:, 2, :], ALU.add).then_inc(h2_done, 1)

            pool.wait_ge(rows_done, 4)
            step(0, 0, False)
            with pool.Fori(0, NT // 2 - 1) as t:
                step(2 * t + 1, 1, False)
                step(2 * t + 2, 0, False)
            step(NT - 1, 1, True)
            pool.wait_ge(v_done, ONE + NQ * QH)
            pool.memset(ones_r[:, :].bitcast(F32), 1.0).then_inc(rconst, 1)
            pool.memset(tri[:, :].bitcast(F32), 1.0).then_inc(pool_chain, 1)
            pool.memset(le16[:, :, :], 1.0).then_inc(pool_chain, 1)
            pool.memset(lt4[:, :, :], 1.0).then_inc(pool_chain, 1)
            for j in range(NG):
                pool.memset(desc4[:, j:j + 1], float(NG - j)).then_inc(rconst, 1)
            pool.wait_ge(pool_chain, 4 + NT // 2 + 3)
            pool.affine_select(out=tri[:, :], in_=tri[:, :].bitcast(F32), compare_op=ALU.is_ge, fill=0.0, base=-1,
                               pattern=[[1, P]], channel_multiplier=-1).then_inc(rconst, 1)
            pool.affine_select(out=le16[:, :, :], in_=le16[:, :, :], compare_op=ALU.is_ge, fill=0.0, base=0,
                               pattern=[[1, NE], [-1, NE]], channel_multiplier=0).then_inc(rconst, 1)
            pool.affine_select(out=lt4[:, :, :], in_=lt4[:, :, :], compare_op=ALU.is_ge, fill=0.0, base=-1,
                               pattern=[[1, EG], [-1, EG]], channel_multiplier=0).then_inc(rconst, 1)
            pool.iota(iota[:, :], pattern=[[1, P]], base=0, channel_multiplier=0,
                      allow_small_or_imprecise_dtypes=True).then_inc(rconst, 1)
            pool.iota(tok1[:, :], pattern=[[S, 2], [1, NT]], base=1, channel_multiplier=NT,
                      allow_small_or_imprecise_dtypes=True).then_inc(rconst, 1)

            pool.wait_ge(src_made, 1)
            pool.tensor_tensor(ic[:, 0:1], src[:, 0:1], zero_i[:, :], ALU.add).then_inc(ic_done[0], 1)
            pool.wait_ge(ic_done[0], 1)
            pool.indirect_dma_start(xg[:, 0, :], None, h2_rows,
                                    bass.IndirectOffsetOnAxis(ap=ic[:, 0:1].bitcast(U32), axis=0)).then_inc(gath[0], 16)
            pool.wait_ge(tables, 1)
            last_st = pool.value_load(counts[0:1, 0:1], min_val=0, max_val=NST - 1)
            st = last_st + 1

            def low(idx, q, e, k, down):
                pool.wait_ge(pr_hi_done, idx + 1)
                if down:
                    pool.tensor_tensor(pr_lo[:, 3, :], raw_d[:, bass.ds(q, 1), k, :].rearrange("p o n -> p (o n)"),
                                       pr_hi[:, 3, :].bitcast(F32), ALU.subtract).then_inc(pr_lo_pool, 1)
                    return None
                return pool.tensor_tensor(pr_lo[:, 3, :].rearrange("p (g n) -> p g n", g=2),
                                          raw_gu[:, bass.ds(q, 1), :, k, :].rearrange("p o g n -> p (o g) n"),
                                          pr_hi[:, 3, :].bitcast(F32).rearrange("p (g n) -> p g n", g=2), ALU.subtract)

            def settle():
                pool.tensor_tensor(gap_p[:, :], epsc[:, :], epsc[:, :], ALU.add)

            def gather(s, b, turned, n):
                if turned is not None:
                    pool.wait_ge(xt_tr, turned)
                pool.tensor_tensor(ic[:, b:b + 1], src[:, bass.ds(2 * s + b, 1)], zero_i[:, :], ALU.add).then_inc(ic_done[b], 1)
                pool.wait_ge(ic_done[b], n)
                settle()
                pool.indirect_dma_start(xg[:, b, :], None, h2_rows,
                                        bass.IndirectOffsetOnAxis(ap=ic[:, b:b + 1].bitcast(U32), axis=0)).then_inc(gath[b], 16)

            def scatter(b, slot, tiles, before, n):
                pool.wait_ge(y0_done, ONE + tiles)
                pool.wait_ge(y1_done, ONE + tiles)
                pool.wait_ge(scat[b], ONE_DMA + 16 * before)
                col_ = dest[:, bass.ds(slot, 1)]
                pool.tensor_tensor(ic[:, 2 + b:3 + b], col_, zero_i[:, :], ALU.add).then_inc(ic_done[2 + b], 1)
                pool.wait_ge(ic_done[2 + b], n)
                settle()
                pool.indirect_dma_start(y_rows, bass.IndirectOffsetOnAxis(ap=ic[:, 2 + b:3 + b].bitcast(U32), axis=0),
                                        ys[:, b, :], None, bounds_check=2 * S - 1, oob_is_err=False
                                        ).then_inc(scat[b], 16)

            def scatter_both(w_s, hb, nb, tiles):
                before = w_s + 0
                n = w_s + 1
                scatter(0, 2 * w_s, tiles + 1, before, n)
                with pool.If(hb > 0):
                    n = nb + 1
                    scatter(1, 2 * w_s + 1, tiles + 2, nb, n)

            w = Step(pool, 0)
            with pool.If(w.h > 0):
                gather(0, 1, None, 1)
            low(3, 0, 0, 3, False).then_inc(pr_lo_pool, 1)
            gather(1, 0, 1, 2)
            with pool.If(w.hn > 0):
                gather(1, 1, w.cn, w.h + 1)
            low(7, 0, 0, 7, False).then_inc(pr_lo_pool, 2)
            after = Step(pool, 1)
            gather(2, 0, w.cn + 1, 3)
            low(15, w.en & 1, 0, 3, False).then_inc(pr_lo_pool, 1)
            with pool.If(after.hn > 0):
                gather(2, 1, w.cn + 1 + w.hn, w.h + w.hn + 1)
            low(19, w.en & 1, 0, 7, False).then_inc(pr_lo_pool, 1)
            def supertile(s):
                w = Step(pool, s)
                low(12 * s + 11, w.ep & 1, 0, 3, True)
                with pool.If(s + 2 < st):
                    gather(s + 2, 0, w.cn + 1, s + 3)
                    pool.wait_ge(tables, 1)
                with pool.Else():
                    pool.wait_ge(tables, 1)
                with pool.If(s + 1 < st):
                    low(12 * s + 15, w.en & 1, 0, 3, False).then_inc(pr_lo_pool, 1)
                with pool.Else():
                    pool.wait_ge(tables, 1)
                w2 = pool.value_load(words[0:1, bass.ds(s + 1, 1)], min_val=0, max_val=(1 << 23) - 1)
                with pool.If(((w2 >> 17) & 1) > 0):
                    gather(s + 2, 1, w.cn + 1 + w.hn, w.nbn + w.hn + 1)
                scatter_both(s - 1, w.hp, w.nbp, w.cp)
                with pool.If(s + 1 < st):
                    low(12 * s + 19, w.en & 1, 0, 7, False).then_inc(pr_lo_pool, 1)
                with pool.Else():
                    pool.wait_ge(tables, 1)
                pool.wait_ge(tables, 1)

            with pool.Fori(1, NE) as s:
                supertile(s)
            with pool.If(st > NE):
                with pool.Fori(NE, NST) as s:
                    with pool.If(s < st):
                        supertile(s)
                    pool.wait_ge(tables, 1)
                pool.wait_ge(tables, 1)
            w = Step(pool, last_st)
            low(12 * st + 3, (NE - 1) % 2, 0, 3, True)
            scatter_both(last_st, w.h, w.nb, w.c)
            pool.wait_ge(scat[0], ONE_DMA + 16 * st)
            pool.wait_ge(scat[1], ONE_DMA + 16 * w.nbn)
            pool.tensor_tensor(tmp8[:, 0:1], epsc[:, :], epsc[:, :], ALU.add).then_inc(all_scattered, 1)
            def residual(i):
                pool.wait_ge(fg_done, i + 1)
                pool.tensor_tensor(x1[:, i, :], x1[:, i, :], fb[:, i % FB, :], ALU.add).then_inc(o_done[0], 1)

            for i in range(NT):
                pool.wait_ge(sqf_done, i + 1)
                pool.tensor_tensor(sf[:, 1, i:i + 1], sf[:, 0, i:i + 1], epsc[:, :], ALU.add).then_inc(sfm_done, 1)
                pool.wait_ge(sfm_done, i + 1)
                pool.tensor_tensor(sf[:, 2, i:i + 1], sf[:, 1, i:i + 1], nhalf[:, 0:1], ALU.pow).then_inc(rf_done, 1)
                if i >= 1 and i - 1 not in DVE_RESIDUAL:
                    residual(i - 1)
            if NT - 1 not in DVE_RESIDUAL:
                residual(NT - 1)

        @block.scalar
        def _(act):
            act.wait_ge(cols_loaded, 16 * 8)
            act.activation(silc[:, 0, :], col[:, 0, :], ACT.Sigmoid).then_inc(sigc_done, 1)

            def square_sum(i):
                act.wait_ge(x_loaded[i // 2], 16)
                if i > 0:
                    act.wait_ge(ssx_done, i)
                act.activation(junk[:, :], xv[:, i, :], ACT.Square, accum_out=ssx[:, i:i + 1]).then_inc(ssx_done, 1)

            for i in range(NT):
                square_sum(i)

            def split_hi(q, k, first):
                act.wait_ge(stage_loaded[k // 2], 16 * (q + 1))
                if not first:
                    if k < 3:
                        act.wait_ge(wi_used, 3 * q + (k - 2))
                    else:
                        act.wait_ge(win_tile, NT * q)
                act.activation(wi_hi[:, 2 * k:2 * k + 2, :],
                               stage[:, k // 2, 1024 * (k % 2):1024 * (k % 2) + 1024].rearrange("p (k n) -> p k n", k=2),
                               ACT.Copy).then_inc(wi_hi_done, 1)

            def split_wout(k):
                act.wait_ge(stage_loaded[(k // 2) % 2], 16 * (NQ + 1 + k // 4))
                act.wait_ge(win_tile, NQ * NT)
                act.activation(sp_hi[:, k, :], stage[:, (k // 2) % 2, 1024 * (k % 2):1024 * (k % 2) + 1024],
                               ACT.Copy).then_inc(wo_hi_done, 1)

            act.wait_ge(ada1_mod, 2)
            act.activation(mod_row[:, 0, :], ps[:, 0:2, :].rearrange("p b n -> p (b n)"), ACT.Copy).then_inc(shift_row, 1)
            for i in range(NT):
                act.wait_ge(xt_done, i + 1)
                b0 = UT[0] if i % 2 == 0 else CV[0]
                act.activation(sp_hi[:, :, P * i:P * i + P], ps[:, b0:b0 + 2, :].rearrange("p b (k a) -> p (b k) a", a=P),
                               ACT.Copy).then_inc(hhi_done, 1)
                if i < 2:
                    split_hi(0, 2 * i, True)
                    split_hi(0, 2 * i + 1, True)

            def ut(q, b):
                act.wait_ge(ut_tr, QB * q + (ONE + b + 1))
                if b < 2:
                    act.wait_ge(conv_done, ONE + QG * q)
                else:
                    act.wait_ge(conv_done, QG * q + (ONE + BG * (b - 1)))
                act.activation(ut_hi[:, b % 2, :, PAD:PAD + P],
                               ps[:, UT[b % 2], :].rearrange("p (g a) -> p g a", g=BG), ACT.Copy).then_inc(uthi_done, 1)

            def quarter(q, last):
                for i in range(NT):
                    act.wait_ge(pre_done, NT * q + (i + 1))
                    act.activation(pre[:, i % 2, CQ:], pre[:, i % 2, CQ:], ACT.Sigmoid).then_inc(sig_done, 1)
                split = (lambda k: split_wout(k)) if last else (lambda k: split_hi(q + 1, k, False))
                ut(q, 0)
                ut(q, 1)
                split(0)
                split(1)
                ut(q, 2)
                split(2)
                ut(q, 3)
                split(3)

            act.wait_ge(const_made, 6)
            with act.Fori(0, NQ - 1) as q:
                quarter(q, False)
            quarter(NQ - 1, True)
            split_wout(4)
            split_wout(5)
            def silu_tile(i, b):
                act.wait_ge(zt_done, i + 1)
                act.wait_ge(sl_done, i)
                for k in range(KT):
                    last = act.activation(s_full[:, k, :], ps[:, PZ + k // 4, P * (k % 4):P * (k % 4) + P], ACT.Silu,
                                          bias=col[:, 6, k:k + 1], scale=col[:, 5, k:k + 1])
                last.then_inc(s_done, 1)
                act.wait_ge(s_done, i + 1)
                if not (type(i) is int and i < 2):
                    act.wait_ge(yh_done, 2 * i - 2)
                act.activation(s_hi[:, b], s_full[:, :, :], ACT.Copy).then_inc(sh_done, 1)

            def h2t_copy(i):
                act.wait_ge(h2_tr, ONE + i + 1)
                act.wait_ge(rt_done, ONE + i)
                act.activation(h2t[:, :, :], ps[:, PH:PH + 2, :].rearrange("p b (k a) -> p (b k) a", a=P),
                               ACT.Copy).then_inc(h2t_done, 1)

            def step(i, b, first, last):
                if not last:
                    silu_tile(i + 1, 1 - b)
                if not first:
                    h2t_copy(i - 1)
                act.wait_ge(yb_done, 2 * i + 2)
                act.wait_ge(sqx_done, i)
                act.activation(junk2[:, :], yb[:, b, :], ACT.Square, scale=D ** -0.5,
                               accum_out=sy[:, b, 0:1]).then_inc(sqy_done, 1)
                act.wait_ge(x1_done, i + 1)
                act.wait_ge(sqy_done, i + 1)
                act.activation(junk2[:, :], x1[:, bass.ds(i, 1), :], ACT.Square, scale=D ** -0.5,
                               accum_out=sx[:, b, 0:1]).then_inc(sqx_done, 1)

            act.wait_ge(v_done, ONE + NQ * QH)
            silu_tile(0, 0)
            split_wout(6)
            split_wout(7)
            for j in range(4):
                act.wait_ge(brow_tr, j + 1)
                dst = rows[:, j, :] if j < 3 else h2[:, 0, :]
                b0 = (PH, PR)[j % 2]
                act.activation(dst, ps[:, b0:b0 + 2, :].rearrange("p b n -> p (b n)"), ACT.Copy).then_inc(rows_done, 1)
            act.wait_ge(wo_lo_done[0], KT // 2)
            act.wait_ge(wo_lo_done[1], KT // 2)
            step(0, 0, True, False)
            with act.Fori(0, NT // 2 - 1) as t:
                step(2 * t + 1, 1, False, False)
                step(2 * t + 2, 0, False, False)
            step(NT - 1, 1, False, True)
            h2t_copy(NT - 1)
            act.wait_ge(log_done, ONE + NT)
            act.activation(aff[:, :, :], logits[:, :, :], ACT.Sigmoid).then_inc(aff_done, 1)

            def landed(j, e):
                act.wait_ge(raw_loaded[0][j], 16 * ((e >> 1) + 1))
                if not (type(e) is int and e == 0):
                    act.wait_ge(raw_loaded[1][j], ONE_DMA + 16 * ((e + 1) >> 1))

            def high(idx, slot_, q, k, down, e, free):
                if free is not None:
                    act.wait_ge(pr_used, free)
                if down:
                    if k % 2 == 0:
                        landed(4 + k // 2, e)
                    act.activation(pr_hi[:, slot_, :], raw_d[:, bass.ds(q, 1), k, :].rearrange("p o n -> p (o n)"),
                                   ACT.Copy).then_inc(pr_hi_done, 1)
                    return
                if k % 4 == 0:
                    landed(2 * (k // 4), e)
                    landed(2 * (k // 4) + 1, e)
                act.activation(pr_hi[:, slot_, :].rearrange("p (g n) -> p g n", g=2),
                               raw_gu[:, bass.ds(q, 1), :, k, :].rearrange("p o g n -> p (o g) n"),
                               ACT.Copy).then_inc(pr_hi_done, 5 if (type(idx) is int and idx == 7) else 1)

            def x_hi(b, n):
                act.wait_ge(xt_tr, n + 1)
                act.activation(xt_hi[:, b], ps[:, TR:TR + 2, :].rearrange("p b (k a) -> p (b k) a", a=P),
                               ACT.Copy).then_inc(xth_done, 1)

            def silu(b, used, n, freed):
                act.wait_ge(pr_used, used)
                act.wait_ge(he_tr, freed)
                act.activation(he[:, b, :], ps[:, 2 * b, :], ACT.Silu).then_inc(sil_done, 1)

            def y_0(b, n, scattered):
                act.wait_ge(d0_done, n + 1)
                act.wait_ge(scat[b], ONE_DMA + 16 * scattered)
                act.activation(ys[:, b, 0:512], ps[:, DN, :], ACT.Copy).then_inc(y0_done, 1)

            def he_hi(b, n):
                act.wait_ge(he_tr, n + 1)
                act.activation(het_hi[:, b], ps[:, TR + b, :].rearrange("p (k a) -> p k a", a=P),
                               ACT.Copy).then_inc(heth_done, 1)

            act.wait_ge(rt_done, ONE + NT)
            act.wait_ge(h2_done, NT)
            for k in range(4):
                high(k, k, 0, k, False, 0, None)
            act.wait_ge(tables, 1)
            last_st = act.value_load(counts[0:1, 0:1], min_val=0, max_val=NST - 1)
            st = last_st + 1
            w = Step(act, 0)
            x_hi(0, 0)
            with act.If(w.h > 0):
                x_hi(1, 1)
            for k in range(4, KT):
                high(k, k % 4, 0, k, False, 0, k - 3)
            silu(0, 8, 0, 0)
            x_hi(0, w.cn)
            with act.If(w.h > 0):
                silu(1, 8, 1, 0)
            with act.If(w.hn > 0):
                x_hi(1, w.cn + 1)
            for k in range(4):
                high(12 + k, k, w.en & 1, k, False, w.en, 9 + k)
            he_hi(0, 0)
            with act.If(w.h > 0):
                he_hi(1, 1)
            for k in range(4, KT):
                high(12 + k, k % 4, w.en & 1, k, False, w.en, 9 + k)
            def supertile(s):
                w = Step(act, s)
                more = s + 1 < st
                qp = w.ep & 1
                for k in range(FT):
                    high(12 * s + 8 + k, k, qp, k, True, w.ep, 12 * s + 5 + k)
                silu(0, 12 * s + 8, w.c, w.c)
                with act.If(more):
                    x_hi(0, w.cn)
                with act.Else():
                    act.wait_ge(tables, 1)
                with act.If(w.h > 0):
                    silu(1, 12 * s + 8, w.c + 1, w.c)
                with act.If(w.hp > 0):
                    y_0(0, w.cp, s - 1)
                with act.If(w.hn > 0):
                    x_hi(1, w.cn + 1)
                with act.If(more):
                    qn = w.en & 1
                    for k in range(4):
                        high(12 * s + 12 + k, k, qn, k, False, w.en, 12 * s + 9 + k)
                with act.Else():
                    act.wait_ge(tables, 1)
                with act.If(w.hp > 0):
                    y_0(1, w.cp + 1, w.nbp)
                with act.Else():
                    y_0(0, w.cp, s - 1)
                he_hi(0, w.c)
                with act.If(w.h > 0):
                    he_hi(1, w.c + 1)
                with act.If(more):
                    qn = w.en & 1
                    for k in range(4, KT):
                        high(12 * s + 12 + k, k % 4, qn, k, False, w.en, 12 * s + 9 + k)
                with act.Else():
                    act.wait_ge(tables, 1)
                act.wait_ge(tables, 1)

            with act.Fori(1, NE) as s:
                supertile(s)
            with act.If(st > NE):
                with act.Fori(NE, NST) as s:
                    with act.If(s < st):
                        supertile(s)
                    act.wait_ge(tables, 1)
                act.wait_ge(tables, 1)
            w = Step(act, last_st)
            for k in range(FT):
                high(12 * st + k, k, (NE - 1) % 2, k, True, NE - 1, 12 * last_st + 9 + k)
            with act.If(w.h > 0):
                y_0(0, w.c, last_st)
                y_0(1, w.c + 1, w.nb)
            with act.Else():
                y_0(0, w.c, last_st)
            def first_choice(i):
                act.wait_ge(yl[i // 2], 32)
                if i >= FB:
                    made, n_made = out_of(i - FB)
                    act.wait_ge(made, n_made)
                act.activation(fb[:, i % FB, :], y_all[:, 0, i, :], ACT.Copy, scale=gates[:, 0, i:i + 1]).then_inc(fa_done, 1)

            first_choice(0)
            for i in range(NT):
                if i + 1 < NT:
                    first_choice(i + 1)
                act.wait_ge(f_done, i + 1)
                act.wait_ge(sqf_done, i)
                act.activation(junk3[:, :], fb[:, i % FB, :], ACT.Square, scale=D ** -0.5,
                               accum_out=sf[:, 0, i:i + 1]).then_inc(sqf_done, 1)

        @block.vector
        def _(dve):
            dve.wait_ge(cols_loaded, 16 * 8)
            dve.wait_ge(sigc_done, 1)
            dve.tensor_tensor(silc[:, 1, :], silc[:, 0, :], col[:, 0, :], ALU.mult).then_inc(silc_done, 1)

            dve.wait_ge(silc_done, 1)
            both = acc01[:, :, :].rearrange("p s d -> p (s d)")
            for k in range(KT):
                dve.wait_ge(ada1_loaded[k // 2 if k < KT - 1 else 4], 16)
                if k == 0:
                    dve.tensor_scalar(both, ada_first[:, k, :], silc[:, 1, k:k + 1], None, ALU.mult).then_inc(acc1_done, 1)
                else:
                    dve.wait_ge(acc1_done, k)
                    dve.scalar_tensor_tensor(out=both, in0=ada_first[:, k, :], scalar=silc[:, 1, k:k + 1],
                                             in1=both, op0=ALU.mult, op1=ALU.add).then_inc(acc1_done, 1)
                if k == 3:
                    dve.wait_ge(brow1_loaded, 32)
                    dve.wait_ge(acc1_done, k + 1)
                    dve.tensor_tensor(acc01[0:1, :, :], acc01[0:1, :, :], mod_row[0:1, 0:2, :], ALU.add).then_inc(bias_done, 1)
                    dve.wait_ge(bias_done, 1)
            dve.wait_ge(ada1_mod, 1)
            dve.scalar_tensor_tensor(out=mod_row[:, 1, :], in0=ps[:, 2:4, :].rearrange("p b n -> p (b n)"), scalar=1.0,
                                     in1=mod_row[:, 2, :], op0=ALU.add, op1=ALU.mult).then_inc(mod1_done, 1)
            dve.wait_ge(mod1_done, 1)

            def split_lo(q, k):
                dve.wait_ge(wi_hi_done, 4 * q + (k + 1))
                dve.tensor_tensor(wi_lo[:, 2 * k:2 * k + 2, :],
                                  stage[:, k // 2, 1024 * (k % 2):1024 * (k % 2) + 1024].rearrange("p (k n) -> p k n", k=2),
                                  wi_hi[:, 2 * k:2 * k + 2, :].bitcast(F32), ALU.subtract).then_inc(wi_lo_done, 1)

            def split_wout(k):
                dve.wait_ge(wo_hi_done, k + 1)
                dve.tensor_tensor(sp_lo[:, k, :], stage[:, (k // 2) % 2, 1024 * (k % 2):1024 * (k % 2) + 1024],
                                  sp_hi[:, k, :].bitcast(F32), ALU.subtract).then_inc(wo_lo_done[0], 1)

            def gained(i):
                dve.wait_ge(rsx_done, i // 2 + 1)
                dve.scalar_tensor_tensor(out=xv[:, i, :], in0=xv[:, i, :], scalar=rsx[:, i:i + 1], in1=mod_row[:, 1, :],
                                         op0=ALU.mult, op1=ALU.mult).then_inc(xn_done, 1)

            def h_lo(i):
                dve.wait_ge(hhi_done, i + 1)
                b0 = UT[0] if i % 2 == 0 else CV[0]
                dve.tensor_tensor(sp_lo[:, :, P * i:P * i + P], ps[:, b0:b0 + 2, :].rearrange("p b (k a) -> p (b k) a", a=P),
                                  sp_hi[:, :, P * i:P * i + P].bitcast(F32), ALU.subtract).then_inc(hlo_done, 1)

            gained(0)
            dve.wait_ge(xn_done, 1)
            dve.wait_ge(shift_row, 1)
            dve.tensor_tensor(xv[:, 0, :], xv[:, 0, :], mod_row[:, 0, :], ALU.add).then_inc(hs_done, 1)
            gained(1)
            gained(2)
            for i in range(NT):
                h_lo(i)
                if i + 3 < NT:
                    gained(i + 3)
                if i == NT - 2:
                    for k in range(3):
                        split_lo(0, k)
            split_lo(0, 3)
            dve.wait_ge(hlo_done, NT)
            dve.wait_ge(const_made, 6)
            dve.wait_ge(eye_made, NT)

            def make_m(q, g):
                if g < MSLOTS:
                    dve.wait_ge(conv_done, ONE + QG * q)
                else:
                    dve.wait_ge(conv_done, QG * q + (ONE + g - MSLOTS + 1))
                dve.tensor_tensor(mx[:, g % MSLOTS, :, 1, :].rearrange("p d (i c) -> p d i c", i=NT),
                                  taps_lo[:, g, :].bitcast(F32).rearrange("p (d i) -> p d i", d=ND).unsqueeze(3)
                                  .to_broadcast([P, ND, NT, GC]),
                                  eye16[:, :].unsqueeze(1).unsqueeze(1).to_broadcast([P, ND, NT, GC]),
                                  ALU.mult).then_inc(mlo_done, 1)

            def ut(q, b):
                dve.wait_ge(uthi_done, QB * q + (b + 1))
                dve.tensor_tensor(ut_lo[:, b % 2, :, PAD:PAD + P],
                                  ps[:, UT[b % 2], :].rearrange("p (g a) -> p g a", g=BG),
                                  ut_hi[:, b % 2, :, PAD:PAD + P].bitcast(F32), ALU.subtract).then_inc(utlo_done, 1)

            def gate(q, i):
                dve.wait_ge(sig_done, NT * q + (i + 1))
                dve.tensor_tensor(u[:, :, GC * i:GC * i + GC], pre[:, i % 2, 0:CQ].rearrange("p (g c) -> p g c", c=GC),
                                  pre[:, i % 2, CQ:].rearrange("p (g c) -> p g c", c=GC),
                                  ALU.mult).then_inc(u_done, 1)

            def half_moments(i, h):
                dve.bn_stats(stats[:, i, h, :], xv[:, i, 512 * h:512 * h + 512]).then_inc(stats_done, 1)

            def moments(i, stats_before):
                dve.wait_ge(stats_done, stats_before + 1)
                dve.bn_aggr(mv[:, i, :], stats[:, i]).then_inc(mv_done, 1)

            def quarter(q, last):
                dve.wait_ge(ut_tr, ONE + QB * q)
                dve.wait_ge(brow_loaded, 16 * q + 16)
                for i in range(NT):
                    dve.wait_ge(ada_loaded[i % 2], 64 * q + (16 * (i // 2) + 16))
                    if i == 0:
                        dve.wait_ge(acc_col, ONE + q)
                        dve.tensor_scalar(acc[:, :], ada_stage[:, 0, :], silc[:, 1, 0:1], None,
                                          ALU.mult).then_inc(acc_done, 1)
                    else:
                        dve.wait_ge(acc_done, KT * q + (ONE + i))
                        dve.scalar_tensor_tensor(out=acc[:, :], in0=ada_stage[:, i % 2, :], scalar=silc[:, 1, i:i + 1],
                                                 in1=acc[:, :], op0=ALU.mult, op1=ALU.add).then_inc(acc_done, 1)
                    dve.wait_ge(win_tile, NT * q + (i + 1))
                    dve.wait_ge(u_done, NT * q + (ONE + max(i - 1, 0)))
                    dve.tensor_tensor(pre[:, i % 2, :], ps[:, WI[i % 3], :], bin_row[:, :],
                                      ALU.add).then_inc(pre_done, 1)
                    if i >= 1:
                        gate(q, i - 1)
                    if i < MSLOTS:
                        if i == 0:
                            dve.wait_ge(taps_split, 2 * q + 2)
                        make_m(q, i)
                gate(q, NT - 1)
                ut(q, 0)
                ut(q, 1)
                dve.wait_ge(acc_col, ONE + q + 1)
                dve.tensor_tensor(modc[:, bass.ds(q, 1), :], ps[:, MODB, 16:16 + KT].unsqueeze(1),
                                  bada[:, bass.ds(q + 2, 1), :], ALU.add).then_inc(modc_done, 1)
                if last:
                    dve.wait_ge(modc_done, ONE + NQ)
                    dve.tensor_tensor(vcol[:, 0, :], modc[:, 0, :], col[:, 2, :], ALU.mult).then_inc(vcol_done, 1)
                    dve.scalar_tensor_tensor(out=vcol[:, 1, :], in0=modc[:, 2, :], scalar=1.0, in1=col[:, 3, :],
                                             op0=ALU.add, op1=ALU.mult).then_inc(vcol_done, 1)
                    dve.tensor_tensor(vcol[:, 2, :], modc[:, 3, :], col[:, 4, :], ALU.mult).then_inc(vcol_done, 1)
                dve.wait_ge(bdw_loaded, 16 * q + 16)
                for b in range(QB):
                    for h in (2 * b, 2 * b + 1):
                        vo = xv[:, :, bass.ds(q * CQ + CG * GC * h, CG * GC)].rearrange("p i (g c) -> p g i c", g=CG)
                        vp = ps[:, CV[h % 2], :].rearrange("p (g s i c) -> p g s i c", g=CG, s=2, i=NT)
                        dve.wait_ge(conv_done, QG * q + (ONE + CG * (h + 1)))
                        dve.tensor_tensor(vo, vp[:, :, 1], bdw_row[:, CG * GC * h:CG * GC * (h + 1)]
                                          .rearrange("p (g c) -> p g c", g=CG).unsqueeze(2)
                                          .to_broadcast([P, CG, NT, GC]), ALU.add).then_inc(vb_done, 1)
                        dve.wait_ge(vb_done, QH * q + (h + 1))
                        dve.tensor_tensor(vo, vp[:, :, 0], vo, ALU.add).then_inc(v_done, 1)
                        if b + 1 < QB:
                            for g in range(CG):
                                make_m(q, CG * h + BG + g)
                    if not last:
                        split_lo(q + 1, b)
                    elif b < 2:
                        split_wout(b)
                    elif b == 2:
                        dve.wait_ge(v_done, ONE + QH * (NQ - 1))
                        half_moments(0, 0)
                        half_moments(1, 0)
                    if b + 2 < QB:
                        ut(q, b + 2)

            with dve.Fori(0, NQ - 1) as q:
                quarter(q, False)
            quarter(NQ - 1, True)
            def normalised(i, first):
                if not first:
                    dve.wait_ge(zt_done, i)
                dve.tensor_scalar(zb[:, :], xv[:, bass.ds(i, 1), :].rearrange("p o d -> p (o d)"),
                                  mv[:, bass.ds(i, 1), 0:1].rearrange("p o j -> p (o j)"),
                                  lnr[:, 1, bass.ds(i, 1)], ALU.subtract, ALU.mult).then_inc(z_done, 1)

            def s_low(i, b, first):
                dve.wait_ge(sh_done, i + 1)
                if not first:
                    dve.wait_ge(yh_done, 2 * i - 2)
                dve.tensor_tensor(s_lo[:, b], s_full[:, :, :], s_hi[:, b].bitcast(F32), ALU.subtract).then_inc(sl_done, 1)

            def y_half(i, b, h):
                dve.wait_ge(yh_done, 2 * i + h + 1)
                cols = slice(512 * h, 512 * h + 512)
                dve.tensor_tensor(yb[:, b, cols], ps[:, PY + h, :], bout_row[:, cols], ALU.add).then_inc(yb_done, 1)

            def logits_of(i):
                dve.wait_ge(rt_done, ONE + i + 1)
                dve.tensor_copy(logits[:, bass.ds(i, 1), :], ps[:, PR, 0:NE].unsqueeze(1)).then_inc(log_done, 1)

            def gained(i, b):
                dve.wait_ge(rx_done, i + 1)
                if type(i) is int and i == 0:
                    dve.wait_ge(g3_stored, 16)
                elif not (type(i) is int and i == 1):
                    dve.wait_ge(h2_stored[b], ONE_DMA + 16 * ((i - b) // 2))
                    dve.wait_ge(h2_tr, ONE + i - 1)
                dve.scalar_tensor_tensor(out=h2[:, b, :], in0=x1[:, bass.ds(i, 1), :].rearrange("p o d -> p (o d)"),
                                         scalar=sx[:, b, 2:3], in1=rows[:, 1, :],
                                         op0=ALU.mult, op1=ALU.mult).then_inc(hg_done, 1)

            def step(i, b, first, last):
                if not last and not first:
                    normalised(i + 1, False)
                if not first:
                    gained(i - 1, 1 - b)
                y_half(i, b, 0)
                if not last:
                    s_low(i + 1, 1 - b, first)
                y_half(i, b, 1)
                dve.wait_ge(ry_done, i + 1)
                dve.scalar_tensor_tensor(out=yb[:, b, :], in0=yb[:, b, :], scalar=sy[:, b, 2:3], in1=rows[:, 0, :],
                                         op0=ALU.mult, op1=ALU.mult).then_inc(t_done, 1)
                dve.wait_ge(t_done, i + 1)
                xi = x1[:, bass.ds(i, 1), :].rearrange("p o d -> p (o d)")
                dve.wait_ge(xr_loaded[b], 16 * ((i - b) // 2) + 16)
                dve.tensor_tensor(xi, yb[:, b, :], xr[:, b, :], ALU.add).then_inc(x1_done, 1)
                if not first:
                    logits_of(i - 1)

            dve.wait_ge(v_done, ONE + NQ * QH)
            half_moments(0, 1)
            moments(0, 2)
            half_moments(1, 1)
            dve.wait_ge(lnr_done, 1)
            dve.wait_ge(mv_done, 1)
            normalised(0, True)
            moments(1, 3)
            split_wout(4)
            split_wout(5)
            for i in range(2, NT):
                half_moments(i, 0)
                half_moments(i, 1)
                moments(i, 2 * i + 1)
                if i == 4:
                    dve.wait_ge(sh_done, 1)
                    dve.tensor_tensor(s_lo[:, 0], s_full[:, :, :], s_hi[:, 0].bitcast(F32),
                                      ALU.subtract).then_inc(sl_done, 1)
            dve.wait_ge(lnr_done, 2)
            dve.wait_ge(mv_done, NT)
            normalised(1, False)
            dve.wait_ge(bout_loaded, 16)
            step(0, 0, True, False)
            step(1, 1, False, False)
            with dve.Fori(1, NT // 2 - 1) as t:
                step(2 * t, 0, False, False)
                step(2 * t + 1, 1, False, False)
            step(NT - 2, 0, False, False)
            step(NT - 1, 1, False, True)
            gained(NT - 1, 1)
            dve.wait_ge(hg_done, NT)
            dve.wait_ge(h2_done, NT - 1)
            dve.tensor_tensor(h2[:, 1, :], h2[:, 1, :], rows[:, 2, :], ALU.add).then_inc(h2_done, 1)
            logits_of(NT - 1)
            def low(turn, slot_, q, k, down, inc):
                dve.wait_ge(pr_hi_done, 4 * turn + slot_ + 1)
                if down:
                    dve.tensor_tensor(pr_lo[:, slot_, :], raw_d[:, bass.ds(q, 1), k, :].rearrange("p o n -> p (o n)"),
                                      pr_hi[:, slot_, :].bitcast(F32), ALU.subtract).then_inc(pr_lo_dve, inc)
                else:
                    dve.tensor_tensor(pr_lo[:, slot_, :].rearrange("p (g n) -> p g n", g=2),
                                      raw_gu[:, bass.ds(q, 1), :, k, :].rearrange("p o g n -> p (o g) n"),
                                      pr_hi[:, slot_, :].bitcast(F32).rearrange("p (g n) -> p g n", g=2),
                                      ALU.subtract).then_inc(pr_lo_dve, inc)

            chain = [0]

            def then(ins):
                ins.then_inc(route_chain, 1)
                chain[0] += 1
                dve.wait_ge(route_chain, chain[0])

            def tt(o, a, b, op):
                then(dve.tensor_tensor(o, a, b, op))

            def ts(o, a, x_, y_, op0, op1=None):
                if op1 is None:
                    then(dve.tensor_scalar(o, a, x_, None, op0))
                else:
                    then(dve.tensor_scalar(o, a, x_, y_, op0, op1))

            def total(o, a, op=ALU.add):
                then(dve.tensor_reduce(o, a, axis=AX_X, op=op))

            dve.wait_ge(aff_done, 1)
            dve.wait_ge(rconst, NG + 6)
            dve.wait_ge(rt_done, ONE + NT)
            dve.wait_ge(h2_done, NT)
            dve.wait_ge(h2_stored[0], ONE_DMA + 16 * (NT // 2))
            dve.wait_ge(h2_stored[1], ONE_DMA + 16 * (NT // 2))
            tt(sel[:, :, :], aff[:, :, :], rb_row[:, :].unsqueeze(1).to_broadcast([P, NT, NE]), ALU.add)
            s4 = sel[:, :, :].rearrange("p t (g h j) -> p (t g) h j", g=NG, h=2)
            tt(pair_max[:, :, :], s4[:, :, :, 0], s4[:, :, :, 1], ALU.max)
            tt(pair_min[:, :, :], s4[:, :, :, 0], s4[:, :, :, 1], ALU.min)

            def g6(j):
                return gs[:, j].rearrange("p t g -> p (t g)")

            tt(g6(0), pair_max[:, :, 0], pair_max[:, :, 1], ALU.max)
            tt(g6(1), pair_max[:, :, 0], pair_max[:, :, 1], ALU.min)
            tt(g6(2), pair_min[:, :, 0], pair_min[:, :, 1], ALU.max)
            tt(g6(1), g6(1), g6(2), ALU.max)
            tt(g6(0), g6(0), g6(1), ALU.add)
            total(gmax[:, 0, :], gs[:, 0], ALU.max)
            tt(gs[:, 3], gs[:, 0], gmax[:, 0, :].unsqueeze(2).to_broadcast([P, NT, NG]), ALU.is_ge)
            tt(gs[:, 3], gs[:, 3], desc4[:, :].unsqueeze(1).to_broadcast([P, NT, NG]), ALU.mult)
            total(gmax[:, 1, :], gs[:, 3], ALU.max)
            tt(gs[:, 4], gs[:, 3], gmax[:, 1, :].unsqueeze(2).to_broadcast([P, NT, NG]), ALU.is_equal)
            chosen = gs[:, 4].unsqueeze(3).to_broadcast([P, NT, NG, EG])
            tt(of4[:, :, :, :], sel[:, :, :].rearrange("p t (g j) -> p t g j", g=NG), chosen, ALU.mult)
            total(four[:, :, :], of4[:, :, :, :].rearrange("p t g j -> p t j g"))
            inner = four[:, :, :].unsqueeze(2).to_broadcast([P, NT, EG, EG])
            outer = four[:, :, :].unsqueeze(3).to_broadcast([P, NT, EG, EG])
            tt(beats[:, 0], inner, outer, ALU.is_gt)
            tt(beats[:, 1], inner, outer, ALU.is_equal)
            tt(beats[:, 1], beats[:, 1], lt4[:, :, :].unsqueeze(1).to_broadcast([P, NT, EG, EG]), ALU.mult)
            tt(beats[:, 0], beats[:, 0], beats[:, 1], ALU.add)
            total(rank[:, :, :], beats[:, 0])
            for k in range(2):
                ts(is_k[:, k], rank[:, :, :], float(k), None, ALU.is_equal)
                tt(mk[:, k].rearrange("p t (g j) -> p t g j", g=NG), is_k[:, k].unsqueeze(2).to_broadcast([P, NT, NG, EG]),
                   chosen, ALU.mult)
            then(dve.memset(m9[:, NT, :].bitcast(F32), 0.0))
            tt(m9[:, 0:NT, :], mk[:, 0], mk[:, 1], ALU.add)
            marks["chosen"] = chain[0]
            for k in range(2):
                tt(prod[:, NT * k:NT * k + NT, :], mk[:, k], aff[:, :, :], ALU.mult)
            total(ak[:, :, :].rearrange("p k t -> p (k t)"), prod[:, :, :])
            tt(den[:, 0, :], ak[:, 0, :], ak[:, 1, :], ALU.add)
            then(dve.reciprocal(den[:, 1, :], den[:, 0, :]))
            tt(gates[:, :, :], ak[:, :, :], den[:, 1, :].unsqueeze(1).to_broadcast([P, 2, NT]), ALU.mult)
            dve.wait_ge(pos_done, 1)
            then(dve.tensor_copy(cnt[:, 0, :], ps[:, PZ, NT * NE:NT * NE + NE]))
            ts(cnt[:, 1, :], cnt[:, 0, :], float(ST_ROWS), None, ALU.is_gt)
            for j in (2, 3):
                then(dve.scalar_tensor_tensor(out=cnt[:, 1, :], in0=cnt[:, 0, :], scalar=float(j * ST_ROWS),
                                              in1=cnt[:, 1, :], op0=ALU.is_gt, op1=ALU.add))
            ts(cnt[:, 1, :], cnt[:, 1, :], 1.0, None, ALU.add)
            tt(prod16[:, :, :], le16[:, :, :], cnt[:, 1, :].unsqueeze(1).to_broadcast([P, NE, NE]), ALU.mult)
            total(cnt[:, 2, :], prod16[:, :, :])
            tt(cnt[:, 3, :], cnt[:, 2, :], cnt[:, 1, :], ALU.subtract)
            ts(cnt[:, 4, :], cnt[:, 3, :], float(ST_ROWS), None, ALU.mult)
            tt(cnt[:, 5, :], cnt[:, 4, :], cnt[:, 0, :], ALU.add)
            tt(pos[:, :, :], ps[:, PZ, 0:NT * NE].rearrange("p (t e) -> p t e", e=NE),
               cnt[:, 4, :].unsqueeze(1).to_broadcast([P, NT, NE]), ALU.add)
            for k in range(2):
                tt(prod[:, NT * k:NT * k + NT, :], mk[:, k], pos[:, :, :], ALU.mult)
            total(slot[:, :], prod[:, :, :])
            then(dve.tensor_copy(slot_i[:, 0, :], slot[:, :]))
            ts(slot_i[:, 1, :], slot_i[:, 0, :], 7, None, ALU.arith_shift_right)
            ts(slot_i[:, 2, :], slot_i[:, 0, :], P - 1, None, ALU.bitwise_and)
            then(dve.tensor_copy(slot_f[:, :, :], slot_i[:, 1:3, :]))
            tt(oh_t[:, :, :], iota[:, 0:2 * NSTC].unsqueeze(1).to_broadcast([P, 2 * NT, 2 * NSTC]),
               slot_f[:, 0, :].unsqueeze(2).to_broadcast([P, 2 * NT, 2 * NSTC]), ALU.is_equal)
            tt(oh_t[:, :, :], oh_t[:, :, :].bitcast(F32), tok1[:, :].unsqueeze(2).to_broadcast([P, 2 * NT, 2 * NSTC]), ALU.mult)
            for j in range(4):
                part = slice(NT // 2 * j, NT // 2 * (j + 1))
                tt(oh_p[:, part, :], iota[:, :].unsqueeze(1).to_broadcast([P, NT // 2, P]),
                   slot_f[:, 1, part].unsqueeze(2).to_broadcast([P, NT // 2, P]), ALU.is_equal)
                marks["slots", j] = chain[0]
            ts(start[:, 0, :], iota[:, 0:NSTC], float(ST_ROWS), None, ALU.mult)
            ts(start[:, 1, :], start[:, 0, :], float(P), None, ALU.add)
            sh3 = [P, NSTC, NE]
            srow = iota[:, 0:NSTC].unsqueeze(2).to_broadcast(sh3)
            tt(st_le[:, :, :], cnt[:, 2, :].unsqueeze(1).to_broadcast(sh3), srow, ALU.is_le)
            tt(st_in[:, :, :], cnt[:, 3, :].unsqueeze(1).to_broadcast(sh3), srow, ALU.is_le)
            dve.wait_ge(slots_done, 1)
            ts(dest[:, :], ps[:, PZ + 1, 0:2 * NSTC], -1.0, None, ALU.add)
            dve.tensor_scalar(src[:, 0:2 * NSTC], dest[:, :], S - 1, None, ALU.bitwise_and).then_inc(src_made, 1)
            tt(st_in[:, :, :], st_in[:, :, :], st_le[:, :, :], ALU.subtract)
            tt(st_ab[:, :, :], cnt[:, 5, :].unsqueeze(1).to_broadcast(sh3),
               start[:, 1, :].unsqueeze(2).to_broadcast(sh3), ALU.is_gt)
            tt(st_ab[:, :, :], st_ab[:, :, :], st_in[:, :, :], ALU.mult)
            then(dve.memset(e_of[:, :], 0.0))
            then(dve.memset(hb_of[:, :, :], 0.0))
            total(e_of[:, 1:NSTC + 1], st_le[:, :, :])
            total(hb_of[:, 0, 16:16 + NSTC], st_ab[:, :, :])
            then(dve.tensor_copy(word_f[:, 1, :], hb_of[:, 0, 16:16 + NSTC]))
            marks["hb"] = chain[0]
            then(dve.scalar_tensor_tensor(out=word_f[:, 0, :], in0=e_of[:, 1:NSTC + 1], scalar=32.0,
                                          in1=e_of[:, 0:NSTC], op0=ALU.mult, op1=ALU.add))
            for scale_, v in ((1024.0, e_of[:, 2:NSTC + 2]), (2.0 ** 15, hb_of[:, 0, 15:15 + NSTC]),
                              (2.0 ** 16, hb_of[:, 0, 16:16 + NSTC]), (2.0 ** 17, hb_of[:, 0, 17:17 + NSTC])):
                then(dve.scalar_tensor_tensor(out=word_f[:, 0, :], in0=v, scalar=scale_,
                                              in1=word_f[:, 0, :], op0=ALU.mult, op1=ALU.add))
            for j, d in enumerate((1, 2, 4, 8, 16)):
                tt(hb_of[:, (j + 1) % 2, 16:16 + NSTC], hb_of[:, j % 2, 16:16 + NSTC],
                   hb_of[:, j % 2, 16 - d:16 - d + NSTC], ALU.add)
            then(dve.scalar_tensor_tensor(out=word_f[:, 0, :], in0=hb_of[:, 1, 14:14 + NSTC], scalar=2.0 ** 18,
                                          in1=word_f[:, 0, :], op0=ALU.mult, op1=ALU.add))
            then(dve.tensor_copy(words[:, :], word_f[:, 0, :]))
            ts(ct_i[:, :], cnt[:, 2, :], -1.0, None, ALU.add)
            ts(counts[:, 0:1], cnt[:, 2, NE - 1:NE], -1.0, None, ALU.add)
            then(dve.tensor_copy(counts[:, 1:2], hb_of[:, 1, 15 + NSTC:16 + NSTC]))
            then(dve.memset(gap[:, :], 0.0))
            dve.tensor_copy(gap[:, :], gmax[:, 0, 0:1]).then_inc(tables, 1)
            for k in range(3):
                low(0, k, 0, k, False, 1)

            last_st = dve.value_load(counts[0:1, 0:1], min_val=0, max_val=NST - 1)
            st = last_st + 1

            def x_lo(b, n):
                dve.wait_ge(xth_done, n + 1)
                dve.tensor_tensor(xt_lo[:, b], ps[:, TR:TR + 2, :].rearrange("p b (k a) -> p (b k) a", a=P),
                                  xt_hi[:, b].bitcast(F32), ALU.subtract).then_inc(xtl_done, 1)

            def times_up(b, n):
                dve.wait_ge(sil_done, n + 1)
                dve.tensor_tensor(he[:, b, :], he[:, b, :], ps[:, 2 * b + 1, :], ALU.mult).then_inc(he_done, 1)

            def y_1(b, sem_, n, scattered):
                dve.wait_ge(sem_, n)
                dve.wait_ge(scat[b], ONE_DMA + 16 * scattered)
                dve.tensor_copy(ys[:, b, 512:1024], ps[:, DN + 1, :]).then_inc(y1_done, 1)

            def he_lo(b, n):
                dve.wait_ge(heth_done, n + 1)
                dve.tensor_tensor(het_lo[:, b], ps[:, TR + b, :].rearrange("p (k a) -> p k a", a=P),
                                  het_hi[:, b].bitcast(F32), ALU.subtract).then_inc(hetl_done, 1)

            w = Step(dve, 0)
            x_lo(0, 0)
            with dve.If(w.h > 0):
                x_lo(1, 1)
            for k in range(3):
                low(1, k, 0, k + 4, False, 4 if k == 2 else 1)
            times_up(0, 0)
            x_lo(0, w.cn)
            with dve.If(w.h > 0):
                times_up(1, 1)
            with dve.If(w.hn > 0):
                x_lo(1, w.cn + 1)
            for k in range(3):
                low(3, k, w.en & 1, k, False, 1)
            he_lo(0, 0)
            with dve.If(w.h > 0):
                he_lo(1, 1)
            for k in range(3):
                low(4, k, w.en & 1, k + 4, False, 1)
            def supertile(s):
                w = Step(dve, s)
                more = s + 1 < st
                qp = w.ep & 1
                for k in range(3):
                    low(3 * s + 2, k, qp, k, True, 1)
                times_up(0, w.c)
                with dve.If(more):
                    x_lo(0, w.cn)
                with dve.Else():
                    dve.wait_ge(tables, 1)
                with dve.If(w.h > 0):
                    times_up(1, w.c + 1)
                with dve.If(w.hp > 0):
                    y_1(0, d1_done, w.nbp + 1, s - 1)
                with dve.If(w.hn > 0):
                    x_lo(1, w.cn + 1)
                with dve.If(more):
                    qn = w.en & 1
                    for k in range(3):
                        low(3 * s + 3, k, qn, k, False, 1)
                with dve.Else():
                    dve.wait_ge(tables, 1)
                with dve.If(w.hp > 0):
                    y_1(1, pr_used, 12 * s + 12, w.nbp)
                with dve.Else():
                    y_1(0, pr_used, 12 * s + 12, s - 1)
                he_lo(0, w.c)
                with dve.If(w.h > 0):
                    he_lo(1, w.c + 1)
                with dve.If(more):
                    qn = w.en & 1
                    for k in range(3):
                        low(3 * s + 4, k, qn, k + 4, False, 1)
                with dve.Else():
                    dve.wait_ge(tables, 1)
                dve.wait_ge(tables, 1)

            with dve.Fori(1, NE) as s:
                supertile(s)
            with dve.If(st > NE):
                with dve.Fori(NE, NST) as s:
                    with dve.If(s < st):
                        supertile(s)
                    dve.wait_ge(tables, 1)
                dve.wait_ge(tables, 1)
            w = Step(dve, last_st)
            for k in range(3):
                low(3 * st, k, (NE - 1) % 2, k, True, 1)
            with dve.If(w.h > 0):
                y_1(0, d1_done, w.nb + 1, last_st)
                y_1(1, pr_used, 12 * st + 4, w.nb)
            with dve.Else():
                y_1(0, pr_used, 12 * st + 4, last_st)
            dve.wait_ge(g3_loaded, 16)

            def scaled(i):
                dve.wait_ge(rf_done, i + 1)
                dve.scalar_tensor_tensor(out=fb[:, i % FB, :], in0=fb[:, i % FB, :], scalar=sf[:, 2, i:i + 1], in1=g3[:, :],
                                         op0=ALU.mult, op1=ALU.mult).then_inc(fg_done, 1)
                if i in DVE_RESIDUAL:
                    dve.wait_ge(fg_done, i + 1)
                    dve.tensor_tensor(x1[:, i, :], x1[:, i, :], fb[:, i % FB, :], ALU.add).then_inc(o_done[1], 1)

            for i in range(NT):
                dve.wait_ge(fa_done, i + 1)
                dve.scalar_tensor_tensor(out=fb[:, i % FB, :], in0=y_all[:, 1, i, :], scalar=gates[:, 1, i:i + 1],
                                         in1=fb[:, i % FB, :], op0=ALU.mult, op1=ALU.add).then_inc(f_done, 1)
                if i >= 1:
                    scaled(i - 1)
            scaled(NT - 1)

        @block.tensor
        def _(pe):
            pe.wait_ge(const_made, 6)
            pe.wait_ge(acc1_done, KT)
            for sec in (1, 0):
                for h in range(2):
                    last = pe.matmul(ps[:, 2 * sec + h, :], ones[:, :], acc01[:, sec, 512 * h:512 * h + 512],
                                     start=True, stop=True)
                last.then_inc(ada1_mod, 1)
            pe.wait_ge(mod1_done, 1)
            pe.wait_ge(shift_row, 1)
            for i in range(NT):
                pe.wait_ge(hs_done, i + 1)
                if i >= 2:
                    pe.wait_ge(hlo_done, i - 1)
                b0 = UT[0] if i % 2 == 0 else CV[0]
                for k in range(KT):
                    last = pe.transpose(ps[:, b0 + k // 4, P * (k % 4):P * (k % 4) + P],
                                        xv[:, i, bass.ds(k, P, step=KT)], ident[:, :])
                last.then_inc(xt_done, 1)

            def quarter(q):
                for i in range(NT):
                    pe.wait_ge(hlo_done, i + 1)
                    if i >= 3:
                        pe.wait_ge(pre_done, NT * q + (i - 2))
                    o = ps[:, WI[i % 3], :]
                    for k in range(KT):
                        if i == 0 and k % 2 == 0:
                            pe.wait_ge(wi_lo_done, 4 * q + (k // 2 + 1))
                        tok = slice(P * i, P * i + P)
                        pe.matmul(o, sp_hi[:, k, tok], wi_hi[:, k, :], start=(k == 0), stop=False)
                        pe.matmul(o, sp_hi[:, k, tok], wi_lo[:, k, :], start=False, stop=False)
                        last = pe.matmul(o, sp_lo[:, k, tok], wi_hi[:, k, :], start=False, stop=(k == KT - 1))
                        if i == NT - 1 and k % 2 == 1 and k < KT - 1:
                            last.then_inc(wi_used, 1)
                    last.then_inc(win_tile, 1)
                pe.wait_ge(acc_done, KT * q + (ONE + KT))
                pe.wait_ge(modc_done, ONE + q)
                for j in range(KT):
                    last = pe.matmul(ps[:, MODB, 16 + j:17 + j], acc[:, bass.ds(j, P, step=KT)], ones[:, 0:1],
                                     start=(j == 0), stop=True, skip_group_check=True)
                last.then_inc(acc_col, 1)

                def turn(b):
                    if b == 0:
                        pe.wait_ge(u_done, NT * q + (ONE + NT))
                    if b >= 2:
                        pe.wait_ge(utlo_done, QB * q + (b - 1))
                    for g in range(BG):
                        last = pe.transpose(ps[:, UT[b % 2], P * g:P * g + P], u[:, BG * b + g, :], ident[:, :])
                    last.then_inc(ut_tr, 1)

                def conv(b):
                    pe.wait_ge(utlo_done, QB * q + (b + 1))
                    for g in range(BG):
                        n = BG * b + g
                        m = n % MSLOTS
                        h = n // CG
                        if g % CG == 0:
                            pe.wait_ge(v_done, QH * q + (ONE + max(h - 1, 0)))
                        pe.wait_ge(mhi_done, QG * q + (n + 1))
                        pe.wait_ge(mlo_done, QG * q + (ONE + n + 1))
                        o = ps[:, CV[h % 2], 2 * P * (g % CG):2 * P * (g % CG) + 2 * P]
                        for d in range(ND):
                            tok = slice(2 * PAD - d, 2 * PAD - d + P)
                            uh, ul = ut_hi[:, b % 2, g, tok], ut_lo[:, b % 2, g, tok]
                            pe.matmul(o, uh, mx[:, m, d].rearrange("p s n -> p (s n)"), start=(d == 0), stop=False,
                                      skip_group_check=True)
                            last = pe.matmul(o[:, 0:P], ul, mx[:, m, d, 0, :], start=False, stop=(d == ND - 1),
                                             skip_group_check=True)
                        last.then_inc(conv_done, 1)

                turn(0)
                turn(1)
                conv(0)
                turn(2)
                conv(1)
                turn(3)
                conv(2)
                conv(3)

            with pe.Fori(0, NQ) as q:
                quarter(q)

            def turn_z(i):
                pe.wait_ge(z_done, i + 1)
                pe.wait_ge(s_done, i)
                for k in range(KT):
                    last = pe.transpose(ps[:, PZ + k // 4, P * (k % 4):P * (k % 4) + P],
                                        zb[:, bass.ds(k, P, step=KT)], ident[:, :])
                last.then_inc(zt_done, 1)

            def y_mm(i, b, h, ks, first=False):
                cols = slice(512 * h, 512 * h + 512)
                o = ps[:, PY + h, :]
                for k in ks:
                    if k == 0:
                        pe.wait_ge(sl_done, i + 1)
                        pe.wait_ge(yb_done, 2 * i)
                    if first and h == 0 and k >= 4:
                        pe.wait_ge(wo_lo_done[k // 2 - 2], k % 2 + 3)
                    pe.matmul(o, s_hi[:, b, k, :], sp_hi[:, k, cols], start=(k == 0), stop=False)
                    pe.matmul(o, s_hi[:, b, k, :], sp_lo[:, k, cols], start=False, stop=False)
                    last = pe.matmul(o, s_lo[:, b, k, :], sp_hi[:, k, cols], start=False, stop=(k == KT - 1))
                if ks[-1] == KT - 1:
                    last.then_inc(yh_done, 1)

            def turn_h2(i, b):
                pe.wait_ge(h2_done, i + 1)
                pe.wait_ge(h2t_done, ONE + i)
                for k in range(KT):
                    last = pe.transpose(ps[:, PH + k // 4, P * (k % 4):P * (k % 4) + P],
                                        h2[:, b, bass.ds(k, P, step=KT)], ident[:, :])
                last.then_inc(h2_tr, 1)

            def route(i):
                pe.wait_ge(h2t_done, ONE + i + 1)
                pe.wait_ge(log_done, ONE + i)
                for k in range(KT):
                    last = pe.matmul(ps[:, PR, 0:NE], h2t[:, k, :], rwt[:, k, :], start=(k == 0), stop=(k == KT - 1))
                last.then_inc(rt_done, 1)

            def step(i, b, first, last):
                y_mm(i, b, 0, list(range(KT)), first)
                if not last:
                    turn_z(i + 1)
                y_mm(i, b, 1, [0, 1, 2, 3, 4, 5])
                if not first:
                    turn_h2(i - 1, 1 - b)
                y_mm(i, b, 1, [6, 7])
                if not first:
                    route(i - 1)

            turn_z(0)
            for j in range(4):
                pe.wait_ge(diag_done, j + 1)
                if j >= 2:
                    pe.wait_ge(rows_done, j - 1)
                if j == 1:
                    pe.wait_ge(modc_done, ONE + NQ)
                b0 = (PH, PR)[j % 2]
                for h in range(2):
                    last = pe.matmul(ps[:, b0 + h, :], ones[:, :],
                                     diag[:, j, 64 * h:64 * h + 64, :].rearrange("p j k -> p (j k)"),
                                     start=True, stop=True)
                last.then_inc(brow_tr, 1)
            pe.wait_ge(rw_loaded, 32)
            for h in range(2):
                pe.wait_ge(wo_lo_done[h], 2)
            step(0, 0, True, False)
            with pe.Fori(0, NT // 2 - 1) as t:
                step(2 * t + 1, 1, False, False)
                step(2 * t + 2, 0, False, False)
            step(NT - 1, 1, False, True)
            turn_h2(NT - 1, 1)
            route(NT - 1)
            pe.wait_ge(route_chain, marks["chosen"])
            pe.matmul(ps[:, PZ, 0:NE * (NT + 1)], tri[:, :], m9[:, :, :].rearrange("p t e -> p (t e)"),
                      start=True, stop=False, skip_group_check=True)
            for t in range(NT):
                last = pe.matmul(ps[:, PZ, NE * (t + 1):NE * (NT + 1)], ones_r[:, :],
                                 m9[:, t:t + 1, :].to_broadcast([P, NT - t, NE]),
                                 start=False, stop=(t == NT - 1), skip_group_check=True)
            last.then_inc(pos_done, 1)
            for j in range(2 * NT):
                if j % (NT // 2) == 0:
                    pe.wait_ge(route_chain, marks["slots", j // (NT // 2)])
                last = pe.matmul(ps[:, PZ + 1, 0:2 * NSTC], oh_p[:, j, :], oh_t[:, j, :],
                                 start=(j == 0), stop=(j == 2 * NT - 1))
            last.then_inc(slots_done, 1)

            pe.wait_ge(tables, 1)
            last_st = pe.value_load(counts[0:1, 0:1], min_val=0, max_val=NST - 1)
            st = last_st + 1

            def turn_x(b, n, held, landed):
                pe.wait_ge(gath[b], 16 * landed)
                pe.wait_ge(xtl_done, n)
                pe.wait_ge(hetl_done, held)
                for k in range(KT):
                    last = pe.transpose(ps[:, TR + k // 4, P * (k % 4):P * (k % 4) + P],
                                        xg[:, b, bass.ds(k, P, step=KT)], ident[:, :])
                last.then_inc(xt_tr, 1)

            def pair(turn, slot_):
                if slot_ < 3:
                    pe.wait_ge(pr_lo_dve, 3 * turn + slot_ + 1)
                else:
                    pe.wait_ge(pr_lo_pool, turn + 1)

            def gate_up(turn, c, cn, h, last_inc):
                pe.wait_ge(xtl_done, cn)
                pe.wait_ge(he_done, ONE + c)

                def tile(b, k):
                    sl = k % RING
                    g, up = ps[:, 2 * b, :], ps[:, 2 * b + 1, :]
                    first, end = k == 0, k == KT - 1
                    xh, xl = xt_hi[:, b, k, :], xt_lo[:, b, k, :]
                    pe.matmul(g, xh, pr_hi[:, sl, 0:F], start=first, stop=False)
                    pe.matmul(up, xh, pr_hi[:, sl, F:], start=first, stop=False)
                    pe.matmul(g, xh, pr_lo[:, sl, 0:F], start=False, stop=False)
                    pe.matmul(up, xh, pr_lo[:, sl, F:], start=False, stop=False)
                    pe.matmul(g, xl, pr_hi[:, sl, 0:F], start=False, stop=end)
                    return pe.matmul(up, xl, pr_hi[:, sl, F:], start=False, stop=end)

                def all_tiles(two):
                    for k in range(KT):
                        pair(turn + k // RING, k % RING)
                        last = tile(0, k)
                        if two:
                            last = tile(1, k)
                        last.then_inc(pr_used, last_inc if k == KT - 1 else 1)

                with pe.If(h > 0):
                    all_tiles(True)
                with pe.Else():
                    all_tiles(False)

            def part(b, k, h):
                cols = slice(512 * h, 512 * h + 512)
                o = ps[:, DN + h, :]
                pe.matmul(o, het_hi[:, b, k, :], pr_hi[:, k, cols], start=(k == 0), stop=False)
                pe.matmul(o, het_hi[:, b, k, :], pr_lo[:, k, cols], start=False, stop=False)
                return pe.matmul(o, het_lo[:, b, k, :], pr_hi[:, k, cols], start=False, stop=(k == FT - 1))

            def down_halves(turn, before):
                pe.wait_ge(y0_done, ONE + before)
                pe.wait_ge(y1_done, ONE + before)
                for h in range(2):
                    for k in range(FT):
                        if h == 0:
                            pair(turn, k)
                        last = part(0, k, h)
                    last.then_inc(d1_done if h else d0_done, 1)

            def down_tiles(b, turn, before, ks):
                if ks[0] == 0:
                    pe.wait_ge(y0_done, ONE + before)
                    pe.wait_ge(y1_done, ONE + before)
                for k in ks:
                    if b == 0:
                        pair(turn, k)
                    last = part(b, k, 0)
                    if k == FT - 1:
                        last.then_inc(d0_done, 1)
                    part(b, k, 1).then_inc(pr_used, 1)

            def turn_he(b, made, xs):
                pe.wait_ge(he_done, ONE + made)
                pe.wait_ge(xtl_done, xs)
                for k in range(FT):
                    last = pe.transpose(ps[:, TR + b, P * k:P * k + P], he[:, b, bass.ds(k, P, step=FT)], ident[:, :])
                last.then_inc(he_tr, 1)

            w = Step(pe, 0)
            turn_x(0, 0, 0, 1)
            with pe.If(w.h > 0):
                turn_x(1, 1, 0, 1)
            gate_up(0, w.c, w.cn, w.h, 5)
            turn_x(0, w.cn, 0, 2)
            with pe.If(w.hn > 0):
                turn_x(1, w.cn + 1, 0, w.h + 1)
            turn_he(0, 1, w.cn + 1 + w.hn)
            with pe.If(w.h > 0):
                turn_he(1, 2, w.cn + 1 + w.hn)
            def supertile(s):
                w = Step(pe, s)
                more = s + 1 < st
                gate_up(3 * s, w.c, w.cn, w.h, 1)
                with pe.If(more):
                    turn_x(0, w.cn, w.c, s + 2)
                with pe.Else():
                    pe.wait_ge(tables, 1)
                pe.wait_ge(hetl_done, w.c)
                with pe.If(w.hp > 0):
                    down_halves(3 * s + 2, w.cp)
                    with pe.If(w.hn > 0):
                        turn_x(1, w.cn + 1, w.c, w.nbn + 1)
                    down_tiles(1, 3 * s + 2, w.cp + 1, (0, 1, 2, 3))
                with pe.Else():
                    down_tiles(0, 3 * s + 2, w.cp, (0, 1))
                    with pe.If(w.hn > 0):
                        turn_x(1, w.cn + 1, w.c, w.nbn + 1)
                    down_tiles(0, 3 * s + 2, w.cp, (2, 3))
                xs = w.cn + w.hn + more
                turn_he(0, w.c + 1, xs)
                with pe.If(w.h > 0):
                    turn_he(1, w.c + 2, xs)
                pe.wait_ge(tables, 1)

            with pe.Fori(1, NE) as s:
                supertile(s)
            with pe.If(st > NE):
                with pe.Fori(NE, NST) as s:
                    with pe.If(s < st):
                        supertile(s)
                    pe.wait_ge(tables, 1)
                pe.wait_ge(tables, 1)
            w = Step(pe, last_st)
            pe.wait_ge(hetl_done, w.cn)
            with pe.If(w.h > 0):
                down_halves(3 * st, w.c)
                down_tiles(1, 3 * st, w.c + 1, (0, 1, 2, 3))
            with pe.Else():
                down_tiles(0, 3 * st, w.c, (0, 1, 2, 3))


def kernel(**inputs):
    import numpy as _np
    import concourse.bacc as _bacc
    from concourse import mybir as _mybir
    from concourse.bass_utils import run_bass_kernel_spmd as _run

    a = {n: _np.ascontiguousarray(v) for n, v in inputs.items()}
    laid = {
        "x": a["x"], "c": a["c"], "w_ada": a["w_ada"], "b_ada": a["b_ada"],
        "g_mix_pre": a["g_mix_pre"], "g_mix_post": a["g_mix_post"],
        "g_ffn_pre": a["g_ffn_pre"], "g_ffn_post": a["g_ffn_post"],
        "w_in": a["conv_w_in"][0].reshape(P, KT, 2, NQ, CQ).transpose(3, 0, 1, 2, 4).reshape(NQ, P, KT * 2 * CQ),
        "b_in": a["conv_b_in"][0].reshape(2, NQ, CQ).transpose(1, 0, 2).reshape(NQ, 2 * CQ),
        "w_dw": a["conv_w_dw"][0][::-1].reshape(TAPS, NQ, QG, GC).transpose(1, 3, 2, 0),
        "b_dw": a["conv_b_dw"], "ln_g": a["conv_ln_g"], "ln_b": a["conv_ln_b"],
        "w_out": a["conv_w_out"], "b_out": a["conv_b_out"],
        "router_w": a["router_w"], "router_b": a["router_b"],
        "w_gate": a["exp_w_gate"], "w_up": a["exp_w_up"], "w_down": a["exp_w_down"],
    }
    nc = _bacc.Bacc("TRN2", target_bir_lowering=False, num_devices=1, dynamic_dma_scratch_size=8192)
    arrays, args = {}, []
    for name, v in laid.items():
        v = _np.ascontiguousarray(v)
        arrays[f"in_{name}"] = v
        args.append(nc.dram_tensor(f"in_{name}", v.shape, _mybir.dt.from_np(v.dtype), kind="ExternalInput").ap())
    args.append(nc.dram_tensor("out_0", (1, S, D), F32, kind="ExternalOutput").ap())
    dit_layer(nc, *args)
    r = _run(nc, [arrays], core_ids=[0])
    return r.results[0]["out_0"]
```
